# Optimizing a Trainium2 kernel written in Bass

```python
import jax
import jax.numpy as jnp
from jax import lax
import numpy as np
import math
import jax, jax.numpy as jnp

D_MODEL = 1024
BATCH = 1
SEQ = 256
DEPTH = 1

GRID_W = 64
CTX_LEN = 256
CHUNK = 64
GLA_HEADS = 4
GLA_DK = 64
GLA_DV = 128
GLA_GATE_RANK = 16
GLA_GATE_TAU = 16.0
RET_HEADS = 4
RET_DK = 128
RET_DV = 128
RET_GAMMA_EXP0 = 5
ROPE_BASE = 10000.0
N_EXPERTS = 16
EC_CAPACITY_FACTOR = 2
EXPERT_FF = 1408
N_ADA = 6
EPS = 1e-6

GLA_QK = GLA_HEADS * GLA_DK
GLA_V = GLA_HEADS * GLA_DV
RET_QK = RET_HEADS * RET_DK
RET_V = RET_HEADS * RET_DV
MIX_WIDTH = GLA_V + RET_V
IN_WIDTHS = (GLA_QK, GLA_QK, GLA_V, 2 * GLA_GATE_RANK, GLA_V, RET_QK, RET_QK, RET_V, RET_V)
IN_WIDTH = sum(IN_WIDTHS)
IN_SPLIT_POINTS = tuple(int(p) for p in np.cumsum(IN_WIDTHS)[:-1])


F32 = jnp.float32

def _rmsnorm(x, w):
    xf = x.astype(F32)
    y = xf * lax.rsqrt(jnp.mean(xf * xf, axis=-1, keepdims=True) + EPS)
    return (y * w).astype(x.dtype)

def _head_rmsnorm(o, w):
    B, T, H, d = o.shape
    of = o.astype(F32)
    y = of * lax.rsqrt(jnp.mean(of * of, axis=-1, keepdims=True) + EPS)
    return y.reshape(B, T, H * d) * w

def _head_layernorm(o, w):
    B, T, H, d = o.shape
    of = o.astype(F32)
    mu = jnp.mean(of, axis=-1, keepdims=True)
    var = jnp.mean(jnp.square(of - mu), axis=-1, keepdims=True)
    return ((of - mu) * lax.rsqrt(var + EPS)).reshape(B, T, H * d) * w

def _flip(a):
    return jnp.flip(a, axis=1)

def _to_chunks(a):
    B, T, H, d = a.shape
    return a.reshape(B, T // CHUNK, CHUNK, H, d).transpose(1, 0, 3, 2, 4)

def _from_chunks(a):
    N, B, H, C, d = a.shape
    return a.transpose(1, 0, 3, 2, 4).reshape(B, N * C, H, d)

def _grid_rope_angles(n_tok):
    rows = n_tok // GRID_W
    row = jnp.broadcast_to(jnp.arange(rows)[:, None], (rows, GRID_W)).reshape(-1).astype(F32)
    col = jnp.broadcast_to(jnp.arange(GRID_W)[None, :], (rows, GRID_W)).reshape(-1).astype(F32)
    n_freq = RET_DK // 4
    inv = ROPE_BASE ** (-jnp.arange(n_freq, dtype=F32) / n_freq)
    return jnp.concatenate([row[:, None] * inv, col[:, None] * inv], axis=-1)

def _apply_rope(a, ang):
    half = a.shape[-1] // 2
    cos = jnp.cos(ang)[None, :, None, :]
    sin = jnp.sin(ang)[None, :, None, :]
    a1, a2 = a[..., :half], a[..., half:]
    return jnp.concatenate([a1 * cos - a2 * sin, a1 * sin + a2 * cos], axis=-1)

def _gla_chunked(q, k, v, log_a, s0):
    mask = jnp.tril(jnp.ones((CHUNK, CHUNK), dtype=bool))[:, :, None]

    def step(s, xs):
        qc, kc, vc, gc = xs
        b = jnp.cumsum(gc, axis=2)
        b_end = b[:, :, -1:, :]
        decay = jnp.exp(jnp.where(mask, b[:, :, :, None, :] - b[:, :, None, :, :], -jnp.inf))
        scores = jnp.einsum('bhik,bhjk,bhijk->bhij', qc, kc, decay)
        o = jnp.einsum('bhij,bhjv->bhiv', scores, vc) + jnp.einsum('bhik,bhkv->bhiv', qc * jnp.exp(b), s)
        s = jnp.exp(b_end)[:, :, 0, :, None] * s + jnp.einsum('bhjk,bhjv->bhkv', kc * jnp.exp(b_end - b), vc)
        return s, o

    s_end, o = lax.scan(step, s0, (_to_chunks(q), _to_chunks(k), _to_chunks(v), _to_chunks(log_a)))
    return _from_chunks(o), s_end

def _retention_chunked(q, k, v, log_gamma, s0):
    pos = jnp.arange(CHUNK, dtype=F32)
    lg = log_gamma.astype(F32)[:, None, None]
    rel = pos[:, None] - pos[None, :]
    d_intra = jnp.where(rel >= 0, jnp.exp(lg * jnp.maximum(rel, 0.0)), 0.0)
    q_decay = jnp.exp(lg * (pos + 1.0)[:, None])
    k_decay = jnp.exp(lg * (CHUNK - 1.0 - pos)[:, None])
    c_decay = jnp.exp(lg * CHUNK)

    def step(s, xs):
        qc, kc, vc = xs
        scores = jnp.einsum('bhik,bhjk->bhij', qc, kc) * d_intra
        o = jnp.einsum('bhij,bhjv->bhiv', scores, vc) + jnp.einsum('bhik,bhkv->bhiv', qc * q_decay, s)
        s = c_decay * s + jnp.einsum('bhjk,bhjv->bhkv', kc * k_decay, vc)
        return s, o

    s_end, o = lax.scan(step, s0, (_to_chunks(q), _to_chunks(k), _to_chunks(v)))
    return _from_chunks(o), s_end

def _gla_final_state(k, v, log_a):
    b = jnp.cumsum(log_a, axis=1)
    w = jnp.exp(b[:, -1:] - b)
    return jnp.einsum('bthk,bthv->bhkv', k * w, v)

def _ret_final_state(k, v, log_gamma):
    T = k.shape[1]
    w = jnp.exp(log_gamma.astype(F32)[None, :] * jnp.arange(T - 1, -1, -1, dtype=F32)[:, None])
    return jnp.einsum('bthk,bthv->bhkv', k * w[None, :, :, None], v)

def _project(h, w_in, gla_gate_w, gla_gate_b, rope):
    B, T, _ = h.shape
    gq, gk, gv, gz, gg, rq, rk, rv, rg = jnp.split(h @ w_in, IN_SPLIT_POINTS, axis=-1)
    gq = gq.reshape(B, T, GLA_HEADS, GLA_DK) * (GLA_DK ** -0.5)
    gk = gk.reshape(B, T, GLA_HEADS, GLA_DK)
    gv = gv.reshape(B, T, GLA_HEADS, GLA_DV)
    pre = jnp.einsum('btdr,drk->btdk', gz.reshape(B, T, 2, GLA_GATE_RANK), gla_gate_w) + gla_gate_b
    log_a = (jax.nn.log_sigmoid(pre.astype(F32)) / GLA_GATE_TAU).reshape(B, T, 2, GLA_HEADS, GLA_DK)
    rq = rq.reshape(B, T, RET_HEADS, RET_DK)
    rk = rk.reshape(B, T, RET_HEADS, RET_DK) * (RET_DK ** -0.5)
    if rope is not None:
        rq = _apply_rope(rq, rope)
        rk = _apply_rope(rk, rope)
    rv = rv.reshape(B, T, RET_HEADS, RET_DV)
    return gq, gk, gv, log_a, gg, rq, rk, rv, rg

def _zero_states(B):
    g = jnp.zeros((B, GLA_HEADS, GLA_DK, GLA_DV), F32)
    r = jnp.zeros((B, RET_HEADS, RET_DK, RET_DV), F32)
    return (g, g, r, r)

def _token_mixer(h, w_in, gla_gate_w, gla_gate_b, ret_decay_logit, gla_norm_w, ret_norm_w, w_out, init_states, rope):
    gq, gk, gv, log_a, gg, rq, rk, rv, rg = _project(h, w_in, gla_gate_w, gla_gate_b, rope)
    log_gamma = jax.nn.log_sigmoid(ret_decay_logit.astype(F32))
    s_gf, s_gb, s_rf, s_rb = init_states
    o_gf, s_gf = _gla_chunked(gq, gk, gv, log_a[:, :, 0], s_gf)
    o_gb, s_gb = _gla_chunked(_flip(gq), _flip(gk), _flip(gv), _flip(log_a[:, :, 1]), s_gb)
    o_rf, s_rf = _retention_chunked(rq, rk, rv, log_gamma[0], s_rf)
    o_rb, s_rb = _retention_chunked(_flip(rq), _flip(rk), _flip(rv), log_gamma[1], s_rb)
    o_g = _head_rmsnorm(o_gf + _flip(o_gb), gla_norm_w) * jax.nn.silu(gg)
    o_r = _head_layernorm(o_rf + _flip(o_rb), ret_norm_w) * jax.nn.silu(rg)
    out = jnp.concatenate([o_g, o_r], axis=-1) @ w_out
    return out, (s_gf, s_gb, s_rf, s_rb)

def _context_states(hc, w_in, gla_gate_w, gla_gate_b, ret_decay_logit):
    _, gk, gv, log_a, _, _, rk, rv, _ = _project(hc, w_in, gla_gate_w, gla_gate_b, None)
    log_gamma = jax.nn.log_sigmoid(ret_decay_logit.astype(F32))
    s_gf = _gla_final_state(gk, gv, log_a[:, :, 0])
    s_gb = _gla_final_state(_flip(gk), _flip(gv), _flip(log_a[:, :, 1]))
    s_rf = _ret_final_state(rk, rv, log_gamma[0])
    s_rb = _ret_final_state(_flip(rk), _flip(rv), log_gamma[1])
    return (s_gf, s_gb, s_rf, s_rb)

def _expert_choice_ffn(h, w_router, w_gate, w_up, w_down):
    B, T, _ = h.shape
    cap = EC_CAPACITY_FACTOR * T // N_EXPERTS
    aff = jax.nn.softmax((h @ w_router).astype(F32), axis=-1)
    gate, idx = lax.top_k(jnp.swapaxes(aff, 1, 2), cap)
    bidx = jnp.arange(B)[:, None, None]
    xe = h[bidx, idx]
    a = jnp.einsum('becd,edf->becf', xe, w_gate)
    u = jnp.einsum('becd,edf->becf', xe, w_up)
    ye = jnp.einsum('becf,efd->becd', jax.nn.silu(a) * u, w_down) * gate[..., None]
    return jnp.zeros_like(h).at[bidx, idx].add(ye.astype(h.dtype))

def first_inputs(seed: int = 0) -> dict:
    key = jax.random.key(seed)
    ks = jax.random.split(key, 24)
    n = lambda k, shape, s: jax.random.normal(k, shape, F32) * s
    logit0 = jnp.asarray(np.log(2.0 ** (RET_GAMMA_EXP0 + np.arange(RET_HEADS)) - 1.0), F32)
    return {
        'x': n(ks[0], (BATCH, SEQ, D_MODEL), 1.0),
        'c': n(ks[1], (BATCH, D_MODEL), 1.0),
        'ctx': n(ks[2], (BATCH, CTX_LEN, D_MODEL), 1.0),
        'c_ctx': n(ks[3], (D_MODEL,), 1.0),
        'w_ada': n(ks[4], (DEPTH, D_MODEL, N_ADA * D_MODEL), 0.02),
        'b_ada': n(ks[5], (DEPTH, N_ADA * D_MODEL), 0.02),
        'norm1_w': 1.0 + n(ks[6], (DEPTH, D_MODEL), 0.02),
        'w_in': n(ks[7], (DEPTH, D_MODEL, IN_WIDTH), D_MODEL ** -0.5),
        'gla_gate_w': n(ks[8], (DEPTH, 2, GLA_GATE_RANK, GLA_QK), GLA_GATE_RANK ** -0.5),
        'gla_gate_b': n(ks[9], (DEPTH, 2, GLA_QK), 0.1),
        'ret_decay_logit': logit0[None, None, :] + n(ks[10], (DEPTH, 2, RET_HEADS), 0.05),
        'gla_norm_w': 1.0 + n(ks[11], (DEPTH, GLA_V), 0.02),
        'ret_norm_w': 1.0 + n(ks[12], (DEPTH, RET_V), 0.02),
        'w_out': n(ks[13], (DEPTH, MIX_WIDTH, D_MODEL), MIX_WIDTH ** -0.5),
        'norm2_w': 1.0 + n(ks[14], (DEPTH, D_MODEL), 0.02),
        'w_router': n(ks[15], (DEPTH, D_MODEL, N_EXPERTS), D_MODEL ** -0.5),
        'w_exp_gate': n(ks[16], (DEPTH, N_EXPERTS, D_MODEL, EXPERT_FF), D_MODEL ** -0.5),
        'w_exp_up': n(ks[17], (DEPTH, N_EXPERTS, D_MODEL, EXPERT_FF), D_MODEL ** -0.5),
        'w_exp_down': n(ks[18], (DEPTH, N_EXPERTS, EXPERT_FF, D_MODEL), EXPERT_FF ** -0.5),
        'final_norm_w': 1.0 + n(ks[19], (D_MODEL,), 0.02),
    }

def first_block(x, c, ctx, c_ctx, w_ada, b_ada, norm1_w, w_in, gla_gate_w, gla_gate_b, ret_decay_logit,
              gla_norm_w, ret_norm_w, w_out, norm2_w, w_router, w_exp_gate, w_exp_up, w_exp_down, final_norm_w):
    B, n_lat, D = x.shape
    rope = _grid_rope_angles(n_lat)
    for i in range(DEPTH):
        last = i == DEPTH - 1
        mod = (jax.nn.silu(c) @ w_ada[i] + b_ada[i]).reshape(B, N_ADA, D)[:, :, None, :]
        mod_c = (jax.nn.silu(c_ctx) @ w_ada[i] + b_ada[i]).reshape(N_ADA, D)
        hc = _rmsnorm(ctx, norm1_w[i]) * (1.0 + mod_c[1]) + mod_c[0]
        if last:
            ctx_states = _context_states(hc, w_in[i], gla_gate_w[i], gla_gate_b[i], ret_decay_logit[i])
        else:
            ctx_out, ctx_states = _token_mixer(hc, w_in[i], gla_gate_w[i], gla_gate_b[i], ret_decay_logit[i],
                                               gla_norm_w[i], ret_norm_w[i], w_out[i], _zero_states(B), None)
        h = _rmsnorm(x, norm1_w[i]) * (1.0 + mod[:, 1]) + mod[:, 0]
        x_out, _ = _token_mixer(h, w_in[i], gla_gate_w[i], gla_gate_b[i], ret_decay_logit[i],
                                gla_norm_w[i], ret_norm_w[i], w_out[i], ctx_states, rope)
        x = x + mod[:, 2] * x_out
        h2 = _rmsnorm(x, norm2_w[i]) * (1.0 + mod[:, 4]) + mod[:, 3]
        x = x + mod[:, 5] * _expert_choice_ffn(h2, w_router[i], w_exp_gate[i], w_exp_up[i], w_exp_down[i])
        if not last:
            ctx = ctx + mod_c[2] * ctx_out
            hc2 = _rmsnorm(ctx, norm2_w[i]) * (1.0 + mod_c[4]) + mod_c[3]
            ctx = ctx + mod_c[5] * _expert_choice_ffn(hc2, w_router[i], w_exp_gate[i], w_exp_up[i], w_exp_down[i])
    return _rmsnorm(x, final_norm_w)


DEPTH_2 = 2

D_MIX = D_MODEL
N_MIXERS = 4
GROUP_W = D_MIX // N_MIXERS
N_PARTS = 10
D_IN = N_PARTS * GROUP_W
CONV_A_K = 31
DIFF_HEADS = 4
DIFF_DQK = GROUP_W // (2 * DIFF_HEADS)
DIFF_DV = 2 * DIFF_DQK
ROPE_HALF = DIFF_DQK // 2
Q_BLOCK = 128
CHUNK_2 = 128
SG_GROUPS = 4
SG_DIM = GROUP_W // SG_GROUPS
CONV_D_K = 3
D_FF = 4 * D_MODEL


def rms_norm(x, g):
    xf = x.astype(jnp.float32)
    y = xf * lax.rsqrt(jnp.mean(xf * xf, axis=-1, keepdims=True) + EPS)
    return (y * g.astype(jnp.float32)).astype(x.dtype)

def layer_norm(x, g, b):
    xf = x.astype(jnp.float32)
    xc = xf - jnp.mean(xf, axis=-1, keepdims=True)
    y = xc * lax.rsqrt(jnp.mean(xc * xc, axis=-1, keepdims=True) + EPS)
    return (y * g.astype(jnp.float32) + b.astype(jnp.float32)).astype(x.dtype)

def modulate(h, shift, scale):
    return h * (1 + scale) + shift

def depthwise_conv(x, w):
    pad = w.shape[0] // 2
    return lax.conv_general_dilated(
        x, w[:, None, :].astype(x.dtype), window_strides=(1,), padding=[(pad, pad)],
        dimension_numbers=('NWC', 'WIO', 'NWC'), feature_group_count=x.shape[-1])

def axial_rope(rows, dtype):
    row = jnp.repeat(jnp.arange(rows, dtype=jnp.float32), GRID_W)
    col = jnp.tile(jnp.arange(GRID_W, dtype=jnp.float32), rows)
    inv = ROPE_BASE ** (-jnp.arange(0, ROPE_HALF, 2, dtype=jnp.float32) / ROPE_HALF)
    ang_r = row[:, None] * inv
    ang_c = col[:, None] * inv
    return (jnp.cos(ang_r)[:, None, :].astype(dtype), jnp.sin(ang_r)[:, None, :].astype(dtype),
            jnp.cos(ang_c)[:, None, :].astype(dtype), jnp.sin(ang_c)[:, None, :].astype(dtype))

def rotate_pairs(t, cos, sin):
    f = t.shape[-1] // 2
    t1, t2 = t[..., :f], t[..., f:]
    return jnp.concatenate([t1 * cos - t2 * sin, t1 * sin + t2 * cos], axis=-1)

def apply_axial_rope(t, rope):
    cos_r, sin_r, cos_c, sin_c = rope
    return jnp.concatenate([rotate_pairs(t[..., :ROPE_HALF], cos_r, sin_r),
                            rotate_pairs(t[..., ROPE_HALF:], cos_c, sin_c)], axis=-1)

def qk_heads(t, rope):
    b, n, _ = t.shape
    t = t.reshape(b, n, DIFF_HEADS, 2, DIFF_DQK)
    t1, t2 = t[..., 0, :], t[..., 1, :]
    if rope is not None:
        t1, t2 = apply_axial_rope(t1, rope), apply_axial_rope(t2, rope)
    return t1, t2

def v_heads(t):
    b, n, _ = t.shape
    return t.reshape(b, n, DIFF_HEADS, DIFF_DV)

def diff_attention(q1, q2, k1, k2, v, lam, lam_init, subln_g):
    b, n = q1.shape[:2]
    nb = n // Q_BLOCK
    scale = DIFF_DQK ** -0.5

    def blocks(t):
        return t.reshape(b, nb, Q_BLOCK, DIFF_HEADS, DIFF_DQK).transpose(1, 0, 2, 3, 4)

    def one_block(qs):
        qb1, qb2 = qs
        p1 = jax.nn.softmax(jnp.einsum('bqhd,bkhd->bhqk', qb1, k1).astype(jnp.float32) * scale, axis=-1)
        p2 = jax.nn.softmax(jnp.einsum('bqhd,bkhd->bhqk', qb2, k2).astype(jnp.float32) * scale, axis=-1)
        w = (p1 - lam * p2).astype(v.dtype)
        return jnp.einsum('bhqk,bkhd->bqhd', w, v)

    o = lax.map(one_block, (blocks(q1), blocks(q2)))
    o = o.transpose(1, 0, 2, 3, 4).reshape(b, n, DIFF_HEADS, DIFF_DV)
    o = rms_norm(o, subln_g) * (1.0 - lam_init)
    return o.reshape(b, n, GROUP_W)

def conformer_conv(a_val, a_gate, conv_w, conv_b, ln_g, ln_b):
    glu = a_val * jax.nn.sigmoid(a_gate)
    y = depthwise_conv(glu, conv_w) + conv_b
    return jax.nn.silu(layer_norm(y, ln_g, ln_b))

def spatial_gating(u, v, ln_g, ln_b, w_s, b_s):
    u = jax.nn.gelu(u)
    v = layer_norm(jax.nn.gelu(v), ln_g, ln_b)
    b, n, _ = v.shape
    vc = v.reshape(b, n // CHUNK_2, CHUNK_2, SG_GROUPS, SG_DIM)
    s = jnp.einsum('gpq,bcqgd->bcpgd', w_s, vc) + b_s.T[:, :, None]
    return u * s.reshape(b, n, GROUP_W)

def short_conv_mixer(bg, cg, xin, conv_w):
    return bg * depthwise_conv(cg * xin, conv_w)

def token_mixers(z, k1, k2, v, rope, lam, lam_init, conv_a_w, conv_a_b, ln_a_g, ln_a_b, subln_g,
                 sg_ln_g, sg_ln_b, sg_w, sg_b, conv_d_w, w_out):
    a_val, a_gate, q, _, _, u, sv, bg, cg, xin = z
    y_a = conformer_conv(a_val, a_gate, conv_a_w, conv_a_b, ln_a_g, ln_a_b)
    q1, q2 = qk_heads(q, rope)
    y_b = diff_attention(q1, q2, k1, k2, v, lam, lam_init, subln_g)
    y_c = spatial_gating(u, sv, sg_ln_g, sg_ln_b, sg_w, sg_b)
    y_d = short_conv_mixer(bg, cg, xin, conv_d_w)
    return jnp.concatenate([y_a, y_b, y_c, y_d], axis=-1) @ w_out

def channel_mixer(h, w1, w2):
    return jnp.square(jax.nn.relu(h @ w1)) @ w2

def second_inputs(seed: int = 0) -> dict:
    key = jax.random.key(seed)
    ks = jax.random.split(key, 32)

    def nrm(k, shape, scale):
        return jax.random.normal(k, shape, jnp.float32) * scale

    def gain(k, shape):
        return 1.0 + nrm(k, shape, 0.05)

    return {
        'x': nrm(ks[0], (BATCH, SEQ, D_MODEL), 1.0),
        'c': nrm(ks[1], (BATCH, D_MODEL), 1.0),
        'ctx': nrm(ks[2], (BATCH, CTX_LEN, D_MODEL), 1.0),
        'c_ctx': nrm(ks[3], (D_MODEL,), 1.0),
        'ada_w': nrm(ks[4], (DEPTH_2, D_MODEL, 6 * D_MODEL), 0.5 * D_MODEL ** -0.5),
        'ada_b': nrm(ks[5], (DEPTH_2, 6 * D_MODEL), 0.01),
        'norm1_g': gain(ks[6], (DEPTH_2, D_MODEL)),
        'norm2_g': gain(ks[7], (DEPTH_2, D_MODEL)),
        'w_in': nrm(ks[8], (DEPTH_2, D_MODEL, D_IN), D_MODEL ** -0.5),
        'conv_a_w': nrm(ks[9], (DEPTH_2, CONV_A_K, GROUP_W), CONV_A_K ** -0.5),
        'conv_a_b': nrm(ks[10], (DEPTH_2, GROUP_W), 0.01),
        'ln_a_g': gain(ks[11], (DEPTH_2, GROUP_W)),
        'ln_a_b': nrm(ks[12], (DEPTH_2, GROUP_W), 0.01),
        'lam_q1': nrm(ks[13], (DEPTH_2, DIFF_DQK), 0.1),
        'lam_k1': nrm(ks[14], (DEPTH_2, DIFF_DQK), 0.1),
        'lam_q2': nrm(ks[15], (DEPTH_2, DIFF_DQK), 0.1),
        'lam_k2': nrm(ks[16], (DEPTH_2, DIFF_DQK), 0.1),
        'subln_g': gain(ks[17], (DEPTH_2, DIFF_DV)),
        'sg_ln_g': gain(ks[18], (DEPTH_2, GROUP_W)),
        'sg_ln_b': nrm(ks[19], (DEPTH_2, GROUP_W), 0.01),
        'sg_w': nrm(ks[20], (DEPTH_2, SG_GROUPS, CHUNK_2, CHUNK_2), CHUNK_2 ** -0.5),
        'sg_b': gain(ks[21], (DEPTH_2, SG_GROUPS, CHUNK_2)),
        'conv_d_w': nrm(ks[22], (DEPTH_2, CONV_D_K, GROUP_W), CONV_D_K ** -0.5),
        'w_out': nrm(ks[23], (DEPTH_2, D_MIX, D_MODEL), D_MIX ** -0.5),
        'mlp_w1': nrm(ks[24], (DEPTH_2, D_MODEL, D_FF), D_MODEL ** -0.5),
        'mlp_w2': nrm(ks[25], (DEPTH_2, D_FF, D_MODEL), D_FF ** -0.5),
        'final_g': gain(ks[26], (D_MODEL,)),
    }

def second_block(x, c, ctx, c_ctx, ada_w, ada_b, norm1_g, norm2_g, w_in, conv_a_w, conv_a_b, ln_a_g,
              ln_a_b, lam_q1, lam_k1, lam_q2, lam_k2, subln_g, sg_ln_g, sg_ln_b, sg_w, sg_b, conv_d_w,
              w_out, mlp_w1, mlp_w2, final_g):
    ROWS = x.shape[1] // GRID_W
    rope = axial_rope(ROWS, x.dtype)
    h_ctx = ctx
    for l in range(DEPTH_2):
        lam_init = 0.8 - 0.6 * math.exp(-0.3 * l)
        lam = (jnp.exp(jnp.sum(lam_q1[l] * lam_k1[l]).astype(jnp.float32))
               - jnp.exp(jnp.sum(lam_q2[l] * lam_k2[l]).astype(jnp.float32)) + lam_init)
        mod_x = jnp.split((jax.nn.silu(c) @ ada_w[l] + ada_b[l])[:, None, :], 6, axis=-1)
        mod_c = jnp.split(jax.nn.silu(c_ctx) @ ada_w[l] + ada_b[l], 6, axis=-1)
        mix_args = (rope, lam, lam_init, conv_a_w[l], conv_a_b[l], ln_a_g[l], ln_a_b[l], subln_g[l],
                    sg_ln_g[l], sg_ln_b[l], sg_w[l], sg_b[l], conv_d_w[l], w_out[l])

        hc = modulate(rms_norm(h_ctx, norm1_g[l]), mod_c[0], mod_c[1])
        zc = jnp.split(hc @ w_in[l], N_PARTS, axis=-1)
        k1c, k2c = qk_heads(zc[3], None)
        vc = v_heads(zc[4])

        hx = modulate(rms_norm(x, norm1_g[l]), mod_x[0], mod_x[1])
        zx = jnp.split(hx @ w_in[l], N_PARTS, axis=-1)
        k1x, k2x = qk_heads(zx[3], rope)
        k1 = jnp.concatenate([k1c, k1x], axis=1)
        k2 = jnp.concatenate([k2c, k2x], axis=1)
        v = jnp.concatenate([vc, v_heads(zx[4])], axis=1)
        x = x + mod_x[2] * token_mixers(zx, k1, k2, v, *mix_args)
        x = x + mod_x[5] * channel_mixer(modulate(rms_norm(x, norm2_g[l]), mod_x[3], mod_x[4]),
                                         mlp_w1[l], mlp_w2[l])

        if l < DEPTH_2 - 1:
            ctx_args = (None,) + mix_args[1:]
            h_ctx = h_ctx + mod_c[2] * token_mixers(zc, k1c, k2c, vc, *ctx_args)
            h_ctx = h_ctx + mod_c[5] * channel_mixer(
                modulate(rms_norm(h_ctx, norm2_g[l]), mod_c[3], mod_c[4]), mlp_w1[l], mlp_w2[l])
    return rms_norm(x, final_g)


def setup_inputs(seed=0):
    out = dict(first_inputs(seed))
    for name, value in second_inputs(seed + 1).items():
        if name != "x":
            out[name + "_2"] = value
    return out


def reference(
    x, c, ctx, c_ctx, w_ada, b_ada, norm1_w, w_in, gla_gate_w, gla_gate_b, ret_decay_logit,
    gla_norm_w, ret_norm_w, w_out, norm2_w, w_router, w_exp_gate, w_exp_up, w_exp_down,
    final_norm_w, c_2, ctx_2, c_ctx_2, ada_w_2, ada_b_2, norm1_g_2, norm2_g_2, w_in_2,
    conv_a_w_2, conv_a_b_2, ln_a_g_2, ln_a_b_2, lam_q1_2, lam_k1_2, lam_q2_2, lam_k2_2,
    subln_g_2, sg_ln_g_2, sg_ln_b_2, sg_w_2, sg_b_2, conv_d_w_2, w_out_2, mlp_w1_2, mlp_w2_2,
    final_g_2,
):
    x = first_block(
        x, c, ctx, c_ctx, w_ada, b_ada, norm1_w, w_in, gla_gate_w, gla_gate_b, ret_decay_logit,
        gla_norm_w, ret_norm_w, w_out, norm2_w, w_router, w_exp_gate, w_exp_up, w_exp_down,
        final_norm_w,
    )
    return second_block(
        x, c_2, ctx_2, c_ctx_2, ada_w_2, ada_b_2, norm1_g_2, norm2_g_2, w_in_2, conv_a_w_2,
        conv_a_b_2, ln_a_g_2, ln_a_b_2, lam_q1_2, lam_k1_2, lam_q2_2, lam_k2_2, subln_g_2,
        sg_ln_g_2, sg_ln_b_2, sg_w_2, sg_b_2, conv_d_w_2, w_out_2, mlp_w1_2, mlp_w2_2,
        final_g_2,
    )


_drawn_inputs = setup_inputs


def setup_inputs(seed=0):
    import zlib

    import numpy as np

    out = dict(_drawn_inputs(seed))
    spreads = {}
    factors = {'norm1_w': 4.676,
     'gla_gate_b': 5.121,
     'gla_norm_w': 8.0,
     'ret_norm_w': 7.799,
     'norm2_w': 5.976,
     'conv_a_b_2': 8.0,
     'ln_a_g_2': 7.263,
     'ln_a_b_2': 64.0,
     'lam_q1_2': 4.025,
     'lam_k1_2': 5.82,
     'lam_q2_2': 8.0,
     'lam_k2_2': 8.0,
     'subln_g_2': 7.027,
     'sg_ln_g_2': 7.622,
     'sg_ln_b_2': 64.0,
     'sg_b_2': 7.55,
     'norm2_g_2': 3.54}
    for name, (base, spread) in spreads.items():
        noise = np.random.default_rng([zlib.crc32(name.encode()), seed]).standard_normal(out[name].shape)
        drawn = base * np.exp(spread * noise) if base else spread * noise
        out[name] = jnp.asarray(drawn.astype(out[name].dtype))
    for name, factor in factors.items():
        out[name] = (out[name] * factor).astype(out[name].dtype)
    return out
```

```python
from contextlib import ExitStack

import numpy as np

import concourse.bass as bass
from concourse import mybir

F32 = mybir.dt.float32
F32R = mybir.dt.float32r
ACT = mybir.ActivationFunctionType
ALU = mybir.AluOpType
AX = mybir.AxisListType

P = 128
T = 256
N2 = 2 * T
D = 1024
KT = D // P
EPS = 1e-6
GATE_TAU = 16.0
CH = 64
NC = T // CH
GH = RH = 4
W_IN1 = 3616
E, CAP, FF = 16, 32, 1408
FT = FF // P
FQ = FF // 4
GW = 256
D_FF = 4096
DQ = 32
LAM_INIT = [0.8 - 0.6 * float(np.exp(-0.3 * l)) for l in range(2)]
EXP_CLAMP = 43.0

SLOT = 4096
NSLOT = 6


def offsets(parts, base=0):
    out, at = {}, base
    for name, size in parts:
        out[name] = (at, size)
        at += size
    return out, at


C0_PARTS = [("ident", P), ("ones", P), ("sel2", 2), ("slot1", 1), ("iota32", CAP), ("incl", P)]
C1_PARTS = [("prefI", P), ("sufI", P), ("prefIm", P), ("sufIm", P), ("sufS", P), ("prefS", P),
            ("sufC", P), ("prefC", P), ("cos1", T), ("sin1", T), ("rot1", P), ("rel", 4 * T),
            ("msk", 4 * T), ("qpos", 2 * T), ("kpos", 16), ("cmask", 2 * CH)]
C2_PARTS = [("cos2", T), ("sin2", T), ("rot2", P), ("ones64", P)]
V0_PARTS = [("cv", 4 * KT), ("norms", 8 * KT), ("bada", 3 * 48), ("gnorm", 4), ("rnorm", 4), ("rdl", 8)]
V2_PARTS = [("caw", 62), ("cab", 2), ("lag", 2), ("lab", 2), ("cdw", 6), ("subg", 1), ("sglng", GW),
            ("sglnb", GW), ("sgb", 2 * P), ("lam", 4 * DQ)]
C0_AT, C0_N = offsets(C0_PARTS)
C1_AT, C1_N = offsets(C1_PARTS)
C2_AT, C2_N = offsets(C2_PARTS)
V0_AT, V0_N = offsets(V0_PARTS)
V2_AT, V2_N = offsets(V2_PARTS)


def shape_constants():
    f = np.float32
    p = np.arange(P)
    j, i = p[:, None], p[None, :]
    same = (j // CH) == (i // CH)
    c0 = {"ident": np.eye(P), "ones": np.ones((P, P)),
          "sel2": (p[:, None] % 32 == np.arange(2)[None, :]),
          "slot1": (p[:, None] % CAP) + 1, "iota32": np.broadcast_to(np.arange(CAP) + 1, (P, CAP)),
          "incl": j <= i}
    tok = np.arange(T)
    pos = np.stack([tok // 64, tok % 64]).astype(f)
    inv = (10000.0 ** (-np.arange(32, dtype=f) / 32)).astype(f)
    ang = np.concatenate([inv[:, None] * pos[0], inv[:, None] * pos[1]], 0).astype(f)
    ang = np.concatenate([ang, ang], 0)
    rot1 = np.zeros((P, P))
    for m in range(64):
        rot1[m + 64, m] = -1.0
        rot1[m, m + 64] = 1.0
    jj = (np.arange(2)[None, :, None] * P + p[:, None, None])
    ii = tok[None, None, :]
    rel = np.stack([np.maximum(ii - jj, 0), np.maximum(jj - ii, 0)], 1)
    msk = np.stack([ii >= jj, jj >= ii], 1)
    qpos = np.broadcast_to(np.stack([tok + 1, T - tok]), (P, 2, T))
    t2 = np.arange(2)[None, :] * P + p[:, None]
    kpos = np.broadcast_to(np.stack([T - 1 - t2, t2], 2)[..., None], (P, 2, 2, 4))
    pc, ic = (p % CH)[:, None], np.arange(CH)[None, :]
    c1 = {"prefI": (j <= i) & same, "sufI": (j >= i) & same,
          "prefIm": ((j <= i) & same) * 1.0 - ((j % CH <= CH // 2 - 1) & same) * 1.0,
          "sufIm": ((j >= i) & same) * 1.0 - ((j % CH >= CH // 2) & same) * 1.0,
          "sufS": (j > i) & same, "prefS": (j < i) & same, "sufC": j > i, "prefC": j < i,
          "cos1": np.cos(ang), "sin1": np.sin(ang), "rot1": rot1, "rel": rel, "msk": msk,
          "qpos": qpos, "kpos": kpos, "cmask": np.stack([pc <= ic, pc >= ic], 1)}
    inv2 = (10000.0 ** (-np.arange(0, 16, 2, dtype=f) / 16)).astype(f)
    d = p % 32
    ang2 = (inv2[d % 8][:, None] * np.where((d < 16)[:, None], pos[0][None], pos[1][None])).astype(f)
    rot2 = np.zeros((P, P))
    for m in range(P):
        if m % 16 < 8:
            rot2[m + 8, m] = -1.0
        else:
            rot2[m - 8, m] = 1.0
    c2 = {"cos2": np.cos(ang2), "sin2": np.sin(ang2), "rot2": rot2, "ones64": (j // 64) == (i // 64)}

    def pack(parts, c):
        return np.ascontiguousarray(np.concatenate(
            [np.asarray(c[n]).astype(f).reshape(P, size) for n, size in parts], 1))

    return pack(C0_PARTS, c0), pack(C1_PARTS, c1), pack(C2_PARTS, c2)


def build(nc, ap, out):
    with ExitStack() as ctx:
        TOTAL = 52995
        big = ctx.enter_context(nc.sbuf_tensor("big", [P, TOTAL], F32))
        PB = [ctx.enter_context(nc.psum_tensor(f"bank{i}", [P, 512], F32))[:, :] for i in range(8)]
        BIG_AT = nc.sbuf_base - 4 * TOTAL
        sems = {}

        def S(name):
            if name not in sems:
                sems[name] = ctx.enter_context(nc.semaphore(name))
            return sems[name]

        names2, pers = offsets([("resid", KT * N2), ("h", KT * N2), ("c0", C0_N), ("cR", C1_N), ("v0", V0_N),
                                ("wr", KT * E), ("csil", 2 * KT * 32), ("modv", 3 * 96), ("asc", 6 * 16),
                                ("rs", N2)])
        PERS = TOTAL - pers
        ARENA1 = 3 * SLOT
        ARENA2 = NSLOT * SLOT

        def view(off, *dims, parts=slice(0, P)):
            n = 1
            for d in dims:
                n *= d
            a = big[parts, off:off + n]
            if len(dims) == 2:
                a = a.rearrange("p (a b) -> p a b", a=dims[0])
            if len(dims) == 3:
                a = a.rearrange("p (a b c) -> p a b c", a=dims[0], b=dims[1])
            if len(dims) == 4:
                a = a.rearrange("p (a b c d) -> p a b c d", a=dims[0], b=dims[1], c=dims[2])
            return a

        def pers_view(name, *dims):
            return view(PERS + names2[name][0], *dims)

        resid = pers_view("resid", KT, N2)
        h = pers_view("h", KT, N2)
        wr = pers_view("wr", KT, E)
        csil = pers_view("csil", 2, KT, 32)
        modv = pers_view("modv", 3, 48, 2)
        asc = pers_view("asc", 6, KT, 2)
        rs = pers_view("rs", N2)

        def c0(name, *dims):
            return view(PERS + names2["c0"][0] + C0_AT[name][0], *dims)

        def c1(name, *dims):
            return view(PERS + names2["cR"][0] + C1_AT[name][0], *dims)

        def c2(name, *dims):
            return view(PERS + names2["cR"][0] + C2_AT[name][0], *dims)

        def v0(name, *dims):
            return view(PERS + names2["v0"][0] + V0_AT[name][0], *dims)

        SW_AT = names2["cR"][0] + C2_N
        V2_BASE = SW_AT + 2 * 4 * P

        def v2(layer, name, *dims):
            return view(PERS + V2_BASE + layer * V2_N + V2_AT[name][0], *dims)

        assert C2_N + 2 * 4 * P + 2 * V2_N <= C1_N
        sgw = view(PERS + SW_AT, 2, 4, P)
        ident, ones, sel2 = c0("ident", P), c0("ones", P), c0("sel2", 2)

        def slot(s, *dims):
            return view(s * SLOT, *dims)

        B1, b1_end = offsets([
            ("gq", 512), ("gk", 512), ("gktm", 1024), ("gv", 2048), ("gz", 512), ("sgg", 1024),
            ("rq", 1024), ("rk", 1024), ("rktm", 1024), ("rv", 2048), ("srg", 1024), ("la", 2048),
            ("kw", 1024), ("kwr", 2048), ("Sg", 2048), ("Sr", 1024), ("ke", 1024), ("EA", 1024),
            ("wgz", 256), ("gw", 512), ("lg", 16), ("wk", 16)], ARENA1)
        assert b1_end <= PERS, (b1_end, PERS)

        def b1(name, *dims):
            return view(B1[name][0], *dims)

        gq, gk = b1("gq", 2, T), b1("gk", 2, T)
        gktm, gv = b1("gktm", 4, 256), b1("gv", 4, 512)
        gz = b1("gz", N2)
        part = view(PERS - 3 * 512, 3, 512)
        sgg, srg = b1("sgg", 4, T), b1("srg", 4, T)
        rq, rk = b1("rq", 4, T), b1("rk", 4, T)
        rktm, rv = b1("rktm", 2, 512), b1("rv", 4, 512)
        la = b1("la", 4, 512)
        kw = b1("kw", 2, 512)
        kwr = b1("kwr", 2, 2, 512)
        Sg = b1("Sg", 2, 4, 2, P)
        Sr = b1("Sr", 2, 4, P)
        ke = b1("ke", 2, 512)
        EA = b1("EA", 2, 512)
        wgz = b1("wgz", KT, 32)
        gw = b1("gw", 512)
        lg = b1("lg", 2, 8)
        wk = b1("wk", 2, 8)
        H_AT = PERS + names2["h"][0]
        qe, qd, kd, em = (view(H_AT + 1024 * n, 2, 512) for n in range(4))
        ep = qd
        prt = view(B1["la"][0], 8, P)
        pg = view(B1["kw"][0], 2, 4, P)
        lt = view(B1["kwr"][0], 4, 512)
        og = view(B1["EA"][0], 4, T)
        orr = view(B1["gktm"][0], 4, T)
        dec = view(H_AT, 2, 1024)
        pr = view(H_AT + 2048, 2, 512)
        rqd = view(H_AT + 3072, 2, 512)
        tmp1 = view(B1["la"][0], 4, 512)
        gn_t = view(H_AT, 4, T)
        mixb1 = view(B1["rv"][0], KT, T)

        B3, b3_end = offsets([
            ("htm", 2 * D), ("xeT", KT * E * CAP), ("sel", 2 * E * CAP), ("xe", KT * CAP), ("gs", FQ), ("gu", FQ),
            ("hx", FT * CAP), ("ye", 256), ("bcs", 512), ("selg", T), ("pa", 512), ("bcm", 512), ("aff", 32),
            ("sm", 8), ("affw", 2 * T), ("m8", 8), ("mk", 32), ("pos", 32), ("mkT", T)], ARENA2)
        assert b3_end <= PERS

        def b3(name, *dims, parts=slice(0, P)):
            return view(B3[name][0], *dims, parts=parts)

        e_rows = slice(0, E)
        htm, xeT, sel = b3("htm", 2, D), b3("xeT", KT, E * CAP), b3("sel", 2, E * CAP)
        xe, gs, gu, hx = b3("xe", KT, CAP), b3("gs", FQ), b3("gu", FQ), b3("hx", FT, CAP)
        ye, bcs, selg = b3("ye", 256), b3("bcs", 512), b3("selg", T)
        pa, bcm = b3("pa", 512, parts=e_rows), b3("bcm", 512, parts=e_rows)
        aff, mk, pos = b3("aff", 2, E), b3("mk", 2, E), b3("pos", 2, E)
        sm, m8 = b3("sm", 8), b3("m8", 8, parts=e_rows)
        affw, mkT = b3("affw", 2, T, parts=e_rows), b3("mkT", T, parts=e_rows)
        DOWN_T = [(0, 3), (3, 6), (6, 9), (9, 11)]

        GLU_W, CX_W = T + 30, T + 2
        B4, b4_end = offsets([
            ("qf", 1024), ("kf", 1024), ("vt", 1024), ("uf", 1024), ("sv", 1024), ("bg", 1024), ("tg", 1024),
            ("tc", 1024), ("glu", 4 * GLU_W), ("cx", 4 * CX_W), ("E", 2048), ("WT", 1024), ("s4", 64)], ARENA2)
        assert b4_end <= PERS, (b4_end, PERS)

        def b4(name, *dims):
            return view(B4[name][0], *dims)

        qf, kf, vt, uf, sv = b4("qf", 2, N2), b4("kf", 2, N2), b4("vt", 4, GW), b4("uf", 2, N2), b4("sv", 4, GW)
        bgf, tg, tc = b4("bg", 2, N2), b4("tg", 2, N2), b4("tc", 2, N2)
        glu = b4("glu", 2, 2, GLU_W)
        cx = b4("cx", 2, 2, CX_W)
        Eb = b4("E", 2, 2, 512)
        acca, accd = view(B4["E"][0], 2, N2), view(B4["E"][0] + 1024, 2, N2)
        WT = b4("WT", 2, 512)
        s4 = b4("s4", 64)
        mix = h

        def parts32r(name, off, *dims):
            n = int(np.prod(dims))
            a = nc.alloc_sbuf_tensor_at(name, [P, n], F32R, offset=BIG_AT + 4 * off)[:, :]
            return a.rearrange("p (a b) -> p a b", a=dims[0]) if len(dims) == 2 else a

        NWB, WU = 4, KT * P
        h_hi = [parts32r(f"h_hi{k}", 4 * SLOT + k * N2, N2) for k in range(KT)]
        h_lo = [parts32r(f"h_lo{k}", H_AT + k * N2, N2) for k in range(KT)]
        w_hi = [parts32r(f"w_hi{n}", 5 * SLOT + n * WU, WU) for n in range(NWB)]
        w_lo = [parts32r(f"w_lo{n}", ARENA2 + n * WU, WU) for n in range(NWB)]
        h1 = view(ARENA2 + NWB * WU, 2, 4, N2)
        h1_lo = [parts32r(f"h1_lo{c}", ARENA2 + NWB * WU + 4 * c * N2, 4, N2) for c in range(2)]
        h1_hi = [parts32r(f"h1_hi{c}", ARENA2 + NWB * WU + (8 + 4 * c) * N2, 4, N2) for c in range(2)]
        assert ARENA2 + NWB * WU + 16 * N2 <= PERS and H_AT % 8 == 0

        def w_unit(n):
            c, q = n // 4 % 2, n % 4
            if n < 8:
                return slot(c, KT, 512)[:, :, q * P:(q + 1) * P]
            return slot(2 + c, 4, D)[:, :, q * 256:(q + 1) * 256]

        def w_split(t, n):
            return t[n % NWB].rearrange("p (k n) -> p k n", k=KT if n < 8 else 4)

        def unit_done(layer, i, n):
            if n < 0:
                i, n = i - 1, n + 16
            c, q = n // 4 % 2, n % 4
            if n < 8:
                return S(f"h1_ps{c}"), 16 * layer + 4 * i + q + 2
            return S(f"y_ps{c}"), 32 * layer + 8 * i + 2 * q + 2 + 9

        mlp_loads = []

        def linker(eng, name):
            n = [0]

            def link(ins):
                n[0] += 1
                ins.then_inc(S(name), 1)
                eng.wait_ge(S(name), n[0])
            return link

        def bc(a, axis, shape):
            return a.unsqueeze(axis).to_broadcast(shape)

        w_in1 = ap["w_in"][0].rearrange("(k p) n -> p k n", p=P)

        def cols(w, a, n):
            return w.rearrange("(k p) n -> p k n", p=P)[:, :, a:a + n]

        PROJ1 = [0, 512, 2080, 2592, 1568, 1056, 3104]

        def tile_table(specs):
            return specs

        def proj1_tiles():
            out = []
            t = []
            for tt in range(4):
                t.append((P, 256, True, 256, tt, "D", gktm[:, tt, :], None))
            for m in range(2):
                t.append((P, T, False, 256 + m * P, None, "A", gk[:, m, :], None))
            for m in range(2):
                t.append((P, T, False, m * P, None, "A", gq[:, m, :], 0.125))
            out.append(t)
            out.append([(P, 512, True, 0, tt, "D", gv[:, tt, :], None) for tt in range(4)])
            s = float(P) ** -0.5
            out.append([(P, 512, True, 0, tt, "A", rktm[:, tt - 2, :], s) for tt in (2, 3)]
                       + [(P, T, False, m * P, None, "A", rk[:, m, :], s) for m in range(4)])
            out.append([(P, 512, True, 0, tt, "D", rv[:, tt, :], None) for tt in range(4)])
            out.append([(P, T, False, m * P, None, "A", rq[:, m, :], None) for m in range(4)])
            out.append([(P, T, False, m * P, None, "A", sgg[:, m, :], "silu") for m in range(4)])
            out.append([(P, T, False, m * P, None, "A", srg[:, m, :], "silu") for m in range(4)])
            return out

        PROJ1_END = [int(x) for x in np.cumsum([len(g) + (n == 1) for n, g in enumerate(proj1_tiles())])]

        class Tiles:

            def __init__(self):
                self.owner = []

            def add(self, owner):
                self.owner.append(owner)
                return len(self.owner) - 1

            def emptied(self, n):
                o = self.owner[n]
                return S("tile_out_" + o), sum(1 for x in self.owner[:n + 1] if x == o)

        NORMS = [(0, 0, N2), (1, 1, T), (None, 2, T), (2, 3, N2), (3, 5, N2), (4, 4, N2), (5, 6, T), (None, 7, T)]

        def affine_no(k):
            return sum(1 for a, _, _ in NORMS[:k] if a is not None)

        def wide_no(k):
            return sum(1 for _, _, n in NORMS[:k] if n == N2)

        PARTS2 = [(8, 9), (0, 1), (2, 3), (4, 5), (6, 7)]

        def proj2_tiles(layer):
            nf = N2 if layer == 0 else T

            def fm(col, m, owner, dst, func, n=nf):
                return (P, n, False, col + m * P, None, owner, dst, func)
            out = [[fm(0, m, "A", tc[:, m, 0:nf], None) for m in range(2)]
                   + [fm(256, m, "D", cx[:, m, 0:nf // T, 1:1 + T], ("times", tc[:, m, 0:nf], m)) for m in range(2)],
                   [fm(256, m, "A", tg[:, m, 0:nf], "sigmoid") for m in range(2)]
                   + [fm(0, m, "D", glu[:, m, 0:nf // T, 15:15 + T], ("times", tg[:, m, 0:nf], m)) for m in range(2)],
                   [fm(0, m, "A", qf[:, m, 0:nf], None) for m in range(2)]
                   + [fm(256, m, "A", kf[:, m, :], None, N2) for m in range(2)],
                   [(P, 256, True, 0, x, "A", vt[:, x, :], None) for x in range(4)]
                   + [fm(256, m, "A", uf[:, m, 0:nf], "gelu") for m in range(2)],
                   [(P, 256, True, 0, x, "A", sv[:, x, :], "gelu") for x in range(nf // P)]
                   + [fm(256, m, "A", bgf[:, m, 0:nf], None) for m in range(2)]]
            return out

        PROJ2_AT, OUT2_AT, at = [], [], PROJ1_END[-1] + KT
        for l_ in range(2):
            PROJ2_AT.append(at)
            at += sum(len(g) for g in proj2_tiles(l_))
            OUT2_AT.append(at)
            at += KT

        def attn_units(layer):
            return [(s_, qt, hh) for s_ in range(2 - layer) for qt in range(2) for hh in range(4)]

        UNIT_AT = [0, 16]

        def n_a(groups):
            return sum(t[5] == "A" for g in groups for t in g)

        def n_d(groups):
            return sum(t[5] == "D" for g in groups for t in g)
        D_TILES_AFTER_OUT = [n_d(proj1_tiles()) + 1 + KT + sum(n_d(proj2_tiles(x)) + KT for x in range(l_ + 1))
                             for l_ in range(2)]
        A_TILES_BEFORE = [n_a(proj1_tiles()), n_a(proj1_tiles()) + n_a(proj2_tiles(0))]
        def credit(eng, names):
            for name in names:
                eng.sem_inc(S(name), 1)

        block = ctx.enter_context(nc.Block())

        @block.sync
        def _(sp):
            used = [0] * NSLOT
            freed = [(S(f"slot_free{c}"), 5) if c < 3 else None for c in range(NSLOT)]

            def load(s, dst, src, freed_by):
                if freed[s] is not None:
                    sp.wait_ge(*freed[s])
                sp.dma_start(dst, src).then_inc(S(f"slot_full{s}"), 16)
                used[s] += 1
                freed[s] = freed_by

            sp.dma_start(big[:, PERS + names2["c0"][0]:PERS + names2["c0"][0] + C0_N], ap["c0"]).then_inc(S("first_in"), 16)
            sp.dma_start(big[:, PERS + names2["v0"][0]:PERS + names2["v0"][0] + V0_N], ap["v0"]).then_inc(S("first_in"), 16)
            w = ap["w_ada"][0].rearrange("(k p) (j n) -> j p k n", p=P, n=512)
            with sp.Fori(0, 4) as i:
                for c in range(3):
                    sp.wait_ge(S(f"slot_free{c}"), i + 1)
                    sp.dma_start(slot(c, KT, 512), w[i * 3 + c]).then_inc(S(f"slot_full{c}"), 16)
            for c in range(3):
                used[c] += 4
            for n, a in enumerate(PROJ1):
                load(n % 3, slot(n % 3, KT, 512), cols(ap["w_in"][0], a, 512), (S("tile_in"), PROJ1_END[n]))
            for r in range(8):
                w = ap["ada_w_2"][r // 4].rearrange("(k p) (j n) -> j p k n", p=P, n=512)
                for q in range(3):
                    c = (1 + q) % 3
                    load(c, slot(c, KT, 512), w[r % 4 * 3 + q], (S(f"slot_free{c}"), 4 + r + 1 + 1))
            for n in range(2):
                load((n + 1) % 3, slot((n + 1) % 3, KT, 512), cols(ap["w_out"][0], 512 * n, 512),
                     (S("tile_in"), PROJ1_END[-1] + 4 * (n + 1)))
            sp.wait_ge(S("tile_in"), PROJ1_END[-1] + KT)
            free0 = [12, 12, 12, 0, 0, 0]
            wg, wu = (ap[n][0].rearrange("e (k p) f -> e p k f", p=P) for n in ("w_exp_gate", "w_exp_up"))
            wd = ap["w_exp_down"][0].rearrange("e (p t) n -> e p t n", t=FT)
            with sp.Fori(0, E) as i:
                for q in range(12):
                    s = q % 6
                    sp.wait_ge(S(f"slot_free{s}"), free0[s] + 2 * i + q // 6 + 1)
                    if q < 4:
                        dst, src = slot(s, 2, FF), wg[i][:, 2 * q:2 * q + 2, :]
                    elif q < 8:
                        dst, src = slot(s, 2, FF), wu[i][:, 2 * q - 8:2 * q - 6, :]
                    else:
                        a, b = DOWN_T[q - 8]
                        dst, src = slot(s, b - a, D), wd[i][:, a:b, :]
                    sp.dma_start(dst, src).then_inc(S(f"slot_full{s}"), 16)
            for s in range(NSLOT):
                used[s] += 2 * E
                freed[s] = (S(f"slot_free{s}"), free0[s] + 2 * E + 1)
            for layer in range(2):
                seq = 0
                groups = proj2_tiles(layer)
                n = PROJ2_AT[layer]
                for (a, b), g in zip(PARTS2, groups):
                    n += len(g)
                    load(seq, slot(seq, KT, 512), cols(ap["w_in_2"][layer], a * GW, 512), (S("tile_in"), n))
                    seq = (seq + 1) % NSLOT
                for q in range(2):
                    load(seq, slot(seq, KT, 512), cols(ap["w_out_2"][layer], 512 * q, 512),
                         (S("tile_in"), OUT2_AT[layer] + 4 * (q + 1)))
                    seq = (seq + 1) % NSLOT
                mlp_loads.append(used[:4])
                for s in range(4):
                    sp.wait_ge(*freed[s])
                w1 = ap["mlp_w1_2"][layer].rearrange("(k p) (j n) -> j p k n", p=P, n=512)
                w2 = ap["mlp_w2_2"][layer].rearrange("(j q p) n -> j p q n", q=4, p=P)
                with sp.Fori(0, 4) as i:
                    for c in range(2):
                        sp.wait_ge(S("w_lo_ready"), 64 * layer + 16 * i + 4 * c + 4)
                        sp.dma_start(slot(c, KT, 512), w1[i * 2 + c]).then_inc(S(f"slot_full{c}"), 16)
                    for c in range(2):
                        sp.wait_ge(S("w_lo_ready"), 64 * layer + 16 * i + 4 * c + 12)
                        sp.dma_start(slot(2 + c, 4, D), w2[i * 2 + c]).then_inc(S(f"slot_full{2 + c}"), 16)
                for c in range(2):
                    used[c] += 4
                    used[2 + c] += 4
                    freed[c] = (S("w_lo_ready"), 64 * (layer + 1) + 4 * c + 4)
                    freed[2 + c] = (S("w_lo_ready"), 64 * (layer + 1) + 4 * c + 12)
                    freed[4 + c] = (S("y_ps1"), 32 * (layer + 1) + 9)
            sp.wait_ge(S("final"), 1)
            sp.dma_start(out, resid[:, :, 0:T]).then_inc(S("stored"), 16)
            sp.wait_ge(S("stored"), 16)

        @block.gpsimd
        def _(pool):
            pool.dma_start(resid[:, :, 0:T], ap["xT"]).then_inc(S("tokens_in"), 16)
            pool.dma_start(resid[:, :, T:N2], ap["ctxT"]).then_inc(S("tokens_in"), 16)
            pool.dma_start(big[:, PERS + names2["cR"][0]:PERS + names2["cR"][0] + C1_N], ap["c1"]).then_inc(S("c1_in"), 16)
            pool.dma_start(wgz, cols(ap["w_in"][0], 1024, 32)).then_inc(S("c1_in"), 16)
            pool.dma_start(gw[0:33, :], ap["gw"]).then_inc(S("c1_in"), 16)
            pool.dma_start(wr, ap["wr"]).then_inc(S("c1_in"), 16)
            pool.wait_ge(S("h_d"), 1)
            pool.wait_ge(S("sq_a"), 1)
            pool.dma_start(resid[:, :, T:N2], ap["ctx2T"]).then_inc(S("second_in"), 16)
            pool.wait_ge(S("mix1_ready"), 1)
            at = PERS + names2["cR"][0]
            pool.dma_start(big[:, at:at + C2_N], ap["c2"]).then_inc(S("second_in"), 16)
            pool.dma_start(big[:, at + C2_N:at + C2_N + 1024], ap["sgw"]).then_inc(S("second_in"), 16)
            at = PERS + V2_BASE
            pool.dma_start(big[:, at:at + 2 * V2_N], ap["v2"]).then_inc(S("second_in"), 16)

        @block.tensor
        def _(pe):
            used = [0] * NSLOT
            tiles = Tiles()
            credit(pe, [f"slot_free{s}" for s in range(NSLOT)] + [f"ada_cols{c}" for c in range(3)]
                   + ["bc_ps", "z_ps", "h1_ps0", "h1_ps1"])
            for c in range(2):
                pe.sem_inc(S(f"y_ps{c}"), 9)

            def mm(o, l, r, start=True, stop=True):
                return nc.tensor.matmul(o, l, r, start=start, stop=stop)

            def take(s):
                pe.wait_ge(S(f"slot_full{s}"), 16 * (used[s] + 1))

            def ada_chunk(c, ring, before, b, block, banks):
                pe.wait_ge(S(f"slot_full{ring}"), b)
                pe.wait_ge(S(f"ada_part{c}"), before + 1)
                for kk in range(2):
                    for g in range(4):
                        k = 2 * g + kk
                        m = mm(PB[banks[c]][32 * g:32 * g + 32, :], csil[:, block, k, :],
                               slot(ring, KT, 512)[:, k, :], kk == 0, kk == 1)
                m.then_inc(S(f"slot_free{ring}"), 1)

            def ada_columns(c, before, first_row, banks):
                pe.wait_ge(S(f"ada_part{c}"), before + 2)
                for q in range(4):
                    m = mm(PB[banks[3]][:, bass.ds(first_row + 2 * q, 2)], part[:, c, q * P:(q + 1) * P], sel2)
                m.then_inc(S(f"ada_cols{c}"), 1)

            def ada_first():
                banks = (4, 5, 6, 7)
                with pe.Fori(0, 4) as i:
                    for c in range(3):
                        ada_chunk(c, c, i, 16 + i * 16, 0, banks)
                        ada_columns(c, i, i * 24 + 8 * c, banks)
                for c in range(3):
                    used[c] += 4

            def ada_round(r):
                banks = (0, 1, 2, 3)
                for c in range(3):
                    ring = (1 + c) % 3
                    ada_chunk(c, ring, 4 + r, 16 * (used[ring] + 1), 1, banks)
                    used[ring] += 1
                    if c:
                        ada_columns(c - 1, 4 + r, 96 * (r // 4) + (r % 4) * 24 + 8 * (c - 1), banks)
                ada_columns(2, 4 + r, 96 * (r // 4) + (r % 4) * 24 + 16, banks)

            def norm(k, n):
                pe.wait_ge(S("sq_a"), k + 1)
                pe.wait_ge(S("sq_d"), k + 1)
                for t in range(KT):
                    m = mm(PB[4][:, 0:n], ones, h[:, t, 0:n], t == 0, t == KT - 1)
                m.then_inc(S("ss"), 1)

            def bank_free(n):
                if n >= 4:
                    s, v = tiles.emptied(n - 4)
                    pe.wait_ge(s, v)

            def project(spec, weights, src, act_view=None):
                M, N, tok_major, col, tt, owner, _, _ = spec
                n = tiles.add(owner)
                bank_free(n)
                for k in range(KT):
                    if tok_major:
                        m = mm(PB[n % 4][0:M, 0:N], src[:, k, tt * P:(tt + 1) * P], weights[:, k, col:col + N],
                               k == 0, k == KT - 1)
                    else:
                        m = mm(PB[n % 4][0:M, 0:N], weights[:, k, col:col + P], src[:, k, 0:N],
                               k == 0, k == KT - 1)
                m.then_inc(S("tile_in"), 1)
                return m

            pe.wait_ge(S("first_in"), 32)
            pe.wait_ge(S("silu_c"), 2)
            ada_first()
            norm(0, N2)
            pe.wait_ge(S("h_a"), 1)
            pe.wait_ge(S("h_d"), 1)
            pe.wait_ge(S("c1_in"), 64)
            for n, group in enumerate(proj1_tiles()):
                take(n % 3)
                for spec in group:
                    m = project(spec, slot(n % 3, KT, 512), h)
                used[n % 3] += 1
                if n == 0:
                    q = tiles.add("D")
                    bank_free(q)
                    for k in range(KT):
                        m = mm(PB[q % 4][0:32, 0:N2], wgz[:, k, :], h[:, k, :], k == 0, k == KT - 1)
                    m.then_inc(S("tile_in"), 1)
                if n == 1:
                    pe.wait_ge(*tiles.emptied(q))
                    for tt in range(4):
                        m = mm(PB[4 + tt], gz[0:33, tt * P:(tt + 1) * P], gw[0:33, :])
                        m.then_inc(S("gate_ps"), 1)
            for x in ("A", "D"):
                pe.wait_ge(S("tile_out_" + x), tiles.owner.count(x))
            for r in (0,):
                ada_round(r)
            pe.wait_ge(S("la_ready"), 1)
            c0t, c1t = la[:, 2, :], la[:, 3, :]
            mm(PB[4][:, 0:256], c1("sufC", P), c0t[:, 0:256], True, False)
            mm(PB[4][:, 0:256], ones, c1t[:, 0:256], False, True)
            mm(PB[4][:, 256:512], c1("prefC", P), c0t[:, 256:512]).then_inc(S("kdec_ps"), 1)
            mm(PB[5][:, 0:256], c1("sufC", P), c1t[:, 0:256])
            mm(PB[5][:, 256:512], ones, c0t[:, 256:512], True, False)
            mm(PB[5][:, 256:512], c1("prefC", P), c1t[:, 256:512], False, True).then_inc(S("kdec_ps"), 1)
            for tt in range(2):
                mm(PB[6 + tt][:, 0:256], c1("sufS", P), la[:, tt, 0:256])
                mm(PB[6 + tt][:, 256:512], c1("prefS", P), la[:, tt, 256:512]).then_inc(S("kdec_ps"), 1)
            for d in range(2):
                pe.wait_ge(S("kdec_out"), d + 1)
                for ht in range(2):
                    for tt in range(2):
                        m = mm(PB[4 + d][:, ht * 256 + tt * P:ht * 256 + (tt + 1) * P],
                               la[:, tt, d * 256 + ht * P:d * 256 + (ht + 1) * P],
                               c1("prefI" if d == 0 else "sufI", P))
                m.then_inc(S("b_ps"), 1)
            for d in range(2):
                pe.wait_ge(S("kdec_out"), d + 3)
                for ht in range(2):
                    for tt in range(2):
                        m = mm(PB[6 + d][:, ht * 256 + tt * P:ht * 256 + (tt + 1) * P],
                               la[:, tt, d * 256 + ht * P:d * 256 + (ht + 1) * P],
                               c1("prefIm" if d == 0 else "sufIm", P))
                m.then_inc(S("bm_ps"), 1)
            for r in (1,):
                ada_round(r)
            pe.wait_ge(S("kwe_ready"), 1)
            pe.wait_ge(S("kwe_ready"), 2)
            pe.wait_ge(S("EA_ready"), 1)
            for d in range(2):
                for hh in range(GH):
                    for tt in range(2):
                        m = mm(PB[4][(hh % 2) * 64:(hh % 2) * 64 + 64, (d * 2 + hh // 2) * P:(d * 2 + hh // 2 + 1) * P],
                               kw[:, tt, d * 256 + hh * 64:d * 256 + hh * 64 + 64],
                               gv[:, 2 + tt, hh * P:(hh + 1) * P], tt == 0, tt == 1)
            m.then_inc(S("S0_ps"), 1)

            def chunk_update(bank, col, c, d):
                a = (c % 2) * 64
                for hh in range(GH):
                    m = mm(PB[bank][(hh % 2) * 64:(hh % 2) * 64 + 64, col + (hh // 2) * P:col + (hh // 2 + 1) * P],
                           ke[a:a + 64, c // 2, d * 256 + hh * 64:d * 256 + hh * 64 + 64],
                           gv[a:a + 64, c // 2, hh * P:(hh + 1) * P])
                return m
            chunk_update(5, 0, 0, 0)
            chunk_update(5, 256, 2, 0).then_inc(S("U_ps"), 1)
            pe.wait_ge(S("bm_out"), 1)
            chunk_update(6, 0, 2, 1).then_inc(S("U_ps"), 1)
            pe.wait_ge(S("bm_out"), 2)
            chunk_update(7, 0, 1, 0)
            chunk_update(7, 256, 1, 1).then_inc(S("U_ps"), 1)
            pe.wait_ge(S("S0_out"), 1)
            chunk_update(4, 0, 3, 1).then_inc(S("U_ps"), 1)
            for r in (2,):
                ada_round(r)
            pe.wait_ge(S("states_done"), 1)
            pe.wait_ge(S("qk_ready"), 1)
            for hp2 in range(2):
                for c in range(NC):
                    for hp in range(2):
                        for d in range(2):
                            a = hp2 * 64
                            col = (((c // 2) * 2 + hp) * 2 + d) * 64
                            m = mm(PB[4 + hp2][(c % 2) * 64:(c % 2) * 64 + 64, col:col + 64],
                                   kd[a:a + 64, d, hp * 256 + c * 64:hp * 256 + c * 64 + 64],
                                   qd[a:a + 64, d, hp * 256 + c * 64:hp * 256 + c * 64 + 64])
                m.then_inc(S("gsc_ps"), 1)
            for r in (3,):
                ada_round(r)
            pe.wait_ge(S("pg_ready"), 1)
            for hh in range(GH):
                for tt in range(2):
                    m = mm(PB[6 + hh // 2][:, (hh % 2) * 256 + tt * P:(hh % 2) * 256 + (tt + 1) * P],
                           gv[:, tt, hh * P:(hh + 1) * P], pg[:, hh % 2, tt * 2 + hh // 2, :])
            m.then_inc(S("gi_ps"), 1)
            for hp2 in range(2):
                a = hp2 * 64
                for hp in range(2):
                    for c in range(NC):
                        for d in range(2):
                            m = mm(PB[4 + hp2][:, hp * 256 + c * 64:hp * 256 + c * 64 + 64],
                                   Sg[a:a + 64, d, c, hp, :], qe[a:a + 64, d, hp * 256 + c * 64:hp * 256 + c * 64 + 64],
                                   d == 0, d == 1)
                m.then_inc(S("gj_ps"), 1)

            for r in (4, 5):
                ada_round(r)
            pe.wait_ge(S("kwr_ready"), 1)
            pe.wait_ge(S("og_ready"), 1)
            for d in range(2):
                for hh in range(RH):
                    for tt in range(2):
                        m = mm(PB[4 + d][:, hh * P:(hh + 1) * P], kwr[:, tt, d, hh * P:(hh + 1) * P],
                               rv[:, 2 + tt, hh * P:(hh + 1) * P], tt == 0, tt == 1)
            m.then_inc(S("Sr_ps"), 1)
            for n, src in enumerate((rq, rk)):
                for half in range(2):
                    b = 6 + half
                    if n:
                        pe.wait_ge(S("rope_out"), half + 1)
                    m = mm(PB[b], c1("rot1", P), src[:, 2 * half:2 * half + 2, :])
                    m.then_inc(S("rope_ps"), 1)
            for r in (6,):
                ada_round(r)
            pe.wait_ge(S("rk_ready"), 1)
            pe.wait_ge(S("Sr_out"), 1)
            for hh in range(RH):
                b = hh % 2
                if hh >= 2:
                    pe.wait_ge(S("pr_ready"), hh - 1)
                for jt in range(2):
                    m = mm(PB[4 + b][:, jt * T:(jt + 1) * T], rk[:, hh, jt * P:(jt + 1) * P], rq[:, hh, :])
                m.then_inc(S("rsc_ps"), 1)
                pe.wait_ge(S("pr_ready"), hh + 1)
                pe.wait_ge(S("rqd_ready"), hh + 1)
                if hh >= 2:
                    pe.wait_ge(S("or_out"), hh - 1)
                for jt in range(2):
                    mm(PB[6 + b][:, 0:T], rv[:, jt, hh * P:(hh + 1) * P], pr[:, b, jt * T:(jt + 1) * T], jt == 0, False)
                for d in range(2):
                    m = mm(PB[6 + b][:, 0:T], Sr[:, d, hh, :], rqd[:, b, d * T:(d + 1) * T], False, d == 1)
                m.then_inc(S("or_ps"), 1)
            pe.wait_ge(S("gsq_ready"), 1)
            for half in range(2):
                m = mm(PB[4 + half], ones, gn_t[:, 2 * half:2 * half + 2, :])
            m.then_inc(S("hnorm_ps"), 1)
            pe.wait_ge(S("or_out"), 4)
            for half in range(2):
                m = mm(PB[6 + half], ones, orr[:, 2 * half:2 * half + 2, :])
            m.then_inc(S("hnorm_ps"), 1)
            pe.wait_ge(S("rsq_ready"), 1)
            for half in range(2):
                m = mm(PB[6 + half], ones, gn_t[:, 2 * half:2 * half + 2, :])
            m.then_inc(S("hnorm_ps"), 1)
            for r in (7,):
                ada_round(r)
            pe.wait_ge(S("mix1_ready"), 1)
            pe.wait_ge(S("mod_out"), 3)
            for n in range(2):
                s = (n + 1) % 3
                take(s)
                for m_ in range(4):
                    m = project((P, T, False, m_ * P, None, "D", None, None), slot(s, KT, 512), mixb1)
                used[s] += 1

            pe.wait_ge(S("tile_out_D"), tiles.owner.count("D"))
            norm(1, T)
            pe.wait_ge(S("h_a"), 2)
            for tt in range(2):
                for k in range(KT):
                    m = mm(PB[5][:, tt * E:(tt + 1) * E], h[:, k, tt * P:(tt + 1) * P], wr[:, k, :], k == 0, k == KT - 1)
            m.then_inc(S("router_ps"), 1)
            for q in range(4):
                for k in range(4):
                    m = nc.tensor.transpose(PB[q][:, k * P:(k + 1) * P],
                                            h[:, (q % 2) * 4 + k, (q // 2) * P:(q // 2 + 1) * P], ident)
                m.then_inc(S("htm_ps"), 1)
            pe.wait_ge(S("routed"), 2)
            for tt in range(2):
                m = nc.tensor.transpose(PB[6][0:E, tt * P:(tt + 1) * P], aff[:, tt, :], ident)
            m.then_inc(S("router_ps"), 1)
            pe.wait_ge(S("routed"), 3)
            for tt in range(2):
                m = nc.tensor.transpose(PB[7][:, tt * E:(tt + 1) * E], mkT[:, tt * P:(tt + 1) * P], ident[0:E, 0:E])
            m.then_inc(S("router_ps"), 1)
            pe.wait_ge(S("routed"), 4)
            mm(PB[4][:, 0:E], c0("incl", P), mk[:, 0, :])
            mm(PB[4][:, E:2 * E], ones, mk[:, 0, :], True, False)
            mm(PB[4][:, E:2 * E], c0("incl", P), mk[:, 1, :], False, True).then_inc(S("router_ps"), 1)
            pe.wait_ge(S("routed"), 5)
            for tt in range(2):
                m = nc.tensor.transpose(PB[6][0:E, tt * P:(tt + 1) * P], pos[:, tt, :], ident)
            m.then_inc(S("router_ps"), 1)
            pe.wait_ge(S("routed"), 6)
            pe.wait_ge(S("htm_out"), 4)
            for k in range(KT):
                if k >= 4:
                    pe.wait_ge(S("xeT_out"), k - 3)
                for tt in range(2):
                    m = mm(PB[k % 4], htm[:, tt, k * P:(k + 1) * P], sel[:, tt, :], tt == 0, tt == 1)
                m.then_inc(S("xeT_ps"), 1)
            pe.wait_ge(S("xeT_out"), KT)
            pe.wait_ge(S("routed"), 7)
            free0 = [12, 12, 12, 0, 0, 0]
            with pe.Fori(0, E) as i:
                pe.wait_ge(S("xe_ready"), i + 1)
                pe.wait_ge(S("gs_out"), i + 1)
                for q in range(12):
                    s = q % 6
                    if q == 4:
                        pe.wait_ge(S("gu_ready"), i + 1)
                    if q == 8:
                        pe.wait_ge(S("bcm_ready"), i + 1)
                        pe.wait_ge(S("bcs_out"), i + 1)
                        mm(PB[7], ones[0:E, :], bcm).then_inc(S("bc_ps"), 1)
                        pe.wait_ge(S("hx_ready"), i + 1)
                        pe.wait_ge(S("ye_out"), i + 1)
                    pe.wait_ge(S(f"slot_full{s}"), 16 * (used[s] + 1 + q // 6) + i * 32)
                    if q < 8:
                        for kk in range(2):
                            k = 2 * (q % 4) + kk
                            for g in range(4):
                                m = mm(PB[4 + q // 4][32 * g:32 * g + 32, 0:FQ], xe[:, k, :],
                                       slot(s, 2, FF)[:, kk, g * FQ:(g + 1) * FQ], k == 0, k == KT - 1)
                    else:
                        a, b = DOWN_T[q - 8]
                        for t in range(a, b):
                            for g in range(4):
                                m = mm(PB[6][32 * g:32 * g + 32, 0:256], hx[:, t, :],
                                       slot(s, b - a, D)[:, t - a, g * 256:(g + 1) * 256], t == 0, t == FT - 1)
                    m.then_inc(S(f"slot_free{s}"), 1)
                pe.wait_ge(S("ye_out"), i + 1 + 1)
                pe.wait_ge(S("selg_ready"), i + 1 + 1)
                pe.wait_ge(S("acc_done"), i + 1)
                for g in range(4):
                    for x in range(2):
                        m = mm(PB[g][:, x * T:(x + 1) * T], ye[32 * g:32 * g + 32, x * P:(x + 1) * P],
                               selg[32 * g:32 * g + 32, :])
                m.then_inc(S("z_ps"), 1)
            for s in range(NSLOT):
                used[s] += 2 * E
            pe.wait_ge(S("acc_done"), E + 1)
            norm(2, T)
            pe.wait_ge(S("second_in"), 64)
            for layer in range(2):
                nf = N2 if layer == 0 else T
                k0 = 3 + 2 * layer
                norm(k0, N2)
                pe.wait_ge(S("h_a"), affine_no(k0) + 1)
                pe.wait_ge(S("h_d"), wide_no(k0) + 1)
                seq = 0
                for group in proj2_tiles(layer):
                    take(seq)
                    for spec in group:
                        project(spec, slot(seq, KT, 512), h)
                    used[seq] += 1
                    seq = (seq + 1) % NSLOT
                for x in ("A", "D"):
                    pe.wait_ge(S("tile_out_" + x), tiles.owner.count(x))
                mm(PB[4], c2("rot2", P), qf[:, :, 0:T]).then_inc(S("rope2_ps"), 1)
                mm(PB[5], c2("rot2", P), kf[:, :, 0:T]).then_inc(S("rope2_ps"), 1)
                for r in range(2):
                    pe.wait_ge(S("ln_in"), 2 * layer + r + 1)
                    for m_ in range(2):
                        src = acca if r == 0 else tg
                        m = mm(PB[6][:, 0:nf], ones, src[:, m_, 0:nf], m_ == 0, m_ == 1)
                    m.then_inc(S("ln_ps"), 1)
                pe.wait_ge(S("svn_ready"), layer + 1)
                for g in range(4):
                    for x in range(nf // P):
                        m = mm(PB[2 + g // 2][(g % 2) * 64:(g % 2) * 64 + 64, x * P:(x + 1) * P],
                               sv[:, x, g * 64:(g + 1) * 64], sgw[:, layer, g, :])
                m.then_inc(S("sg_ps"), 1)
                pe.wait_ge(S("qk2_ready"), layer + 1)
                pe.wait_ge(S("mixers_done"), layer + 1)
                units = attn_units(layer)
                u0 = UNIT_AT[layer]

                def scores(u):
                    s_, qt, hh = units[u]
                    if u >= 2:
                        pe.wait_ge(S("exp_done"), u0 + u - 1)
                    a, nk = (hh % 2) * 64, 512 if s_ == 0 else 256
                    for comp in range(2):
                        r = slice(a + 32 * comp, a + 32 * comp + 32)
                        m = mm(PB[2 * (u % 2) + comp][:, 0:nk], qf[r, hh // 2, s_ * T + qt * P:s_ * T + (qt + 1) * P],
                               kf[r, hh // 2, N2 - nk:N2])
                    m.then_inc(S("asc_ps"), 1)

                scores(0)
                scores(1)
                for u, (s_, qt, hh) in enumerate(units):
                    nkt = 4 if s_ == 0 else 2
                    pe.wait_ge(S("w_ready"), u0 + u + 1)
                    if u >= 2:
                        pe.wait_ge(S("wt_ready"), u0 + u - 1)
                    for kt in range(nkt):
                        m = nc.tensor.transpose(PB[4 + u % 2][:, kt * P:(kt + 1) * P],
                                                Eb[:, u % 2, 0, kt * P:(kt + 1) * P], ident)
                    m.then_inc(S("wt_ps"), 1)
                    if u + 2 < len(units):
                        scores(u + 2)
                    pe.wait_ge(S("wt_ready"), u0 + u + 1)
                    for kt in range(nkt):
                        m = mm(PB[6 + s_][(hh % 2) * 64:(hh % 2) * 64 + 64,
                                          (hh // 2) * T + qt * P:(hh // 2) * T + (qt + 1) * P],
                               vt[:, 4 - nkt + kt, hh * 64:(hh + 1) * 64], WT[:, u % 2, kt * P:(kt + 1) * P],
                               kt == 0, kt == nkt - 1)
                    m.then_inc(S("pv_ps"), 1)
                pe.wait_ge(S("osq_ready"), layer + 1)
                for m_ in range(2):
                    m = mm(PB[m_][:, 0:nf], c2("ones64", P), tg[:, m_, 0:nf])
                m.then_inc(S("oss_ps"), 1)
                pe.wait_ge(S("mix2_ready"), layer + 1)
                for q in range(2):
                    take(seq)
                    for m_ in range(4):
                        project((P, nf, False, m_ * P, None, "D", None, None), slot(seq, KT, 512), mix)
                    used[seq] += 1
                    seq = (seq + 1) % NSLOT
                pe.wait_ge(S("tile_out_D"), tiles.owner.count("D"))
                norm(k0 + 1, nf)
                pe.wait_ge(S("h_a"), affine_no(k0 + 1) + 1)
                if nf == N2:
                    pe.wait_ge(S("h_d"), wide_no(k0 + 1) + 1)
                pe.wait_ge(S("h_split"), KT * (layer + 1))

                def split_product(o, wa, k, m, hi, lo, first, last):
                    wh, wl = (w_split(t, wa)[:, k, m * P:(m + 1) * P] for t in (w_hi, w_lo))
                    mm(o, wh, hi, first, False)
                    mm(o, wl, hi, False, False)
                    return mm(o, wh, lo, False, last)

                with pe.Fori(0, 4) as i:
                    for c in range(2):
                        for q in range(4):
                            n = 4 * c + q
                            pe.wait_ge(S("w_lo_ready"), 64 * layer + 16 * i + n + 17)
                            pe.wait_ge(S("h1_relu"), 32 * layer + 8 * i + n + 1)
                            for k in range(KT):
                                m = split_product(PB[q][:, 0:nf], n, k, 0, h_hi[k][:, 0:nf], h_lo[k][:, 0:nf],
                                                  k == 0, k == KT - 1)
                            m.then_inc(S(f"h1_ps{c}"), 1)
                    for c in range(2):
                        pe.wait_ge(S("h1_ready"), 32 * layer + 8 * i + 4 * c + 4)
                        for dt in range(KT):
                            n = 8 + 4 * c + dt // 2
                            if dt % 2 == 0:
                                pe.wait_ge(S("w_lo_ready"), 64 * layer + 16 * i + n + 17)
                            pe.wait_ge(S("y_out"), 64 * layer + 16 * i + 8 * c + dt + 1)
                            for q in range(4):
                                m = split_product(PB[4 + dt % 4][:, 0:nf], n, q, dt % 2, h1_hi[c][:, q, 0:nf],
                                                  h1_lo[c][:, q, 0:nf], q == 0, q == 3)
                            m.then_inc(S(f"y_ps{c}"), 1)
                for s in range(4):
                    used[s] += 4
                pe.wait_ge(S("y_out"), 64 * (layer + 1) + 4)
            norm(7, T)

        NORM_SETS = [(0, 0, 8), (0, 1, 32), (1, 3, 8), (1, 5, 32), (2, 4, 8), (2, 6, 32)]
        U_AT = {(0, 0): (5, 0), (2, 0): (5, 256), (2, 1): (6, 0), (1, 0): (7, 0), (1, 1): (7, 256), (3, 1): (4, 0)}

        @block.scalar
        def _(act):
            link = linker(act, "act_chain")
            A = nc.scalar.activation
            credit(act, [f"ada_part{c}" for c in range(3)] + ["gs_out", "bcs_out", "ye_out"])
            act.sem_inc(S("h1_relu"), 4)
            ntile = [0]

            def ada_first():
                with act.Fori(0, 4) as i:
                    for c in range(3):
                        act.wait_ge(S(f"slot_free{c}"), i + 2)
                        act.wait_ge(S(f"ada_cols{c}"), i + 1)
                        A(part[:, c, :], PB[4 + c], ACT.Copy).then_inc(S(f"ada_part{c}"), 1)

            def ada_round(r):
                for c in range(3):
                    act.wait_ge(S(f"slot_free{(1 + c) % 3}"), 4 + r + 2)
                    act.wait_ge(S(f"ada_cols{c}"), 4 + r + 1)
                    A(part[:, c, :], PB[c], ACT.Copy).then_inc(S(f"ada_part{c}"), 1)

            def norm_squares(k, n):
                A(h[:, 0:4, 0:n], resid[:, 0:4, 0:n], ACT.Square).then_inc(S("sq_a"), 1)

            def norm_sqrt(k, n):
                act.wait_ge(S("ms"), k + 1)
                A(rs[:, 0:n], rs[:, 0:n], ACT.Sqrt).then_inc(S("rms"), 1)

            def norm_affine(k):
                act.wait_ge(S("hn"), affine_no(k) + 1)
                a = NORMS[k][0]
                layer, _, row = NORM_SETS[a]
                for t in range(KT):
                    i_ = A(h[:, t, 0:T], h[:, t, 0:T], ACT.Identity, bias=modv[:, layer, row - 8 + t, 0:1],
                           scale=asc[:, a, t, 0:1])
                i_.then_inc(S("h_a"), 1)

            def tile_out(ins_fn):
                ins_fn().then_inc(S("tile_out_A"), 1)

            act.wait_ge(S("first_in"), 32)
            act.wait_ge(S("csil_zero"), 1)
            for b in range(2):
                A(csil[:, b, :, 0:2], v0("cv", 2, 2, KT)[:, b, :, :].rearrange("p s k -> p k s"), ACT.Silu) \
                    .then_inc(S("silu_c"), 1)
            A(lg[:, 1, :], v0("rdl", 8), ACT.Abs).then_inc(S("lg_steps"), 1)
            ada_first()
            act.wait_ge(S("tokens_in"), 32)
            norm_squares(0, N2)
            norm_sqrt(0, N2)
            norm_affine(0)
            n = 0
            for g, group in enumerate(proj1_tiles()):
                if g == 1:
                    n += 1
                if g == 2:
                    for tt in range(4):
                        act.wait_ge(S("gate_ps"), tt + 1)
                        A(la[:, tt, :], PB[4 + tt], ACT.Copy).then_inc(S("gate_out"), 1)
                for M, N, _, _, _, owner, dst, func in group:
                    if owner == "A":
                        act.wait_ge(S("tile_in"), n + 1)
                        if func == "silu":
                            i_ = A(dst, PB[n % 4][0:M, 0:N], ACT.Silu)
                        else:
                            i_ = A(dst, PB[n % 4][0:M, 0:N], ACT.Copy, scale=func or 1.0)
                        i_.then_inc(S("tile_out_A"), 1)
                    n += 1
            act.wait_ge(S("gate_out"), 4)
            link(A(lt, la, ACT.Abs))
            link(A(lt, lt, ACT.Exp, scale=-1.0))
            act.wait_ge(S("lg_steps"), 1)
            link(A(lg[:, 1, :], lg[:, 1, :], ACT.Exp, scale=-1.0))
            A(lt, lt, ACT.Ln, bias=1.0).then_inc(S("lt_ready"), 1)
            A(lg[:, 1, :], lg[:, 1, :], ACT.Ln, bias=1.0).then_inc(S("lg_steps"), 1)
            for r in (0,):
                ada_round(r)
            for n in range(4):
                act.wait_ge(S("kdec_ps"), n + 1)
                dst = kw[:, n, :] if n < 2 else ke[:, n - 2, :]
                A(dst, PB[4 + n], ACT.Exp, scale=1 / GATE_TAU).then_inc(S("kdec_out"), 1)
            for d in range(2):
                act.wait_ge(S("b_ps"), d + 1)
                i_ = A(EA[:, d, :], PB[4 + d], ACT.Exp, scale=1 / GATE_TAU)
            i_.then_inc(S("EA_ready"), 1)
            act.wait_ge(S("bm_out"), 2)
            link(A(ep, em, ACT.Exp, scale=1 / GATE_TAU))
            A(em, em, ACT.Exp, scale=-1 / GATE_TAU).then_inc(S("e_ready"), 1)
            act.wait_ge(S("wk_in"), 1)
            A(wk, wk, ACT.Exp).then_inc(S("wk_ready"), 1)
            for r in (1, 2, 3):
                ada_round(r)
            for hp2 in range(2):
                act.wait_ge(S("gj_ps"), hp2 + 1)
                A(og[:, hp2:GH:2, :], PB[4 + hp2][:, :].rearrange("p (a b) -> p a b", a=2), ACT.Copy).then_inc(S("j_out"), 1)
            for r in (4, 5):
                ada_round(r)
            act.wait_ge(S("Sr_ps"), 1)
            for d in range(2):
                i_ = A(Sr[:, d, :, :], PB[4 + d][:, :].rearrange("p (a b) -> p a b", a=4), ACT.Copy)
            i_.then_inc(S("Sr_out"), 1)
            for r in (6,):
                ada_round(r)
            act.wait_ge(S("lg_ready"), 1)
            act.wait_ge(S("og_ready"), 1)

            def decays(hh):
                b = hh % 2
                if hh >= 2:
                    act.wait_ge(S("pr_ready"), hh - 1)
                    act.wait_ge(S("or_ps"), hh - 1)
                for d in range(2):
                    i_ = A(dec[:, b, d * 512:(d + 1) * 512], c1("rel", 2, 512)[:, d, :], ACT.Exp,
                           scale=lg[:, 0, d * 4 + hh:d * 4 + hh + 1])
                i_.then_inc(S("dec_in"), 1)
                for d in range(2):
                    i_ = A(rqd[:, b, d * T:(d + 1) * T], c1("qpos", 2, T)[:, d, :], ACT.Exp,
                           scale=lg[:, 0, d * 4 + hh:d * 4 + hh + 1])
                i_.then_inc(S("rqe"), 1)

            decays(0)
            for hh in range(RH):
                if hh + 1 < RH:
                    decays(hh + 1)
                act.wait_ge(S("or_ps"), hh + 1)
                A(orr[:, hh, :], PB[6 + hh % 2][:, 0:T], ACT.Copy).then_inc(S("or_out"), 1)
            act.wait_ge(S("hn_ms"), 1)
            A(tmp1, tmp1, ACT.Sqrt).then_inc(S("hn_rms"), 1)
            ada_round(7)

            def norm(k):
                n = NORMS[k][2]
                norm_squares(k, n)
                norm_sqrt(k, n)
                if NORMS[k][0] is not None:
                    norm_affine(k)

            act.wait_ge(S("tile_out_D"), 13 + KT)
            norm(1)
            for q in range(4):
                act.wait_ge(S("htm_ps"), q + 1)
                A(htm[:, q // 2, (q % 2) * 512:(q % 2 + 1) * 512], PB[q], ACT.Copy).then_inc(S("htm_out"), 1)
            act.wait_ge(S("routed"), 1)
            A(aff, aff, ACT.Exp).then_inc(S("affe"), 1)
            for k in range(KT):
                act.wait_ge(S("xeT_ps"), k + 1)
                A(xeT[:, k, :], PB[k % 4], ACT.Copy).then_inc(S("xeT_out"), 1)
            act.wait_ge(S("xeT_out"), KT)
            with act.Fori(0, E) as i:
                act.wait_ge(S("slot_free1"), 12 + 2 * i + 1)
                A(xe, xeT[:, :, bass.ds(i * CAP, CAP)], ACT.Copy).then_inc(S("xe_ready"), 1)
                act.wait_ge(S("slot_free3"), 2 * i + 1 + 1)
                act.wait_ge(S("gu_ready"), i + 1)
                A(gs, PB[4][:, 0:FQ], ACT.Silu).then_inc(S("gs_out"), 1)
                act.wait_ge(S("bc_ps"), i + 1 + 1)
                act.wait_ge(S("selg_ready"), i + 1)
                A(bcs, PB[7], ACT.Copy).then_inc(S("bcs_out"), 1)
                act.wait_ge(S("slot_free5"), 2 * i + 2 + 1)
                act.wait_ge(S("z_ps"), i + 1)
                A(ye, PB[6][:, 0:256], ACT.Copy).then_inc(S("ye_out"), 1)
            act.wait_ge(S("acc_done"), E + 1)
            norm(2)
            act.wait_ge(S("x_in2"), 1)
            act.wait_ge(S("second_in"), 64)
            FUNC = {None: ACT.Copy, "silu": ACT.Silu, "gelu": ACT.Gelu_apprx_tanh, "sigmoid": ACT.Sigmoid}
            for layer in range(2):
                nf = N2 if layer == 0 else T
                k0 = 3 + 2 * layer
                norm(k0)
                n = PROJ2_AT[layer]
                for group in proj2_tiles(layer):
                    for M, N, _, _, _, owner, dst, func in group:
                        if owner == "A":
                            act.wait_ge(S("tile_in"), n + 1)
                            A(dst, PB[n % 4][0:M, 0:N], FUNC[func]).then_inc(S("tile_out_A"), 1)
                        n += 1
                act.wait_ge(S("lam_in"), layer + 1)
                A(s4[:, 2:4], s4[:, 0:2], ACT.Exp).then_inc(S("lam_exp"), 1)
                act.wait_ge(S("ln_var"), layer + 1)
                A(rs[:, 0:nf], rs[:, 0:nf], ACT.Sqrt).then_inc(S("ln_std"), 1)
                act.wait_ge(S("sv_var"), layer + 1)
                A(s4[:, 12:12 + nf // P], s4[:, 12:12 + nf // P], ACT.Sqrt).then_inc(S("sv_std"), 1)
                act.wait_ge(S("ln_out"), layer + 1)
                for m_ in range(2):
                    i_ = A(mix[:, m_, 0:nf], acca[:, m_, 0:nf], ACT.Silu, bias=v2(layer, "lab", 2)[:, m_:m_ + 1],
                           scale=v2(layer, "lag", 2)[:, m_:m_ + 1])
                i_.then_inc(S("ya_ready"), 1)
                units = attn_units(layer)
                u0 = UNIT_AT[layer]

                def exps(u):
                    nk = 512 if units[u][0] == 0 else 256
                    act.wait_ge(S("amax"), u0 + u + 1)
                    if u >= 2:
                        act.wait_ge(S("wt_ps"), u0 + u - 1)
                    for comp in range(2):
                        i_ = A(Eb[:, u % 2, comp, 0:nk], PB[2 * (u % 2) + comp][:, 0:nk], ACT.Exp,
                               bias=s4[:, 16 + 2 * (u % 2) + comp:17 + 2 * (u % 2) + comp], scale=float(DQ) ** -0.5,
                               accum_out=s4[:, 20 + 2 * (u % 2) + comp:21 + 2 * (u % 2) + comp])
                    i_.then_inc(S("exp_done"), 1)

                exps(0)
                for u, (s_, qt, hh) in enumerate(units):
                    if u + 1 < len(units):
                        exps(u + 1)
                    nk = 512 if s_ == 0 else 256
                    act.wait_ge(S("wt_ps"), u0 + u + 1)
                    if u >= 2:
                        act.wait_ge(S("pv_ps"), u0 + u - 1)
                    A(WT[:, u % 2, 0:nk], PB[4 + u % 2][:, 0:nk], ACT.Copy).then_inc(S("wt_ready"), 1)
                act.wait_ge(S("o_ms"), layer + 1)
                A(tc[:, :, 0:nf], tc[:, :, 0:nf], ACT.Sqrt).then_inc(S("o_rms"), 1)
                act.wait_ge(S("tile_out_D"), D_TILES_AFTER_OUT[layer])
                norm(k0 + 1)
                if nf == N2:
                    act.wait_ge(S("h_d"), wide_no(k0 + 1) + 1)
                link(A(s4[:, 58:59], s4[:, 58:59], ACT.Copy))
                for k in range(KT):
                    A(h_hi[k][:, 0:nf], h[:, k, 0:nf], ACT.Copy).then_inc(S("h_hi_ready"), 1)
                with act.Fori(0, 4) as i:
                    for n in range(16):
                        if n % 4 == 0:
                            s = n // 4
                            act.wait_ge(S(f"slot_full{s}"), 16 * (mlp_loads[layer][s] + 1) + i * 16)
                        act.wait_ge(*unit_done(layer, i, n - NWB))
                        if 4 <= n < 12:
                            c, q = (n - 4) // 4, n % 4
                            act.wait_ge(*unit_done(layer, i - 1, 11 + 4 * c))
                            A(h1[:, c, q, 0:nf], PB[q][:, 0:nf], ACT.Relu).then_inc(S("h1_relu"), 1)
                        A(w_split(w_hi, n), w_unit(n), ACT.Copy).then_inc(S("w_hi_ready"), 1)
                        if 4 <= n < 12:
                            act.wait_ge(S("h1_sq"), 32 * layer + 8 * i + n - 4 + 1)
                            A(h1_hi[c][:, q, 0:nf], h1[:, c, q, 0:nf], ACT.Copy).then_inc(S("h1_hi_ready"), 1)
                act.wait_ge(S("y_out"), 64 * (layer + 1) + 4)
            norm(7)

        @block.vector
        def _(dve):
            link = linker(dve, "dve_chain")
            V = nc.vector
            credit(dve, ["gu_ready", "acc_done", "selg_ready"])
            dve.sem_inc(S("w_lo_ready"), 16)
            dve.sem_inc(S("y_out"), 4)

            def tt(o, a, b, op):
                return V.tensor_tensor(o, a, b, op)

            def norm_squares(k, n):
                tt(h[:, 4:8, 0:n], resid[:, 4:8, 0:n], resid[:, 4:8, 0:n], ALU.mult).then_inc(S("sq_d"), 1)

            def norm_final(k, n, w):
                for t in range(KT):
                    i_ = V.scalar_tensor_tensor(resid[:, t, 0:n], resid[:, t, 0:n], v0("norms", 8, KT)[:, w, t:t + 1],
                                                rs[:, 0:n], ALU.mult, ALU.mult)
                return i_

            def norm_rest(k, n):
                dve.wait_ge(S("ss"), k + 1)
                V.tensor_scalar(rs[:, 0:n], PB[4][:, 0:n], 1.0 / D, EPS, ALU.mult, ALU.add).then_inc(S("ms"), 1)
                dve.wait_ge(S("rms"), k + 1)
                link(V.reciprocal(rs[:, 0:n], rs[:, 0:n]))
                a, w, _ = NORMS[k]
                if a is None:
                    return norm_final(k, n, w)
                tt(h[:, :, 0:T], resid[:, :, 0:T], bc(rs[:, 0:T], 1, [P, KT, T]), ALU.mult).then_inc(S("hn"), 1)
                if n > T:
                    layer, _, row = NORM_SETS[a]
                    link(tt(h[:, :, T:N2], resid[:, :, T:N2], bc(rs[:, T:N2], 1, [P, KT, T]), ALU.mult))
                    for t in range(KT):
                        i_ = V.tensor_scalar(h[:, t, T:N2], h[:, t, T:N2], asc[:, a, t, 1:2],
                                             modv[:, layer, row - 8 + t, 1:2], ALU.mult, ALU.add)
                    i_.then_inc(S("h_d"), 1)

            TAPS_AT = [0]
            d_out = [n_d(proj1_tiles()) + 1 + KT]
            V.memset(csil, 0.0).then_inc(S("csil_zero"), 1)
            V.memset(gz[32:33, :], 1.0)
            dve.wait_ge(S("tokens_in"), 32)
            norm_squares(0, N2)
            def modulation(layers, rounds, bank, sets):
                for c in range(3):
                    dve.wait_ge(S(f"ada_cols{c}"), rounds + 1)
                for x, layer in enumerate(layers):
                    tt(modv[:, layer, :, :], PB[bank][:, 96 * x:96 * x + 96].rearrange("p (a b) -> p a b", a=48),
                       bc(v0("bada", 3, 48)[:, layer, :], 2, [P, 48, 2]), ALU.add).then_inc(S("mod_out"), 1)
                dve.wait_ge(S("mod_out"), layers[-1] + 1)
                for k in sets:
                    layer, w, row = NORM_SETS[k]
                    i_ = V.scalar_tensor_tensor(asc[:, k, :, :], modv[:, layer, row:row + 8, :], 1.0,
                                                bc(v0("norms", 8, KT)[:, w, :], 2, [P, KT, 2]), ALU.add, ALU.mult)
                link(i_)

            dve.wait_ge(S("first_in"), 32)
            modulation([0], 4, 7, (0, 1))
            norm_rest(0, N2)
            n = 0
            for g, group in enumerate(proj1_tiles()):
                for M, N, _, _, _, owner, dst, func in group:
                    if owner == "D":
                        dve.wait_ge(S("tile_in"), n + 1)
                        V.tensor_copy(dst, PB[n % 4][0:M, 0:N]).then_inc(S("tile_out_D"), 1)
                    n += 1
                if g == 0:
                    dve.wait_ge(S("tile_in"), n + 1)
                    V.tensor_copy(gz[0:32, :], PB[n % 4][0:32, 0:N2]).then_inc(S("tile_out_D"), 1)
                    n += 1
            dve.wait_ge(S("lt_ready"), 1)
            V.scalar_tensor_tensor(la, la, 0.0, lt, ALU.min, ALU.subtract).then_inc(S("la_ready"), 1)
            dve.wait_ge(S("lg_steps"), 2)
            V.scalar_tensor_tensor(lg[:, 0, :], v0("rdl", 8), 0.0, lg[:, 1, :], ALU.min, ALU.subtract) \
                .then_inc(S("lg_ready"), 1)
            dve.wait_ge(S("c1_in"), 64)
            dve.wait_ge(S("lg_ready"), 1)
            tt(wk, c1("kpos", 2, 8), bc(lg[:, 0, :], 1, [P, 2, 8]), ALU.mult).then_inc(S("wk_in"), 1)
            dve.wait_ge(S("kdec_out"), 2)
            for x in range(2):
                i_ = tt(kw[:, x, :].rearrange("p (a b) -> p a b", a=2), kw[:, x, :].rearrange("p (a b) -> p a b", a=2),
                        bc(gktm[:, 2 + x, :], 1, [P, 2, 256]), ALU.mult)
            i_.then_inc(S("kwe_ready"), 1)
            dve.wait_ge(S("kdec_out"), 4)
            for x in range(2):
                i_ = tt(ke[:, x, :].rearrange("p (a b) -> p a b", a=2), ke[:, x, :].rearrange("p (a b) -> p a b", a=2),
                        bc(gktm[:, x, :], 1, [P, 2, 256]), ALU.mult)
            i_.then_inc(S("kwe_ready"), 1)
            dve.wait_ge(S("tile_in"), PROJ1_END[-1])
            for d in range(2):
                dve.wait_ge(S("bm_ps"), d + 1)
                V.tensor_scalar(em[:, d, :], PB[6 + d], EXP_CLAMP * GATE_TAU, -EXP_CLAMP * GATE_TAU,
                                ALU.min, ALU.max).then_inc(S("bm_out"), 1)
            dve.wait_ge(S("EA_ready"), 1)
            gq2, gk2 = b1("gq", 512), b1("gk", 512)
            tt(qe, EA, bc(gq2, 1, [P, 2, 512]), ALU.mult)
            dve.wait_ge(S("e_ready"), 1)
            tt(qd, qd, bc(gq2, 1, [P, 2, 512]), ALU.mult)
            tt(kd, em, bc(gk2, 1, [P, 2, 512]), ALU.mult).then_inc(S("qk_ready"), 1)
            dve.wait_ge(S("S0_ps"), 1)
            V.tensor_copy(Sg[:, 0, 0, :, :], PB[4][:, 0:256].rearrange("p (a b) -> p a b", a=2))
            V.tensor_copy(Sg[:, 1, 3, :, :], PB[4][:, 256:512].rearrange("p (a b) -> p a b", a=2)) \
                .then_inc(S("S0_out"), 1)
            dve.wait_ge(S("S0_out"), 1)
            V.memset(pg, 0.0)
            dve.wait_ge(S("U_ps"), 4)
            for step in range(1, 4):
                for d, (c_old, c_new) in enumerate(((step - 1, step), (4 - step, 3 - step))):
                    bank, col = U_AT[(c_old, d)]
                    for hp in range(2):
                        e = hp * 256 + c_old * 64 + (63 if d == 0 else 0)
                        i_ = V.scalar_tensor_tensor(Sg[:, d, c_new, hp, :], Sg[:, d, c_old, hp, :],
                                                    EA[:, d, e:e + 1], PB[bank][:, col + hp * P:col + (hp + 1) * P],
                                                    ALU.mult, ALU.add)
                        if d == 1 and hp == 1 and step == 3:
                            i_.then_inc(S("states_done"), 1)
                        elif d == 1 and hp == 1:
                            link(i_)
            dve.wait_ge(S("gsc_ps"), 2)
            for hp2 in range(2):
                i_ = tt(prt[:, 4 * hp2:4 * hp2 + 4, :], PB[4 + hp2][:, :].rearrange("p (a b) -> p a b", a=4),
                        bc(c1("cmask", P), 1, [P, 4, P]), ALU.mult)
            link(i_)
            for hp2 in range(2):
                for cp in range(2):
                    ps_ = slice(64 * cp, 64 * cp + 64)
                    i_ = tt(pg[ps_, hp2, :, 64 * cp:64 * cp + 64], prt[ps_, 4 * hp2:4 * hp2 + 4, 0:64],
                            prt[ps_, 4 * hp2:4 * hp2 + 4, 64:128], ALU.add)
            i_.then_inc(S("pg_ready"), 1)
            dve.wait_ge(S("gi_ps"), 1)
            dve.wait_ge(S("j_out"), 2)
            for hp in range(2):
                i_ = tt(og[:, 2 * hp:2 * hp + 2, :], og[:, 2 * hp:2 * hp + 2, :],
                        PB[6 + hp][:, :].rearrange("p (a b) -> p a b", a=2), ALU.add)
            i_.then_inc(S("og_ready"), 1)
            dve.wait_ge(S("wk_ready"), 1)
            for x in range(2):
                for d in range(2):
                    i_ = tt(kwr[:, x, d, :].rearrange("p (a b) -> p a b", a=4), rktm[:, x, :].rearrange("p (a b) -> p a b", a=4),
                            bc(wk[:, x, d * 4:d * 4 + 4], 2, [P, 4, P]), ALU.mult)
            i_.then_inc(S("kwr_ready"), 1)
            for n, src in enumerate((rq, rk)):
                for half in range(2):
                    dve.wait_ge(S("rope_ps"), 2 * n + half + 1)
                    tmp = tmp1[:, 2 * n + half, :].rearrange("p (a b) -> p a b", a=2)
                    tt(tmp, PB[6 + half][:, :].rearrange("p (a b) -> p a b", a=2), bc(c1("sin1", T), 1, [P, 2, T]), ALU.mult) \
                        .then_inc(S("rope_out"), 1)
                    sh = src[:, 2 * half:2 * half + 2, :]
                    link(tt(sh, sh, bc(c1("cos1", T), 1, [P, 2, T]), ALU.mult))
                    i_ = tt(sh, sh, tmp, ALU.add)
            i_.then_inc(S("rk_ready"), 1)
            dve.wait_ge(S("rk_ready"), 1)
            for hh in range(RH):
                b = hh % 2
                dve.wait_ge(S("dec_in"), hh + 1)
                link(tt(dec[:, b, :], dec[:, b, :], c1("msk", 1024), ALU.mult))
                link(tt(dec[:, b, 0:512], dec[:, b, 0:512], dec[:, b, 512:1024], ALU.add))
                if hh >= 2:
                    dve.wait_ge(S("or_ps"), hh - 1)
                dve.wait_ge(S("rsc_ps"), hh + 1)
                tt(pr[:, b, :], PB[4 + b], dec[:, b, 0:512], ALU.mult).then_inc(S("pr_ready"), 1)
                dve.wait_ge(S("rqe"), hh + 1)
                q2 = rqd[:, b, :].rearrange("p (a b) -> p a b", a=2)
                tt(q2, q2, bc(rq[:, hh, :], 1, [P, 2, T]), ALU.mult).then_inc(S("rqd_ready"), 1)
            dve.wait_ge(S("or_out"), 4)
            tt(gn_t, og, og, ALU.mult).then_inc(S("gsq_ready"), 1)
            dve.wait_ge(S("hnorm_ps"), 2)
            for half in range(2):
                o2 = orr[:, 2 * half:2 * half + 2, :]
                i_ = V.scalar_tensor_tensor(o2, PB[6 + half][:, :].rearrange("p (a b) -> p a b", a=2), -1.0 / P, o2,
                                            ALU.mult, ALU.add)
            link(i_)
            tt(gn_t, orr, orr, ALU.mult).then_inc(S("rsq_ready"), 1)
            for half in range(2):
                V.tensor_scalar(tmp1[:, half, :], PB[4 + half], 1.0 / P, EPS, ALU.mult, ALU.add)
            dve.wait_ge(S("hnorm_ps"), 3)
            for half in range(2):
                i_ = V.tensor_scalar(tmp1[:, 2 + half, :], PB[6 + half], 1.0 / P, EPS, ALU.mult, ALU.add)
            i_.then_inc(S("hn_ms"), 1)
            dve.wait_ge(S("hn_rms"), 1)
            link(V.reciprocal(tmp1, tmp1))
            t4 = view(B1["la"][0], 8, T)
            tt(og, og, t4[:, 0:4, :], ALU.mult)
            link(tt(orr, orr, t4[:, 4:8, :], ALU.mult))
            for hh in range(GH):
                V.scalar_tensor_tensor(mixb1[:, hh, :], og[:, hh, :], v0("gnorm", 4)[:, hh:hh + 1], sgg[:, hh, :],
                                       ALU.mult, ALU.mult)
            for hh in range(RH):
                i_ = V.scalar_tensor_tensor(mixb1[:, 4 + hh, :], orr[:, hh, :], v0("rnorm", 4)[:, hh:hh + 1], srg[:, hh, :],
                                            ALU.mult, ALU.mult)
            i_.then_inc(S("mix1_ready"), 1)
            modulation([1, 2], 12, 3, (2, 3, 4, 5))
            n = PROJ1_END[-1]
            for mt in range(KT):
                dve.wait_ge(S("tile_in"), n + 1)
                V.scalar_tensor_tensor(resid[:, mt, 0:T], PB[n % 4][:, 0:T], modv[:, 0, 16 + mt, 0:1], resid[:, mt, 0:T],
                                       ALU.mult, ALU.add).then_inc(S("tile_out_D"), 1)
                n += 1

            def norm(k):
                norm_squares(k, NORMS[k][2])
                return norm_rest(k, NORMS[k][2])

            dve.wait_ge(S("tile_out_D"), 13 + KT)
            norm(1)
            lgt = PB[5][:, 0:2 * E].rearrange("p (a b) -> p a b", a=2)
            dve.wait_ge(S("router_ps"), 1)
            link(V.reduce_max(sm[:, 0:2], lgt, AX.X))
            tt(aff, lgt, bc(sm[:, 0:2], 2, [P, 2, E]), ALU.subtract).then_inc(S("routed"), 1)
            dve.wait_ge(S("affe"), 1)
            link(V.reduce_sum(sm[:, 2:4], aff, AX.X))
            link(V.reciprocal(sm[:, 4:6], sm[:, 2:4]))
            tt(aff, aff, bc(sm[:, 4:6], 2, [P, 2, E]), ALU.mult).then_inc(S("routed"), 1)
            dve.wait_ge(S("router_ps"), 2)
            V.tensor_copy(pa[:, T:2 * T], PB[6][0:E, 0:T])
            link(V.tensor_copy(affw[:, 0, :], PB[6][0:E, 0:T]))
            for r in range(CAP // 8):
                link(V.max(m8, affw[:, r % 2, :]))
                link(V.match_replace(affw[:, 1 - r % 2, :], m8, affw[:, r % 2, :], -1.0))
            V.tensor_scalar(mkT, affw[:, 0, :], 0.0, None, ALU.is_lt).then_inc(S("routed"), 1)
            dve.wait_ge(S("router_ps"), 3)
            V.tensor_copy(mk, PB[7][:, 0:2 * E].rearrange("p (a b) -> p a b", a=2)).then_inc(S("routed"), 1)
            dve.wait_ge(S("router_ps"), 4)
            dve.wait_ge(S("routed"), 4)
            tt(pos, PB[4][:, 0:2 * E].rearrange("p (a b) -> p a b", a=2), mk, ALU.mult).then_inc(S("routed"), 1)
            dve.wait_ge(S("routed"), 5)
            for x in range(2):
                i_ = tt(sel[:, x, :].rearrange("p (a b) -> p a b", a=E), bc(pos[:, x, :], 2, [P, E, CAP]),
                        bc(c0("iota32", CAP), 1, [P, E, CAP]), ALU.is_equal)
            i_.then_inc(S("routed"), 1)
            dve.wait_ge(S("router_ps"), 5)
            V.tensor_copy(pa[:, 0:T], PB[6][0:E, 0:T]).then_inc(S("routed"), 1)
            dve.wait_ge(S("routed"), 7)
            with dve.Fori(0, E) as i:
                dve.wait_ge(S("bc_ps"), i + 1)
                V.tensor_scalar(bcm, pa, ident[0:E, bass.ds(i, 1)], None, ALU.mult).then_inc(S("bcm_ready"), 1)
                dve.wait_ge(S("gs_out"), i + 1 + 1)
                dve.wait_ge(S("slot_free1"), 12 + 2 * i + 2 + 1)
                tt(gu, gs, PB[5][:, 0:FQ], ALU.mult).then_inc(S("gu_ready"), 1)
                dve.wait_ge(S("gu_ready"), i + 1 + 1)
                dve.wait_ge(S("slot_free5"), 2 * i + 1)
                V.transpose(hx, gu.rearrange("p (q t) -> p t q", t=FT)).then_inc(S("hx_ready"), 1)
                dve.wait_ge(S("bcs_out"), i + 1 + 1)
                dve.wait_ge(S("z_ps"), i + 1)
                V.scalar_tensor_tensor(selg, bcs[:, 0:T], c0("slot1", 1), bcs[:, T:2 * T], ALU.is_equal, ALU.mult) \
                    .then_inc(S("selg_ready"), 1)
                dve.wait_ge(S("z_ps"), i + 1 + 1)
                for t in range(KT):
                    i_ = V.scalar_tensor_tensor(resid[:, t, 0:T], PB[t // 2][:, (t % 2) * T:(t % 2 + 1) * T],
                                                modv[:, 0, 40 + t, 0:1], resid[:, t, 0:T], ALU.mult, ALU.add)
                i_.then_inc(S("acc_done"), 1)
                dve.wait_ge(S("acc_done"), i + 1 + 1)
            norm(2).then_inc(S("x_in2"), 1)
            dve.wait_ge(S("x_in2"), 1)
            dve.wait_ge(S("second_in"), 64)
            for layer in range(2):
                nf = N2 if layer == 0 else T
                ns = nf // T
                k0 = 3 + 2 * layer
                V.memset(glu, 0.0)
                link(V.memset(cx, 0.0))
                norm(k0)
                lam = v2(layer, "lam", 2, 2, DQ)
                link(tt(s4[:, 24:56].rearrange("p (a b) -> p a b", a=1), lam[:, 0:1, 0, :], lam[:, 0:1, 1, :], ALU.mult))
                link(V.reduce_sum(s4[:, 0:1], s4[:, 24:56], AX.X))
                link(tt(s4[:, 24:56].rearrange("p (a b) -> p a b", a=1), lam[:, 1:2, 0, :], lam[:, 1:2, 1, :], ALU.mult))
                V.reduce_sum(s4[:, 1:2], s4[:, 24:56], AX.X).then_inc(S("lam_in"), 1)
                n = PROJ2_AT[layer]
                a_out = A_TILES_BEFORE[layer]

                def seg(t, m):
                    return t[:, m, 0:nf].rearrange("p (s t) -> p s t", s=ns)

                def taps(src, acc, w, width, bias):
                    for x in range(width):
                        for m in range(2):
                            win = src[:, m, 0:ns, x:x + T]
                            sc = w[:, m, x:x + 1]
                            if x:
                                dve.wait_ge(S("taps"), TAPS_AT[0] - 1)
                                i_ = V.scalar_tensor_tensor(seg(acc, m), win, sc, seg(acc, m), ALU.mult, ALU.add)
                            else:
                                b_ = bias[:, m:m + 1] if bias is not None else 0.0
                                i_ = V.tensor_scalar(seg(acc, m), win, sc, b_, ALU.mult, ALU.add) if bias is not None \
                                    else V.tensor_scalar(seg(acc, m), win, sc, None, ALU.mult)
                            i_.then_inc(S("taps"), 1)
                            TAPS_AT[0] += 1
                    dve.wait_ge(S("taps"), TAPS_AT[0])

                for g, group in enumerate(proj2_tiles(layer)[:2]):
                    for M, N, _, _, _, owner, dst, func in group:
                        if owner == "D":
                            dve.wait_ge(S("tile_in"), n + 1)
                            dve.wait_ge(S("tile_out_A"), a_out)
                            tt(dst, PB[n % 4][0:M, 0:N].rearrange("p (s t) -> p s t", s=ns),
                               func[1].rearrange("p (s t) -> p s t", s=ns), ALU.mult).then_inc(S("tile_out_D"), 1)
                            d_out[0] += 1
                        else:
                            a_out += 1
                        n += 1
                    dve.wait_ge(S("tile_out_D"), d_out[0])
                    if g == 0:
                        taps(cx, accd, v2(layer, "cdw", 2, 3), 3, None)
                    else:
                        taps(glu, acca, v2(layer, "caw", 2, 31), 31, v2(layer, "cab", 2))
                V.tensor_copy(s4[:, 56:57], s4[:, 0:1]).then_inc(S("ln_in"), 1)
                dve.wait_ge(S("tile_out_A"), A_TILES_BEFORE[layer] + n_a(proj2_tiles(layer)))
                dve.wait_ge(S("ln_ps"), 2 * layer + 1)
                for m_ in range(2):
                    i_ = V.scalar_tensor_tensor(acca[:, m_, 0:nf], PB[6][:, 0:nf], -1.0 / GW, acca[:, m_, 0:nf],
                                                ALU.mult, ALU.add)
                link(i_)
                tt(tg[:, :, 0:nf], acca[:, :, 0:nf], acca[:, :, 0:nf], ALU.mult).then_inc(S("ln_in"), 1)
                dve.wait_ge(S("ln_ps"), 2 * layer + 2)
                V.tensor_scalar(rs[:, 0:nf], PB[6][:, 0:nf], 1.0 / GW, EPS, ALU.mult, ALU.add).then_inc(S("ln_var"), 1)
                nt = nf // P
                svv = sv[:, 0:nt, :]
                tmp = tg[:, :, :].rearrange("p a (b c) -> p (a b) c", c=GW)[:, 0:nt, :]
                link(V.reduce_sum(s4[:, 8:8 + nt], svv, AX.X))
                link(V.tensor_scalar(s4[:, 8:8 + nt], s4[:, 8:8 + nt], 1.0 / GW, None, ALU.mult))
                link(tt(svv, svv, bc(s4[:, 8:8 + nt], 2, [P, nt, GW]), ALU.subtract))
                link(tt(tmp, svv, svv, ALU.mult))
                link(V.reduce_sum(s4[:, 12:12 + nt], tmp, AX.X))
                V.tensor_scalar(s4[:, 12:12 + nt], s4[:, 12:12 + nt], 1.0 / GW, EPS, ALU.mult, ALU.add) \
                    .then_inc(S("sv_var"), 1)
                dve.wait_ge(S("ln_std"), layer + 1)
                link(V.reciprocal(rs[:, 0:nf], rs[:, 0:nf]))
                tt(acca[:, :, 0:nf], acca[:, :, 0:nf], bc(rs[:, 0:nf], 1, [P, 2, nf]), ALU.mult).then_inc(S("ln_out"), 1)
                dve.wait_ge(S("sv_std"), layer + 1)
                link(V.reciprocal(s4[:, 12:12 + nt], s4[:, 12:12 + nt]))
                link(tt(svv, svv, bc(s4[:, 12:12 + nt], 2, [P, nt, GW]), ALU.mult))
                link(tt(svv, svv, bc(v2(layer, "sglng", GW), 1, [P, nt, GW]), ALU.mult))
                tt(svv, svv, bc(v2(layer, "sglnb", GW), 1, [P, nt, GW]), ALU.add).then_inc(S("svn_ready"), 1)
                for x, src in enumerate((qf, kf)):
                    dve.wait_ge(S("rope2_ps"), 2 * layer + x + 1)
                    t2 = tc[:, :, 0:T]
                    link(tt(t2, PB[4 + x][:, :].rearrange("p (a b) -> p a b", a=2), bc(c2("sin2", T), 1, [P, 2, T]), ALU.mult))
                    link(tt(src[:, :, 0:T], src[:, :, 0:T], bc(c2("cos2", T), 1, [P, 2, T]), ALU.mult))
                    i_ = tt(src[:, :, 0:T], src[:, :, 0:T], t2, ALU.add)
                    if x == 0:
                        link(i_)
                i_.then_inc(S("qk2_ready"), 1)
                dve.wait_ge(S("lam_exp"), layer + 1)
                link(tt(s4[:, 4:5], s4[:, 3:4], s4[:, 2:3], ALU.subtract))
                link(V.tensor_scalar(s4[:, 4:5], s4[:, 4:5], LAM_INIT[layer], None, ALU.subtract))
                tt(mix[:, 6:8, 0:nf], accd[:, :, 0:nf], bgf[:, :, 0:nf], ALU.mult)
                dve.wait_ge(S("sg_ps"), layer + 1)
                for gt in range(2):
                    m4 = mix[:, 4 + gt, 0:nf].rearrange("p (a b) -> p a b", b=P)
                    i_ = tt(m4, PB[2 + gt][:, 0:nf].rearrange("p (a b) -> p a b", b=P),
                            bc(v2(layer, "sgb", 2, P)[:, gt, :], 1, [P, nt, P]), ALU.add)
                link(i_)
                tt(mix[:, 4:6, 0:nf], mix[:, 4:6, 0:nf], uf[:, :, 0:nf], ALU.mult)
                dve.wait_ge(S("ya_ready"), layer + 1)
                V.tensor_copy(s4[:, 57:58], s4[:, 4:5]).then_inc(S("mixers_done"), 1)
                units = attn_units(layer)
                u0 = UNIT_AT[layer]

                def maxima(u):
                    nk = 512 if units[u][0] == 0 else 256
                    dve.wait_ge(S("asc_ps"), u0 + u + 1)
                    for comp in range(2):
                        c_ = 16 + 2 * (u % 2) + comp
                        i_ = V.reduce_max(s4[:, c_:c_ + 1], PB[2 * (u % 2) + comp][:, 0:nk], AX.X, negate=True)
                    link(i_)
                    c_ = 16 + 2 * (u % 2)
                    V.tensor_scalar(s4[:, c_:c_ + 2], s4[:, c_:c_ + 2], float(DQ) ** -0.5, None, ALU.mult) \
                        .then_inc(S("amax"), 1)

                maxima(0)
                for u, (s_, qt, hh) in enumerate(units):
                    if u + 1 < len(units):
                        maxima(u + 1)
                    nk = 512 if s_ == 0 else 256
                    c_ = 20 + 2 * (u % 2)
                    dve.wait_ge(S("exp_done"), u0 + u + 1)
                    link(V.reciprocal(s4[:, c_:c_ + 2], s4[:, c_:c_ + 2]))
                    link(tt(s4[:, c_ + 1:c_ + 2], s4[:, c_ + 1:c_ + 2], s4[:, 4:5], ALU.mult))
                    e1, e2 = Eb[:, u % 2, 0, 0:nk], Eb[:, u % 2, 1, 0:nk]
                    link(V.tensor_scalar(e1, e1, s4[:, c_:c_ + 1], None, ALU.mult))
                    V.scalar_tensor_tensor(e1, e2, s4[:, c_ + 1:c_ + 2], e1, ALU.mult, ALU.add).then_inc(S("w_ready"), 1)
                dve.wait_ge(S("pv_ps"), u0 + len(units))
                for s_ in range(ns):
                    i_ = V.tensor_copy(mix[:, 2:4, s_ * T:(s_ + 1) * T], PB[6 + s_][:, :].rearrange("p (a b) -> p a b", a=2))
                link(i_)
                tt(tg[:, :, 0:nf], mix[:, 2:4, 0:nf], mix[:, 2:4, 0:nf], ALU.mult).then_inc(S("osq_ready"), 1)
                dve.wait_ge(S("oss_ps"), layer + 1)
                for m_ in range(2):
                    i_ = V.tensor_scalar(tc[:, m_, 0:nf], PB[m_][:, 0:nf], 1.0 / 64, EPS, ALU.mult, ALU.add)
                i_.then_inc(S("o_ms"), 1)
                dve.wait_ge(S("o_rms"), layer + 1)
                link(V.reciprocal(tc[:, :, 0:nf], tc[:, :, 0:nf]))
                link(tt(mix[:, 2:4, 0:nf], mix[:, 2:4, 0:nf], tc[:, :, 0:nf], ALU.mult))
                V.tensor_scalar(mix[:, 2:4, 0:nf], mix[:, 2:4, 0:nf], v2(layer, "subg", 1), 1.0 - LAM_INIT[layer],
                                ALU.mult, ALU.mult).then_inc(S("mix2_ready"), 1)
                n = OUT2_AT[layer]

                def add_residual(dt, bank, row):
                    for s_ in range(ns):
                        c_ = slice(s_ * T, (s_ + 1) * T)
                        i_ = V.scalar_tensor_tensor(resid[:, dt, c_], bank[:, c_], modv[:, 1 + layer, row + dt, s_:s_ + 1],
                                                    resid[:, dt, c_], ALU.mult, ALU.add)
                    return i_

                for dt in range(KT):
                    dve.wait_ge(S("tile_in"), n + dt + 1)
                    add_residual(dt, PB[(n + dt) % 4], 16).then_inc(S("tile_out_D"), 1)
                    d_out[0] += 1
                dve.wait_ge(S("tile_out_D"), d_out[0])
                norm(k0 + 1)
                for k in range(KT):
                    dve.wait_ge(S("h_hi_ready"), KT * layer + k + 1)
                    tt(h_lo[k][:, 0:nf], h[:, k, 0:nf], h_hi[k][:, 0:nf].bitcast(F32), ALU.subtract) \
                        .then_inc(S("h_split"), 1)

                def take_unit(i, n):
                    c, q = n // 4 % 2, n % 4
                    if n < 8:
                        dve.wait_ge(S("h1_relu"), 32 * layer + 8 * i + n + 1 + 4)
                        tt(h1[:, c, q, 0:nf], h1[:, c, q, 0:nf], h1[:, c, q, 0:nf], ALU.mult) \
                            .then_inc(S("h1_sq"), 1)
                        return
                    for dt in (2 * q, 2 * q + 1):
                        dve.wait_ge(S(f"y_ps{c}"), 32 * layer + 8 * i + dt + 1 + 9)
                        dve.wait_ge(S("y_out"), 64 * layer + 16 * i + 8 * c + dt + 1)
                        add_residual(dt, PB[4 + dt % 4], 40).then_inc(S("y_out"), 1)

                def h1_low(i, n):
                    c, q = n // 4, n % 4
                    dve.wait_ge(S("h1_hi_ready"), 32 * layer + 8 * i + n + 1)
                    tt(h1_lo[c][:, q, 0:nf], h1[:, c, q, 0:nf], h1_hi[c][:, q, 0:nf].bitcast(F32), ALU.subtract) \
                        .then_inc(S("h1_ready"), 1)

                def mlp_round(i, first):
                    for n in range(16):
                        if n >= 4 or not first:
                            take_unit(i if n >= 4 else i - 1, (n - 4) % 16)
                        dve.wait_ge(S("w_hi_ready"), 64 * layer + 16 * i + n + 1)
                        tt(w_split(w_lo, n), w_unit(n), w_split(w_hi, n).bitcast(F32), ALU.subtract) \
                            .then_inc(S("w_lo_ready"), 1)
                        if 4 <= n < 12:
                            h1_low(i, n - 4)

                mlp_round(0, True)
                with dve.Fori(1, 4) as i:
                    mlp_round(i, False)
                for n in range(12, 16):
                    take_unit(3, n)
                dve.wait_ge(S("y_out"), 64 * (layer + 1) + 4)
            norm(7).then_inc(S("final"), 1)
    return


def pack_inputs(inputs):
    I = {k: np.asarray(v) for k, v in inputs.items()}

    def fm(a):
        return np.ascontiguousarray(a.T.reshape(-1, P, a.shape[0]).transpose(1, 0, 2))

    def vec(a):
        return a.reshape(-1, P).T

    def rows(a):
        return np.broadcast_to(a.reshape(1, -1), (P, a.size))

    c0, c1, c2 = shape_constants()
    arr = {"xT": fm(I["x"][0]), "ctxT": fm(I["ctx"][0]), "ctx2T": fm(I["ctx_2"][0]), "c0": c0, "c1": c1, "c2": c2}
    cv = [I["c"][0], I["c_ctx"], I["c_2"][0], I["c_ctx_2"]]
    norms = [I["norm1_w"][0], I["norm2_w"][0], I["final_norm_w"], I["norm1_g_2"][0], I["norm1_g_2"][1],
             I["norm2_g_2"][0], I["norm2_g_2"][1], I["final_g_2"]]
    bada = [I["b_ada"][0], I["ada_b_2"][0], I["ada_b_2"][1]]
    arr["v0"] = np.ascontiguousarray(np.concatenate(
        [vec(a) for a in cv + norms + bada] + [vec(I["gla_norm_w"][0]), vec(I["ret_norm_w"][0]),
                                               rows(I["ret_decay_logit"][0])], 1))
    per = []
    for l in range(2):
        sgb = I["sg_b_2"][l]
        sgb = sgb.reshape(2, 2, 1, P)
        sgb = np.broadcast_to(sgb, (2, 2, 64, P)).transpose(1, 2, 0, 3).reshape(P, 2 * P)
        lam = np.concatenate([I["lam_q1_2"][l], I["lam_k1_2"][l], I["lam_q2_2"][l], I["lam_k2_2"][l]])
        per += [I["conv_a_w_2"][l].T.reshape(2, P, 31).transpose(1, 0, 2).reshape(P, 62),
                vec(I["conv_a_b_2"][l]), vec(I["ln_a_g_2"][l]), vec(I["ln_a_b_2"][l]),
                I["conv_d_w_2"][l].T.reshape(2, P, 3).transpose(1, 0, 2).reshape(P, 6),
                np.concatenate([I["subln_g_2"][l], I["subln_g_2"][l]]).reshape(P, 1),
                rows(I["sg_ln_g_2"][l]), rows(I["sg_ln_b_2"][l]), sgb, rows(lam)]
    arr["v2"] = np.ascontiguousarray(np.concatenate(per, 1))
    arr["sgw"] = np.ascontiguousarray(I["sg_w_2"].transpose(3, 0, 1, 2).reshape(P, -1))
    arr["wr"] = np.ascontiguousarray(I["w_router"][0].reshape(KT, P, E).transpose(1, 0, 2))
    gw = np.zeros((33, 512), np.float32)
    gw[0:16, 0:256] = I["gla_gate_w"][0, 0]
    gw[16:32, 256:512] = I["gla_gate_w"][0, 1]
    gw[32] = I["gla_gate_b"][0].reshape(-1)
    arr["gw"] = gw
    for name in ("w_ada", "w_in", "w_out", "w_exp_gate", "w_exp_up", "w_exp_down", "ada_w_2", "w_in_2", "w_out_2",
                 "mlp_w1_2", "mlp_w2_2"):
        arr[name] = np.ascontiguousarray(I[name])
    return arr


def kernel(**inputs):
    import concourse.bacc as bacc
    from concourse.bass_utils import run_bass_kernel_spmd

    nc = bacc.Bacc("TRN2", target_bir_lowering=False, num_devices=1)
    arrays = pack_inputs(inputs)
    aps = {k: nc.dram_tensor(f"in_{k}", a.shape, mybir.dt.from_np(a.dtype), kind="ExternalInput").ap()
           for k, a in arrays.items()}
    out = nc.dram_tensor("out", (P, KT, T), F32, kind="ExternalOutput").ap()
    build(nc, aps, out)
    r = run_bass_kernel_spmd(nc, [{f"in_{k}": a for k, a in arrays.items()}], core_ids=[0])
    got = r.results[0]["out"]
    return np.ascontiguousarray(got.transpose(2, 1, 0).reshape(1, T, D))
```

```python
from contextlib import ExitStack

import numpy as np

import concourse.bass as bass
from concourse import mybir

F32 = mybir.dt.float32
F32R = mybir.dt.float32r
ACT = mybir.ActivationFunctionType
ALU = mybir.AluOpType
AX = mybir.AxisListType

P = 128
T = 256
N2 = 2 * T
D = 1024
KT = D // P
EPS = 1e-6
GATE_TAU = 16.0
CH = 64
NC = T // CH
GH = RH = 4
W_IN1 = 3616
E, CAP, FF = 16, 32, 1408
FT = FF // P
FQ = FF // 4
GW = 256
D_FF = 4096
DQ = 32
LAM_INIT = [0.8 - 0.6 * float(np.exp(-0.3 * l)) for l in range(2)]
EXP_CLAMP = 43.0

SLOT = 4096
NSLOT = 6


def offsets(parts, base=0):
    out, at = {}, base
    for name, size in parts:
        out[name] = (at, size)
        at += size
    return out, at


C0_PARTS = [("ident", P), ("ones", P), ("sel2", 2), ("slot1", 1), ("iota32", CAP), ("incl", P)]
C1_PARTS = [("prefI", P), ("sufI", P), ("prefIm", P), ("sufIm", P), ("sufS", P), ("prefS", P),
            ("sufC", P), ("prefC", P), ("cos1", T), ("sin1", T), ("rot1", P), ("rel", 4 * T),
            ("msk", 4 * T), ("qpos", 2 * T), ("kpos", 16), ("cmask", 2 * CH)]
C2_PARTS = [("cos2", T), ("sin2", T), ("rot2", P), ("ones64", P)]
V0_PARTS = [("cv", 4 * KT), ("norms", 8 * KT), ("bada", 3 * 48), ("gnorm", 4), ("rnorm", 4), ("rdl", 8)]
V2_PARTS = [("caw", 62), ("cab", 2), ("lag", 2), ("lab", 2), ("cdw", 6), ("subg", 1), ("sglng", GW),
            ("sglnb", GW), ("sgb", 2 * P), ("lam", 4 * DQ)]
C0_AT, C0_N = offsets(C0_PARTS)
C1_AT, C1_N = offsets(C1_PARTS)
C2_AT, C2_N = offsets(C2_PARTS)
V0_AT, V0_N = offsets(V0_PARTS)
V2_AT, V2_N = offsets(V2_PARTS)


def shape_constants():
    f = np.float32
    p = np.arange(P)
    j, i = p[:, None], p[None, :]
    same = (j // CH) == (i // CH)
    c0 = {"ident": np.eye(P), "ones": np.ones((P, P)),
          "sel2": (p[:, None] % 32 == np.arange(2)[None, :]),
          "slot1": (p[:, None] % CAP) + 1, "iota32": np.broadcast_to(np.arange(CAP) + 1, (P, CAP)),
          "incl": j <= i}
    tok = np.arange(T)
    pos = np.stack([tok // 64, tok % 64]).astype(f)
    inv = (10000.0 ** (-np.arange(32, dtype=f) / 32)).astype(f)
    ang = np.concatenate([inv[:, None] * pos[0], inv[:, None] * pos[1]], 0).astype(f)
    ang = np.concatenate([ang, ang], 0)
    rot1 = np.zeros((P, P))
    for m in range(64):
        rot1[m + 64, m] = -1.0
        rot1[m, m + 64] = 1.0
    jj = (np.arange(2)[None, :, None] * P + p[:, None, None])
    ii = tok[None, None, :]
    rel = np.stack([np.maximum(ii - jj, 0), np.maximum(jj - ii, 0)], 1)
    msk = np.stack([ii >= jj, jj >= ii], 1)
    qpos = np.broadcast_to(np.stack([tok + 1, T - tok]), (P, 2, T))
    t2 = np.arange(2)[None, :] * P + p[:, None]
    kpos = np.broadcast_to(np.stack([T - 1 - t2, t2], 2)[..., None], (P, 2, 2, 4))
    pc, ic = (p % CH)[:, None], np.arange(CH)[None, :]
    c1 = {"prefI": (j <= i) & same, "sufI": (j >= i) & same,
          "prefIm": ((j <= i) & same) * 1.0 - ((j % CH <= CH // 2 - 1) & same) * 1.0,
          "sufIm": ((j >= i) & same) * 1.0 - ((j % CH >= CH // 2) & same) * 1.0,
          "sufS": (j > i) & same, "prefS": (j < i) & same, "sufC": j > i, "prefC": j < i,
          "cos1": np.cos(ang), "sin1": np.sin(ang), "rot1": rot1, "rel": rel, "msk": msk,
          "qpos": qpos, "kpos": kpos, "cmask": np.stack([pc <= ic, pc >= ic], 1)}
    inv2 = (10000.0 ** (-np.arange(0, 16, 2, dtype=f) / 16)).astype(f)
    d = p % 32
    ang2 = (inv2[d % 8][:, None] * np.where((d < 16)[:, None], pos[0][None], pos[1][None])).astype(f)
    rot2 = np.zeros((P, P))
    for m in range(P):
        if m % 16 < 8:
            rot2[m + 8, m] = -1.0
        else:
            rot2[m - 8, m] = 1.0
    c2 = {"cos2": np.cos(ang2), "sin2": np.sin(ang2), "rot2": rot2, "ones64": (j // 64) == (i // 64)}

    def pack(parts, c):
        return np.ascontiguousarray(np.concatenate(
            [np.asarray(c[n]).astype(f).reshape(P, size) for n, size in parts], 1))

    return pack(C0_PARTS, c0), pack(C1_PARTS, c1), pack(C2_PARTS, c2)


def build(nc, ap, out):
    with ExitStack() as ctx:
        TOTAL = 53003
        big = ctx.enter_context(nc.sbuf_tensor("big", [P, TOTAL], F32))
        PB = [ctx.enter_context(nc.psum_tensor(f"bank{i}", [P, 512], F32))[:, :] for i in range(8)]
        BIG_AT = nc.sbuf_base - 4 * TOTAL
        sems = {}

        def S(name):
            if name not in sems:
                sems[name] = ctx.enter_context(nc.semaphore(name))
            return sems[name]

        names2, pers = offsets([("resid", KT * N2), ("h", KT * N2), ("c0", C0_N), ("cR", C1_N), ("v0", V0_N),
                                ("wr", KT * E), ("csil", 2 * KT * 32), ("modv", 3 * 96), ("asc", 6 * 16),
                                ("rs", N2), ("rm", 8)])
        PERS = TOTAL - pers
        ARENA1 = 3 * SLOT
        ARENA2 = NSLOT * SLOT

        def view(off, *dims, parts=slice(0, P)):
            n = 1
            for d in dims:
                n *= d
            a = big[parts, off:off + n]
            if len(dims) == 2:
                a = a.rearrange("p (a b) -> p a b", a=dims[0])
            if len(dims) == 3:
                a = a.rearrange("p (a b c) -> p a b c", a=dims[0], b=dims[1])
            if len(dims) == 4:
                a = a.rearrange("p (a b c d) -> p a b c d", a=dims[0], b=dims[1], c=dims[2])
            return a

        def pers_view(name, *dims):
            return view(PERS + names2[name][0], *dims)

        resid = pers_view("resid", KT, N2)
        h = pers_view("h", KT, N2)
        wr = pers_view("wr", KT, E)
        csil = pers_view("csil", 2, KT, 32)
        modv = pers_view("modv", 3, 48, 2)
        asc = pers_view("asc", 6, KT, 2)
        rs = pers_view("rs", N2)
        rm = pers_view("rm", 8)

        def c0(name, *dims):
            return view(PERS + names2["c0"][0] + C0_AT[name][0], *dims)

        def c1(name, *dims):
            return view(PERS + names2["cR"][0] + C1_AT[name][0], *dims)

        def c2(name, *dims):
            return view(PERS + names2["cR"][0] + C2_AT[name][0], *dims)

        def v0(name, *dims):
            return view(PERS + names2["v0"][0] + V0_AT[name][0], *dims)

        SW_AT = names2["cR"][0] + C2_N
        V2_BASE = SW_AT + 2 * 4 * P

        def v2(layer, name, *dims):
            return view(PERS + V2_BASE + layer * V2_N + V2_AT[name][0], *dims)

        assert C2_N + 2 * 4 * P + 2 * V2_N <= C1_N
        sgw = view(PERS + SW_AT, 2, 4, P)
        ident, ones, sel2 = c0("ident", P), c0("ones", P), c0("sel2", 2)

        def slot(s, *dims):
            return view(s * SLOT, *dims)

        B1, b1_end = offsets([
            ("gq", 512), ("gk", 512), ("gktm", 1024), ("gv", 2048), ("gz", 512), ("sgg", 1024),
            ("rq", 1024), ("rk", 1024), ("rktm", 1024), ("rv", 2048), ("srg", 1024), ("la", 2048),
            ("kw", 1024), ("kwr", 2048), ("Sg", 2048), ("Sr", 1024), ("ke", 1024), ("EA", 1024),
            ("wgz", 256), ("gw", 512), ("lg", 16), ("wk", 16)], ARENA1)
        assert b1_end <= PERS, (b1_end, PERS)

        def b1(name, *dims):
            return view(B1[name][0], *dims)

        gq, gk = b1("gq", 2, T), b1("gk", 2, T)
        gktm, gv = b1("gktm", 4, 256), b1("gv", 4, 512)
        gz = b1("gz", N2)
        part = view(PERS - 3 * 512, 3, 512)
        sgg, srg = b1("sgg", 4, T), b1("srg", 4, T)
        rq, rk = b1("rq", 4, T), b1("rk", 4, T)
        rktm, rv = b1("rktm", 2, 512), b1("rv", 4, 512)
        la = b1("la", 4, 512)
        kw = b1("kw", 2, 512)
        kwr = b1("kwr", 2, 2, 512)
        Sg = b1("Sg", 2, 4, 2, P)
        Sr = b1("Sr", 2, 4, P)
        ke = b1("ke", 2, 512)
        EA = b1("EA", 2, 512)
        wgz = b1("wgz", KT, 32)
        gw = b1("gw", 512)
        lg = b1("lg", 2, 8)
        wk = b1("wk", 2, 8)
        H_AT = PERS + names2["h"][0]
        qe, qd, kd, em = (view(H_AT + 1024 * n, 2, 512) for n in range(4))
        ep = qd
        prt = view(B1["la"][0], 8, P)
        pg = view(B1["kw"][0], 2, 4, P)
        lt = view(B1["kwr"][0], 4, 512)
        og = view(B1["EA"][0], 4, T)
        orr = view(B1["gktm"][0], 4, T)
        dec = view(H_AT, 2, 1024)
        pr = view(H_AT + 2048, 2, 512)
        rqd = view(H_AT + 3072, 2, 512)
        tmp1 = view(B1["la"][0], 4, 512)
        gn_t = view(H_AT, 4, T)
        mixb1 = view(B1["rv"][0], KT, T)

        B3, b3_end = offsets([
            ("htm", 2 * D), ("xeT", KT * E * CAP), ("sel", 2 * E * CAP), ("xe", KT * CAP), ("gs", FQ), ("gu", FQ),
            ("hx", FT * CAP), ("ye", 256), ("bcs", 512), ("selg", T), ("pa", 512), ("bcm", 512), ("aff", 32),
            ("sm", 8), ("affw", 2 * T), ("m8", 8), ("mk", 32), ("pos", 32), ("mkT", T)], ARENA2)
        assert b3_end <= PERS

        def b3(name, *dims, parts=slice(0, P)):
            return view(B3[name][0], *dims, parts=parts)

        e_rows = slice(0, E)
        htm, xeT, sel = b3("htm", 2, D), b3("xeT", KT, E * CAP), b3("sel", 2, E * CAP)
        xe, gs, gu, hx = b3("xe", KT, CAP), b3("gs", FQ), b3("gu", FQ), b3("hx", FT, CAP)
        ye, bcs, selg = b3("ye", 256), b3("bcs", 512), b3("selg", T)
        pa, bcm = b3("pa", 512, parts=e_rows), b3("bcm", 512, parts=e_rows)
        aff, mk, pos = b3("aff", 2, E), b3("mk", 2, E), b3("pos", 2, E)
        sm, m8 = b3("sm", 8), b3("m8", 8, parts=e_rows)
        affw, mkT = b3("affw", 2, T, parts=e_rows), b3("mkT", T, parts=e_rows)
        DOWN_T = [(0, 3), (3, 6), (6, 9), (9, 11)]

        GLU_W, CX_W = T + 30, T + 2
        B4, b4_end = offsets([
            ("qf", 1024), ("kf", 1024), ("vt", 1024), ("uf", 1024), ("sv", 1024), ("bg", 1024), ("tg", 1024),
            ("tc", 1024), ("glu", 4 * GLU_W), ("cx", 4 * CX_W), ("E", 2048), ("WT", 1024), ("s4", 64)], ARENA2)
        assert b4_end <= PERS, (b4_end, PERS)

        def b4(name, *dims):
            return view(B4[name][0], *dims)

        qf, kf, vt, uf, sv = b4("qf", 2, N2), b4("kf", 2, N2), b4("vt", 4, GW), b4("uf", 2, N2), b4("sv", 4, GW)
        bgf, tg, tc = b4("bg", 2, N2), b4("tg", 2, N2), b4("tc", 2, N2)
        glu = b4("glu", 2, 2, GLU_W)
        cx = b4("cx", 2, 2, CX_W)
        Eb = b4("E", 2, 2, 512)
        acca, accd = tg, tc
        ln_sq = view(B4["glu"][0], 2, N2)
        sv_sq = view(B4["cx"][0], 4, GW)
        rope_t = view(B4["E"][0], 2, T)
        WT = b4("WT", 2, 512)
        s4 = b4("s4", 64)
        mix = h

        def parts32r(name, off, *dims):
            n = int(np.prod(dims))
            a = nc.alloc_sbuf_tensor_at(name, [P, n], F32R, offset=BIG_AT + 4 * off)[:, :]
            return a.rearrange("p (a b) -> p a b", a=dims[0]) if len(dims) == 2 else a

        NWB, WU = 4, KT * P
        h_hi = [parts32r(f"h_hi{k}", 3 * SLOT + k * N2, N2) for k in range(KT)]
        h_lo = [parts32r(f"h_lo{k}", H_AT + k * N2, N2) for k in range(KT)]
        w_hi = [parts32r(f"w_hi{n}", 4 * SLOT + n * WU, WU) for n in range(NWB)]
        w_lo = [parts32r(f"w_lo{n}", 5 * SLOT + n * WU, WU) for n in range(NWB)]
        assert NWB * WU == SLOT and ARENA2 == 6 * SLOT
        MLP_SLOT = [0, 1, 2, 6]
        h1 = view(ARENA2 + SLOT, 2, 4, N2)
        h1_lo = [parts32r(f"h1_lo{c}", ARENA2 + SLOT + 4 * c * N2, 4, N2) for c in range(2)]
        h1_hi = [parts32r(f"h1_hi{c}", ARENA2 + SLOT + (8 + 4 * c) * N2, 4, N2) for c in range(2)]
        assert ARENA2 + SLOT + 16 * N2 <= PERS and H_AT % 8 == 0

        UNITS = 20 + KT + 4 * 16
        LEAD = 16
        PAIRS = (12, 13, 16, 17)

        def proj_unit(layer, j):
            if j < 20:
                g = j // 4
                if j in PAIRS:
                    return slot(g % 3, KT, 512)[:, 4 * (j % 2):4 * (j % 2) + 4, 0:256]
                col = proj2_tiles(layer)[g][j % 4][3]
                return slot(g % 3, KT, 512)[:, :, col:col + P]
            q = j - 20
            return slot((5 + q // 4) % 3, KT, 512)[:, :, q % 4 * P:(q % 4 + 1) * P]

        def w_unit(n):
            c, q = n // 4 % 2, n % 4
            if n < 8:
                return slot(MLP_SLOT[c], KT, 512)[:, :, q * P:(q + 1) * P]
            return slot(MLP_SLOT[2 + c], 4, D)[:, :, q * 256:(q + 1) * 256]

        def w_split(t, n, k=KT):
            return t[n % NWB].rearrange("p (k n) -> p k n", k=k)

        def proj_split(t, j):
            return w_split(t, j, 4 if j in PAIRS else KT)

        def unit_tiles(j):
            return j + 2 if j in PAIRS and j % 2 == 0 else j + 1

        def round_split(t, n):
            return w_split(t, n, KT if n < 8 else 4)

        def split_no(layer, j):
            return UNITS * layer + j

        def unit_done(layer, i, n):
            c, q = n // 4 % 2, n % 4
            if n < 8:
                return S(f"h1_ps{c}"), 16 * layer + 4 * i + q + 2
            return S(f"y_ps{c}"), 32 * layer + 8 * i + 2 * q + 2 + 9

        MIX_ORDER = [0, 1, 6, 7, 4, 5, 2, 3]

        mlp_loads = []

        def linker(eng, name):
            n = [0]

            def link(ins):
                n[0] += 1
                ins.then_inc(S(name), 1)
                eng.wait_ge(S(name), n[0])
            return link

        def bc(a, axis, shape):
            return a.unsqueeze(axis).to_broadcast(shape)

        w_in1 = ap["w_in"][0].rearrange("(k p) n -> p k n", p=P)

        def cols(w, a, n):
            return w.rearrange("(k p) n -> p k n", p=P)[:, :, a:a + n]

        PROJ1 = [0, 512, 2080, 2592, 1568, 1056, 3104]

        def tile_table(specs):
            return specs

        def proj1_tiles():
            out = []
            t = []
            for tt in range(4):
                t.append((P, 256, True, 256, tt, "D", gktm[:, tt, :], None))
            for m in range(2):
                t.append((P, T, False, 256 + m * P, None, "A", gk[:, m, :], None))
            for m in range(2):
                t.append((P, T, False, m * P, None, "A", gq[:, m, :], 0.125))
            out.append(t)
            out.append([(P, 512, True, 0, tt, "D", gv[:, tt, :], None) for tt in range(4)])
            s = float(P) ** -0.5
            out.append([(P, 512, True, 0, tt, "A", rktm[:, tt - 2, :], s) for tt in (2, 3)]
                       + [(P, T, False, m * P, None, "A", rk[:, m, :], s) for m in range(4)])
            out.append([(P, 512, True, 0, tt, "D", rv[:, tt, :], None) for tt in range(4)])
            out.append([(P, T, False, m * P, None, "A", rq[:, m, :], None) for m in range(4)])
            out.append([(P, T, False, m * P, None, "A", sgg[:, m, :], "silu") for m in range(4)])
            out.append([(P, T, False, m * P, None, "A", srg[:, m, :], "silu") for m in range(4)])
            return out

        PROJ1_END = [int(x) for x in np.cumsum([len(g) + (n == 1) for n, g in enumerate(proj1_tiles())])]

        class Tiles:

            def __init__(self):
                self.owner = []

            def add(self, owner):
                self.owner.append(owner)
                return len(self.owner) - 1

            def emptied(self, n):
                o = self.owner[n]
                return S("tile_out_" + o), sum(1 for x in self.owner[:n + 1] if x == o)

        NORMS = [(0, 0, N2), (1, 1, T), (None, 2, T), (2, 3, N2), (3, 5, N2), (4, 4, N2), (5, 6, T), (None, 7, T)]

        def affine_no(k):
            return sum(1 for a, _, _ in NORMS[:k] if a is not None)

        def wide_no(k):
            return sum(1 for _, _, n in NORMS[:k] if n == N2)

        PARTS2 = [(0, 1), (8, 9), (2, 3), (4, 5), (6, 7)]

        def proj2_tiles(layer):
            nf = N2 if layer == 0 else T

            def fm(col, m, owner, dst, func, n=nf):
                return (P, n, False, col + m * P, None, owner, dst, func)
            out = [[fm(256, m, "A", tg[:, m, 0:nf], "sigmoid") for m in range(2)]
                   + [fm(0, m, "D", glu[:, m, 0:nf // T, 15:15 + T], ("times", tg[:, m, 0:nf], m)) for m in range(2)],
                   [fm(0, m, "A", tc[:, m, 0:nf], None) for m in range(2)]
                   + [fm(256, m, "D", cx[:, m, 0:nf // T, 1:1 + T], ("times", tc[:, m, 0:nf], m)) for m in range(2)],
                   [fm(0, m, "A", qf[:, m, 0:nf], None) for m in range(2)]
                   + [fm(256, m, "A", kf[:, m, :], None, N2) for m in range(2)],
                   [(P, 512, True, 0, None, "A", vt[:, 2 * m:2 * m + 2, :], None) for m in range(2)]
                   + [fm(256, m, "A", uf[:, m, 0:nf], "gelu") for m in range(2)],
                   [(P, nf, True, 0, None, "A", sv[:, m * nf // T:(m + 1) * nf // T, :], "gelu") for m in range(2)]
                   + [fm(256, m, "A", bgf[:, m, 0:nf], None) for m in range(2)]]
            return out

        sq_out, ROLLED = view(ARENA2 + 2 * SLOT, KT, N2), {4: "out", 5: "h", 6: "out", 7: "h"}

        PROJ2_AT, OUT2_AT, at = [], [], PROJ1_END[-1] + KT
        for l_ in range(2):
            PROJ2_AT.append(at)
            at += sum(len(g) for g in proj2_tiles(l_))
            OUT2_AT.append(at)
            at += KT

        def attn_units(layer):
            return [(s_, qt, hh) for s_ in range(2 - layer) for qt in range(2) for hh in range(4)]

        UNIT_AT = [0, 16]

        def n_a(groups):
            return sum(t[5] == "A" for g in groups for t in g)

        def n_d(groups):
            return sum(t[5] == "D" for g in groups for t in g)
        D_TILES_AFTER_OUT = [n_d(proj1_tiles()) + 1 + KT + sum(n_d(proj2_tiles(x)) + KT for x in range(l_ + 1))
                             for l_ in range(2)]
        A_TILES_BEFORE = [n_a(proj1_tiles()), n_a(proj1_tiles()) + n_a(proj2_tiles(0))]
        def credit(eng, names):
            for name in names:
                eng.sem_inc(S(name), 1)

        block = ctx.enter_context(nc.Block())

        @block.sync
        def _(sp):
            used = [0] * NSLOT
            freed = [(S(f"slot_free{c}"), 5) if c < 3 else None for c in range(NSLOT)]

            def load(s, dst, src, freed_by):
                if freed[s] is not None:
                    sp.wait_ge(*freed[s])
                sp.dma_start(dst, src).then_inc(S(f"slot_full{s}"), 16)
                used[s] += 1
                freed[s] = freed_by

            sp.dma_start(big[:, PERS + names2["c0"][0]:PERS + names2["c0"][0] + C0_N], ap["c0"]).then_inc(S("first_in"), 16)
            sp.dma_start(big[:, PERS + names2["v0"][0]:PERS + names2["v0"][0] + V0_N], ap["v0"]).then_inc(S("first_in"), 16)
            w = ap["w_ada"][0].rearrange("(k p) (j n) -> j p k n", p=P, n=512)
            with sp.Fori(0, 4) as i:
                for c in range(3):
                    sp.wait_ge(S(f"slot_free{c}"), i + 1)
                    sp.dma_start(slot(c, KT, 512), w[i * 3 + c]).then_inc(S(f"slot_full{c}"), 16)
            for c in range(3):
                used[c] += 4
            for n, a in enumerate(PROJ1):
                load(n % 3, slot(n % 3, KT, 512), cols(ap["w_in"][0], a, 512), (S("tile_in"), PROJ1_END[n]))
            for r in range(8):
                w = ap["ada_w_2"][r // 4].rearrange("(k p) (j n) -> j p k n", p=P, n=512)
                for q in range(3):
                    c = (1 + q) % 3
                    load(c, slot(c, KT, 512), w[r % 4 * 3 + q], (S(f"slot_free{c}"), 4 + r + 1 + 1))
            for n in range(2):
                load((n + 1) % 3, slot((n + 1) % 3, KT, 512), cols(ap["w_out"][0], 512 * n, 512),
                     (S("tile_in"), PROJ1_END[-1] + 4 * (n + 1)))
            sp.wait_ge(S("tile_in"), PROJ1_END[-1] + KT)
            free0 = [12, 12, 12, 0, 0, 0]
            wg, wu = (ap[n][0].rearrange("e (k p) f -> e p k f", p=P) for n in ("w_exp_gate", "w_exp_up"))
            wd = ap["w_exp_down"][0].rearrange("e (p t) n -> e p t n", t=FT)
            with sp.Fori(0, E) as i:
                for q in range(12):
                    s = q % 6
                    sp.wait_ge(S(f"slot_free{s}"), free0[s] + 2 * i + q // 6 + 1)
                    if q < 4:
                        dst, src = slot(s, 2, FF), wg[i][:, 2 * q:2 * q + 2, :]
                    elif q < 8:
                        dst, src = slot(s, 2, FF), wu[i][:, 2 * q - 8:2 * q - 6, :]
                    else:
                        a, b = DOWN_T[q - 8]
                        dst, src = slot(s, b - a, D), wd[i][:, a:b, :]
                    sp.dma_start(dst, src).then_inc(S(f"slot_full{s}"), 16)
            for s in range(NSLOT):
                used[s] += 2 * E
                freed[s] = (S(f"slot_free{s}"), free0[s] + 2 * E + 1)
            freed[3] = freed[4] = freed[5] = None
            for layer in range(2):
                for q in range(7):
                    if q < 5:
                        a, b = PARTS2[q]
                        src = cols(ap["w_in_2"][layer], a * GW, 512)
                    else:
                        src = cols(ap["w_out_2"][layer], 512 * (q - 5), 512)
                    load(q % 3, slot(q % 3, KT, 512), src,
                         (S("w_lo_ready"), split_no(layer, 4 * (q + 1)) + LEAD))
                mlp_loads.append(used[:4])
                for s in range(3):
                    sp.wait_ge(*freed[s])
                sp.wait_ge(S("mix2_ready"), layer + 1)
                b = split_no(layer, 28)
                w1 = ap["mlp_w1_2"][layer].rearrange("(k p) (j n) -> j p k n", p=P, n=512)
                w2 = ap["mlp_w2_2"][layer].rearrange("(j q p) n -> j p q n", q=4, p=P)
                with sp.Fori(0, 4) as i:
                    for c in range(2):
                        sp.wait_ge(S("w_lo_ready"), b + 16 * i + 4 * c + 4)
                        sp.dma_start(slot(c, KT, 512), w1[i * 2 + c]).then_inc(S(f"slot_full{c}"), 16)
                    for c in range(2):
                        sp.wait_ge(S("w_lo_ready"), b + 16 * i + 4 * c + 12)
                        sp.dma_start(slot(MLP_SLOT[2 + c], 4, D), w2[i * 2 + c]).then_inc(S(f"slot_full{2 + c}"), 16)
                for c in range(2):
                    used[c] += 4
                    used[2 + c] += 4
                for s in range(3):
                    freed[s] = (S("w_lo_ready"), b + 64 + 4 * s + 4)
            sp.wait_ge(S("final"), 1)
            sp.dma_start(out, resid[:, :, 0:T]).then_inc(S("stored"), 16)
            sp.wait_ge(S("stored"), 16)

        @block.gpsimd
        def _(pool):
            pool.dma_start(resid[:, :, 0:T], ap["xT"]).then_inc(S("tokens_in"), 16)
            pool.dma_start(resid[:, :, T:N2], ap["ctxT"]).then_inc(S("tokens_in"), 16)
            pool.dma_start(big[:, PERS + names2["cR"][0]:PERS + names2["cR"][0] + C1_N], ap["c1"]).then_inc(S("c1_in"), 16)
            pool.dma_start(wgz, cols(ap["w_in"][0], 1024, 32)).then_inc(S("c1_in"), 16)
            pool.dma_start(gw[0:33, :], ap["gw"]).then_inc(S("c1_in"), 16)
            pool.dma_start(wr, ap["wr"]).then_inc(S("c1_in"), 16)
            pool.wait_ge(S("h_d"), 1)
            pool.wait_ge(S("sq_a"), 1)
            pool.dma_start(resid[:, :, T:N2], ap["ctx2T"]).then_inc(S("second_in"), 16)
            pool.wait_ge(S("mix1_ready"), 1)
            at = PERS + names2["cR"][0]
            pool.dma_start(big[:, at:at + C2_N], ap["c2"]).then_inc(S("second_in"), 16)
            pool.dma_start(big[:, at + C2_N:at + C2_N + 1024], ap["sgw"]).then_inc(S("second_in"), 16)
            at = PERS + V2_BASE
            pool.dma_start(big[:, at:at + 2 * V2_N], ap["v2"]).then_inc(S("second_in"), 16)

        @block.tensor
        def _(pe):
            used = [0] * NSLOT
            tiles = Tiles()
            credit(pe, [f"slot_free{s}" for s in range(NSLOT)] + [f"ada_cols{c}" for c in range(3)]
                   + ["bc_ps", "z_ps", "h1_ps0", "h1_ps1"])
            for c in range(2):
                pe.sem_inc(S(f"y_ps{c}"), 9)

            def mm(o, l, r, start=True, stop=True):
                return nc.tensor.matmul(o, l, r, start=start, stop=stop)

            def take(s):
                pe.wait_ge(S(f"slot_full{s}"), 16 * (used[s] + 1))

            def ada_chunk(c, ring, before, b, block, banks):
                pe.wait_ge(S(f"slot_full{ring}"), b)
                pe.wait_ge(S(f"ada_part{c}"), before + 1)
                for kk in range(2):
                    for g in range(4):
                        k = 2 * g + kk
                        m = mm(PB[banks[c]][32 * g:32 * g + 32, :], csil[:, block, k, :],
                               slot(ring, KT, 512)[:, k, :], kk == 0, kk == 1)
                m.then_inc(S(f"slot_free{ring}"), 1)

            def ada_columns(c, before, first_row, banks):
                pe.wait_ge(S(f"ada_part{c}"), before + 2)
                for q in range(4):
                    m = mm(PB[banks[3]][:, bass.ds(first_row + 2 * q, 2)], part[:, c, q * P:(q + 1) * P], sel2)
                m.then_inc(S(f"ada_cols{c}"), 1)

            def ada_first():
                banks = (4, 5, 6, 7)
                with pe.Fori(0, 4) as i:
                    for c in range(3):
                        ada_chunk(c, c, i, 16 + i * 16, 0, banks)
                        ada_columns(c, i, i * 24 + 8 * c, banks)
                for c in range(3):
                    used[c] += 4

            def ada_round(r):
                banks = (0, 1, 2, 3)
                for c in range(3):
                    ring = (1 + c) % 3
                    ada_chunk(c, ring, 4 + r, 16 * (used[ring] + 1), 1, banks)
                    used[ring] += 1
                    if c:
                        ada_columns(c - 1, 4 + r, 96 * (r // 4) + (r % 4) * 24 + 8 * (c - 1), banks)
                ada_columns(2, 4 + r, 96 * (r // 4) + (r % 4) * 24 + 16, banks)

            def norm(k, n):
                pe.wait_ge(S("sq_a"), k + 1)
                if k not in ROLLED:
                    pe.wait_ge(S("sq_d"), k + 1)
                sq = sq_out if ROLLED.get(k) == "out" else h
                for tt in range(n // P):
                    for t in range(KT):
                        m = mm(PB[4][:, 2 * tt:2 * tt + 2], sq[:, t, tt * P:(tt + 1) * P], ones[:, 0:2],
                               t == 0, t == KT - 1)
                m.then_inc(S("ss"), 1)
                pe.wait_ge(S("diag"), k + 1)
                mm(PB[4][:, 0:n], ones, rs[:, 0:n]).then_inc(S("rstd_ps"), 1)

            def bank_free(n):
                if n >= 4:
                    s, v = tiles.emptied(n - 4)
                    pe.wait_ge(s, v)

            def project(spec, weights, src, act_view=None):
                M, N, tok_major, col, tt, owner, _, _ = spec
                n = tiles.add(owner)
                bank_free(n)
                for k in range(KT):
                    if tok_major:
                        m = mm(PB[n % 4][0:M, 0:N], src[:, k, tt * P:(tt + 1) * P], weights[:, k, col:col + N],
                               k == 0, k == KT - 1)
                    else:
                        m = mm(PB[n % 4][0:M, 0:N], weights[:, k, col:col + P], src[:, k, 0:N],
                               k == 0, k == KT - 1)
                m.then_inc(S("tile_in"), 1)
                return m

            pe.wait_ge(S("first_in"), 32)
            pe.wait_ge(S("silu_c"), 2)
            ada_first()
            norm(0, N2)
            pe.wait_ge(S("h_a"), 1)
            pe.wait_ge(S("h_d"), 1)
            pe.wait_ge(S("c1_in"), 64)
            for n, group in enumerate(proj1_tiles()):
                take(n % 3)
                for spec in group:
                    m = project(spec, slot(n % 3, KT, 512), h)
                used[n % 3] += 1
                if n == 0:
                    q = tiles.add("D")
                    bank_free(q)
                    for k in range(KT):
                        m = mm(PB[q % 4][0:32, 0:N2], wgz[:, k, :], h[:, k, :], k == 0, k == KT - 1)
                    m.then_inc(S("tile_in"), 1)
                if n == 1:
                    pe.wait_ge(*tiles.emptied(q))
                    for tt in range(4):
                        m = mm(PB[4 + tt], gz[0:33, tt * P:(tt + 1) * P], gw[0:33, :])
                        m.then_inc(S("gate_ps"), 1)
            for x in ("A", "D"):
                pe.wait_ge(S("tile_out_" + x), tiles.owner.count(x))
            for r in (0,):
                ada_round(r)
            pe.wait_ge(S("la_ready"), 1)
            c0t, c1t = la[:, 2, :], la[:, 3, :]
            mm(PB[4][:, 0:256], c1("sufC", P), c0t[:, 0:256], True, False)
            mm(PB[4][:, 0:256], ones, c1t[:, 0:256], False, True)
            mm(PB[4][:, 256:512], c1("prefC", P), c0t[:, 256:512]).then_inc(S("kdec_ps"), 1)
            mm(PB[5][:, 0:256], c1("sufC", P), c1t[:, 0:256])
            mm(PB[5][:, 256:512], ones, c0t[:, 256:512], True, False)
            mm(PB[5][:, 256:512], c1("prefC", P), c1t[:, 256:512], False, True).then_inc(S("kdec_ps"), 1)
            for tt in range(2):
                mm(PB[6 + tt][:, 0:256], c1("sufS", P), la[:, tt, 0:256])
                mm(PB[6 + tt][:, 256:512], c1("prefS", P), la[:, tt, 256:512]).then_inc(S("kdec_ps"), 1)
            for d in range(2):
                pe.wait_ge(S("kdec_out"), d + 1)
                for ht in range(2):
                    for tt in range(2):
                        m = mm(PB[4 + d][:, ht * 256 + tt * P:ht * 256 + (tt + 1) * P],
                               la[:, tt, d * 256 + ht * P:d * 256 + (ht + 1) * P],
                               c1("prefI" if d == 0 else "sufI", P))
                m.then_inc(S("b_ps"), 1)
            for d in range(2):
                pe.wait_ge(S("kdec_out"), d + 3)
                for ht in range(2):
                    for tt in range(2):
                        m = mm(PB[6 + d][:, ht * 256 + tt * P:ht * 256 + (tt + 1) * P],
                               la[:, tt, d * 256 + ht * P:d * 256 + (ht + 1) * P],
                               c1("prefIm" if d == 0 else "sufIm", P))
                m.then_inc(S("bm_ps"), 1)
            for r in (1,):
                ada_round(r)
            pe.wait_ge(S("kwe_ready"), 1)
            pe.wait_ge(S("kwe_ready"), 2)
            pe.wait_ge(S("EA_ready"), 1)
            for d in range(2):
                for hh in range(GH):
                    for tt in range(2):
                        m = mm(PB[4][(hh % 2) * 64:(hh % 2) * 64 + 64, (d * 2 + hh // 2) * P:(d * 2 + hh // 2 + 1) * P],
                               kw[:, tt, d * 256 + hh * 64:d * 256 + hh * 64 + 64],
                               gv[:, 2 + tt, hh * P:(hh + 1) * P], tt == 0, tt == 1)
            m.then_inc(S("S0_ps"), 1)

            def chunk_update(bank, col, c, d):
                a = (c % 2) * 64
                for hh in range(GH):
                    m = mm(PB[bank][(hh % 2) * 64:(hh % 2) * 64 + 64, col + (hh // 2) * P:col + (hh // 2 + 1) * P],
                           ke[a:a + 64, c // 2, d * 256 + hh * 64:d * 256 + hh * 64 + 64],
                           gv[a:a + 64, c // 2, hh * P:(hh + 1) * P])
                return m
            chunk_update(5, 0, 0, 0)
            chunk_update(5, 256, 2, 0).then_inc(S("U_ps"), 1)
            pe.wait_ge(S("bm_out"), 1)
            chunk_update(6, 0, 2, 1).then_inc(S("U_ps"), 1)
            pe.wait_ge(S("bm_out"), 2)
            chunk_update(7, 0, 1, 0)
            chunk_update(7, 256, 1, 1).then_inc(S("U_ps"), 1)
            pe.wait_ge(S("S0_out"), 1)
            chunk_update(4, 0, 3, 1).then_inc(S("U_ps"), 1)
            for r in (2,):
                ada_round(r)
            pe.wait_ge(S("states_done"), 1)
            pe.wait_ge(S("qk_ready"), 1)
            for hp2 in range(2):
                for c in range(NC):
                    for hp in range(2):
                        for d in range(2):
                            a = hp2 * 64
                            col = (((c // 2) * 2 + hp) * 2 + d) * 64
                            m = mm(PB[4 + hp2][(c % 2) * 64:(c % 2) * 64 + 64, col:col + 64],
                                   kd[a:a + 64, d, hp * 256 + c * 64:hp * 256 + c * 64 + 64],
                                   qd[a:a + 64, d, hp * 256 + c * 64:hp * 256 + c * 64 + 64])
                m.then_inc(S("gsc_ps"), 1)
            for r in (3,):
                ada_round(r)
            pe.wait_ge(S("pg_ready"), 1)
            for hh in range(GH):
                for tt in range(2):
                    m = mm(PB[6 + hh // 2][:, (hh % 2) * 256 + tt * P:(hh % 2) * 256 + (tt + 1) * P],
                           gv[:, tt, hh * P:(hh + 1) * P], pg[:, hh % 2, tt * 2 + hh // 2, :])
            m.then_inc(S("gi_ps"), 1)
            for hp2 in range(2):
                a = hp2 * 64
                for hp in range(2):
                    for c in range(NC):
                        for d in range(2):
                            m = mm(PB[4 + hp2][:, hp * 256 + c * 64:hp * 256 + c * 64 + 64],
                                   Sg[a:a + 64, d, c, hp, :], qe[a:a + 64, d, hp * 256 + c * 64:hp * 256 + c * 64 + 64],
                                   d == 0, d == 1)
                m.then_inc(S("gj_ps"), 1)

            for r in (4, 5):
                ada_round(r)
            pe.wait_ge(S("kwr_ready"), 1)
            pe.wait_ge(S("og_ready"), 1)
            for d in range(2):
                for hh in range(RH):
                    for tt in range(2):
                        m = mm(PB[4 + d][:, hh * P:(hh + 1) * P], kwr[:, tt, d, hh * P:(hh + 1) * P],
                               rv[:, 2 + tt, hh * P:(hh + 1) * P], tt == 0, tt == 1)
            m.then_inc(S("Sr_ps"), 1)
            for n, src in enumerate((rq, rk)):
                for half in range(2):
                    b = 6 + half
                    if n:
                        pe.wait_ge(S("rope_out"), half + 1)
                    m = mm(PB[b], c1("rot1", P), src[:, 2 * half:2 * half + 2, :])
                    m.then_inc(S("rope_ps"), 1)
            for r in (6,):
                ada_round(r)
            pe.wait_ge(S("rk_ready"), 1)
            pe.wait_ge(S("Sr_out"), 1)
            for hh in range(RH):
                b = hh % 2
                if hh >= 2:
                    pe.wait_ge(S("pr_ready"), hh - 1)
                for jt in range(2):
                    m = mm(PB[4 + b][:, jt * T:(jt + 1) * T], rk[:, hh, jt * P:(jt + 1) * P], rq[:, hh, :])
                m.then_inc(S("rsc_ps"), 1)
                pe.wait_ge(S("pr_ready"), hh + 1)
                pe.wait_ge(S("rqd_ready"), hh + 1)
                if hh >= 2:
                    pe.wait_ge(S("or_out"), hh - 1)
                for jt in range(2):
                    mm(PB[6 + b][:, 0:T], rv[:, jt, hh * P:(hh + 1) * P], pr[:, b, jt * T:(jt + 1) * T], jt == 0, False)
                for d in range(2):
                    m = mm(PB[6 + b][:, 0:T], Sr[:, d, hh, :], rqd[:, b, d * T:(d + 1) * T], False, d == 1)
                m.then_inc(S("or_ps"), 1)
            pe.wait_ge(S("gsq_ready"), 1)
            for half in range(2):
                m = mm(PB[4 + half], ones, gn_t[:, 2 * half:2 * half + 2, :])
            m.then_inc(S("hnorm_ps"), 1)
            pe.wait_ge(S("or_out"), 4)
            for half in range(2):
                m = mm(PB[6 + half], ones, orr[:, 2 * half:2 * half + 2, :])
            m.then_inc(S("hnorm_ps"), 1)
            pe.wait_ge(S("rsq_ready"), 1)
            for half in range(2):
                m = mm(PB[6 + half], ones, gn_t[:, 2 * half:2 * half + 2, :])
            m.then_inc(S("hnorm_ps"), 1)
            for r in (7,):
                ada_round(r)
            pe.wait_ge(S("mix1_ready"), 1)
            pe.wait_ge(S("mod_out"), 3)
            for n in range(2):
                s = (n + 1) % 3
                take(s)
                for m_ in range(4):
                    m = project((P, T, False, m_ * P, None, "D", None, None), slot(s, KT, 512), mixb1)
                used[s] += 1

            pe.wait_ge(S("tile_out_D"), tiles.owner.count("D"))
            norm(1, T)
            pe.wait_ge(S("h_a"), 2)
            for tt in range(2):
                for k in range(KT):
                    m = mm(PB[5][:, tt * E:(tt + 1) * E], h[:, k, tt * P:(tt + 1) * P], wr[:, k, :], k == 0, k == KT - 1)
            m.then_inc(S("router_ps"), 1)
            for q in range(4):
                for k in range(4):
                    m = nc.tensor.transpose(PB[q][:, k * P:(k + 1) * P],
                                            h[:, (q % 2) * 4 + k, (q // 2) * P:(q // 2 + 1) * P], ident)
                m.then_inc(S("htm_ps"), 1)
            pe.wait_ge(S("routed"), 2)
            for tt in range(2):
                m = nc.tensor.transpose(PB[6][0:E, tt * P:(tt + 1) * P], aff[:, tt, :], ident)
            m.then_inc(S("router_ps"), 1)
            pe.wait_ge(S("routed"), 3)
            for tt in range(2):
                m = nc.tensor.transpose(PB[7][:, tt * E:(tt + 1) * E], mkT[:, tt * P:(tt + 1) * P], ident[0:E, 0:E])
            m.then_inc(S("router_ps"), 1)
            pe.wait_ge(S("routed"), 4)
            mm(PB[4][:, 0:E], c0("incl", P), mk[:, 0, :])
            mm(PB[4][:, E:2 * E], ones, mk[:, 0, :], True, False)
            mm(PB[4][:, E:2 * E], c0("incl", P), mk[:, 1, :], False, True).then_inc(S("router_ps"), 1)
            pe.wait_ge(S("routed"), 5)
            for tt in range(2):
                m = nc.tensor.transpose(PB[6][0:E, tt * P:(tt + 1) * P], pos[:, tt, :], ident)
            m.then_inc(S("router_ps"), 1)
            pe.wait_ge(S("routed"), 6)
            pe.wait_ge(S("htm_out"), 4)
            for k in range(KT):
                if k >= 4:
                    pe.wait_ge(S("xeT_out"), k - 3)
                for tt in range(2):
                    m = mm(PB[k % 4], htm[:, tt, k * P:(k + 1) * P], sel[:, tt, :], tt == 0, tt == 1)
                m.then_inc(S("xeT_ps"), 1)
            pe.wait_ge(S("xeT_out"), KT)
            pe.wait_ge(S("routed"), 7)
            free0 = [12, 12, 12, 0, 0, 0]
            with pe.Fori(0, E) as i:
                pe.wait_ge(S("xe_ready"), i + 1)
                pe.wait_ge(S("gs_out"), i + 1)
                for q in range(12):
                    s = q % 6
                    if q == 4:
                        pe.wait_ge(S("gu_ready"), i + 1)
                    if q == 8:
                        pe.wait_ge(S("bcm_ready"), i + 1)
                        pe.wait_ge(S("bcs_out"), i + 1)
                        mm(PB[7], ones[0:E, :], bcm).then_inc(S("bc_ps"), 1)
                        pe.wait_ge(S("hx_ready"), i + 1)
                        pe.wait_ge(S("ye_out"), i + 1)
                    pe.wait_ge(S(f"slot_full{s}"), 16 * (used[s] + 1 + q // 6) + i * 32)
                    if q < 8:
                        for kk in range(2):
                            k = 2 * (q % 4) + kk
                            for g in range(4):
                                m = mm(PB[4 + q // 4][32 * g:32 * g + 32, 0:FQ], xe[:, k, :],
                                       slot(s, 2, FF)[:, kk, g * FQ:(g + 1) * FQ], k == 0, k == KT - 1)
                    else:
                        a, b = DOWN_T[q - 8]
                        for t in range(a, b):
                            for g in range(4):
                                m = mm(PB[6][32 * g:32 * g + 32, 0:256], hx[:, t, :],
                                       slot(s, b - a, D)[:, t - a, g * 256:(g + 1) * 256], t == 0, t == FT - 1)
                    m.then_inc(S(f"slot_free{s}"), 1)
                pe.wait_ge(S("ye_out"), i + 1 + 1)
                pe.wait_ge(S("selg_ready"), i + 1 + 1)
                pe.wait_ge(S("acc_done"), i + 1)
                for g in range(4):
                    for x in range(2):
                        m = mm(PB[g][:, x * T:(x + 1) * T], ye[32 * g:32 * g + 32, x * P:(x + 1) * P],
                               selg[32 * g:32 * g + 32, :])
                m.then_inc(S("z_ps"), 1)
            for s in range(NSLOT):
                used[s] += 2 * E
            pe.wait_ge(S("acc_done"), E + 1)
            norm(2, T)
            pe.wait_ge(S("second_in"), 64)
            for layer in range(2):
                nf = N2 if layer == 0 else T
                k0 = 3 + 2 * layer
                norm(k0, N2)

                def layer_norm_sums(r):
                    pe.wait_ge(S("ln_in"), 2 * layer + r + 1)
                    for m_ in range(2):
                        src = acca if r == 0 else ln_sq
                        m = mm(PB[6][:, 0:nf], ones, src[:, m_, 0:nf], m_ == 0, m_ == 1)
                    m.then_inc(S("ln_ps"), 1)

                def split_product(o, st, mv, first, last):
                    mm(o, st[0], mv[0], first, False)
                    mm(o, st[1], mv[0], False, False)
                    return mm(o, st[0], mv[1], False, last)

                def w_parts(n, k, kts=KT, m=0):
                    return tuple(w_split(t, n, kts)[:, k, m * P:(m + 1) * P] for t in (w_hi, w_lo))

                def unit_product(j, n, tok_major, owner, tokens):
                    t = tiles.add(owner)
                    bank_free(t)
                    pe.wait_ge(S("w_lo_ready"), split_no(layer, unit_tiles(j)) + LEAD)
                    o = PB[t % 4]
                    if tok_major:
                        for x in range(n // GW):
                            a = (j % 2 * n // GW + x) * P
                            for k in range(KT):
                                w = tuple(w_split(v, j - j % 2 + k // 4, 4)[:, k % 4, :] for v in (w_hi, w_lo))
                                m = split_product(o[:, x * GW:(x + 1) * GW],
                                                  (h_hi[k][:, a:a + P], h_lo[k][:, a:a + P]), w, k == 0, k == KT - 1)
                    else:
                        for k in range(KT):
                            if tokens is not None:
                                pe.wait_ge(S("h_split"), tokens + k + 1)
                            m = split_product(o[:, 0:n], w_parts(j, k), (h_hi[k][:, 0:n], h_lo[k][:, 0:n]),
                                              k == 0, k == KT - 1)
                    m.then_inc(S("tile_in"), 1)

                for g, group in enumerate(proj2_tiles(layer)):
                    if g == 4:
                        pe.wait_ge(S("tile_out_A"), A_TILES_BEFORE[layer] + n_a(proj2_tiles(layer)[:3]))
                        mm(PB[4], c2("rot2", P), qf[:, :, 0:T]).then_inc(S("rope2_ps"), 1)
                        mm(PB[5], c2("rot2", P), kf[:, :, 0:T]).then_inc(S("rope2_ps"), 1)
                        layer_norm_sums(0)
                    for x, (_, n, tok_major, _, _, owner, _, _) in enumerate(group):
                        if g == 4 and x == 2:
                            layer_norm_sums(1)
                        unit_product(4 * g + x, n, tok_major, owner, 24 * layer if 4 * g + x == 0 else None)
                for x in ("A", "D"):
                    pe.wait_ge(S("tile_out_" + x), tiles.owner.count(x))
                pe.wait_ge(S("qk2_ready"), layer + 1)
                units = attn_units(layer)
                u0 = UNIT_AT[layer]

                def scores(u):
                    s_, qt, hh = units[u]
                    if u >= 2:
                        pe.wait_ge(S("exp_done"), u0 + u - 1)
                    a, nk = (hh % 2) * 64, 512 if s_ == 0 else 256
                    for comp in range(2):
                        r = slice(a + 32 * comp, a + 32 * comp + 32)
                        m = mm(PB[2 * (u % 2) + comp][:, 0:nk], qf[r, hh // 2, s_ * T + qt * P:s_ * T + (qt + 1) * P],
                               kf[r, hh // 2, N2 - nk:N2])
                    m.then_inc(S("asc_ps"), 1)

                def weigh_values(u):
                    s_, qt, hh = units[u]
                    nkt = 4 if s_ == 0 else 2
                    pe.wait_ge(S("wt_ready"), u0 + u + 1)
                    for kt in range(nkt):
                        m = mm(PB[6 + s_][(hh % 2) * 64:(hh % 2) * 64 + 64,
                                          (hh // 2) * T + qt * P:(hh // 2) * T + (qt + 1) * P],
                               vt[:, 4 - nkt + kt, hh * 64:(hh + 1) * 64], WT[:, u % 2, kt * P:(kt + 1) * P],
                               kt == 0, kt == nkt - 1)
                    m.then_inc(S("pv_ps"), 1)

                scores(0)
                scores(1)
                for u, (s_, qt, hh) in enumerate(units):
                    if u + 2 < len(units):
                        scores(u + 2)
                    pe.wait_ge(S("w_ready"), u0 + u + 1)
                    if u >= 2:
                        pe.wait_ge(S("wt_ready"), u0 + u - 1)
                    for kt in range(4 if s_ == 0 else 2):
                        m = nc.tensor.transpose(PB[4 + u % 2][:, kt * P:(kt + 1) * P],
                                                Eb[:, u % 2, 0, kt * P:(kt + 1) * P], ident)
                    m.then_inc(S("wt_ps"), 1)
                    if u:
                        weigh_values(u - 1)
                    if u == len(units) - 1:
                        pe.wait_ge(S("exp_done"), u0 + len(units))
                        pe.wait_ge(S("svn_ready"), layer + 1)
                        for g in range(4):
                            for x in range(nf // P):
                                m = mm(PB[g // 2][(g % 2) * 64:(g % 2) * 64 + 64, x * P:(x + 1) * P],
                                       sv[:, x, g * 64:(g + 1) * 64], sgw[:, layer, g, :])
                        m.then_inc(S("sg_ps"), 1)
                weigh_values(len(units) - 1)
                pe.wait_ge(S("osq_ready"), layer + 1)
                for m_ in range(2):
                    m = mm(PB[2 + m_][:, 0:nf], c2("ones64", P), tg[:, m_, 0:nf])
                m.then_inc(S("oss_ps"), 1)
                pe.wait_ge(S("h_split"), 24 * layer + 16)
                for q in range(KT):
                    unit_product(20 + q, nf, False, "D", None)
                pe.wait_ge(S("tile_out_D"), tiles.owner.count("D"))
                norm(k0 + 1, nf)
                b = split_no(layer, 28) + LEAD
                with pe.Fori(0, 4) as i:
                    for c in range(2):
                        for q in range(4):
                            n = 4 * c + q
                            pe.wait_ge(S("w_lo_ready"), b + 16 * i + n + 1)
                            pe.wait_ge(S("h1_relu"), 32 * layer + 8 * i + n + 1)
                            for k in range(KT):
                                if n == 0:
                                    pe.wait_ge(S("h_split"), 24 * layer + 16 + k + 1)
                                m = split_product(PB[q][:, 0:nf], w_parts(n, k), (h_hi[k][:, 0:nf], h_lo[k][:, 0:nf]),
                                                  k == 0, k == KT - 1)
                            m.then_inc(S(f"h1_ps{c}"), 1)
                    for c in range(2):
                        pe.wait_ge(S("h1_ready"), 32 * layer + 8 * i + 4 * c + 4)
                        for dt in range(KT):
                            n = 8 + 4 * c + dt // 2
                            if dt % 2 == 0:
                                pe.wait_ge(S("w_lo_ready"), b + 16 * i + n + 1)
                            pe.wait_ge(S("y_out"), 64 * layer + 16 * i + 8 * c + dt + 1)
                            for q in range(4):
                                m = split_product(PB[4 + dt % 4][:, 0:nf], w_parts(n, q, 4, dt % 2),
                                                  (h1_hi[c][:, q, 0:nf], h1_lo[c][:, q, 0:nf]), q == 0, q == 3)
                            m.then_inc(S(f"y_ps{c}"), 1)
                pe.wait_ge(S("y_out"), 64 * (layer + 1) + 4)
            norm(7, T)

        NORM_SETS = [(0, 0, 8), (0, 1, 32), (1, 3, 8), (1, 5, 32), (2, 4, 8), (2, 6, 32)]
        U_AT = {(0, 0): (5, 0), (2, 0): (5, 256), (2, 1): (6, 0), (1, 0): (7, 0), (1, 1): (7, 256), (3, 1): (4, 0)}

        @block.scalar
        def _(act):
            link = linker(act, "act_chain")
            A = nc.scalar.activation
            credit(act, [f"ada_part{c}" for c in range(3)] + ["gs_out", "bcs_out", "ye_out"])
            act.sem_inc(S("h1_relu"), 4)
            ntile = [0]

            def ada_first():
                with act.Fori(0, 4) as i:
                    for c in range(3):
                        act.wait_ge(S(f"slot_free{c}"), i + 2)
                        act.wait_ge(S(f"ada_cols{c}"), i + 1)
                        A(part[:, c, :], PB[4 + c], ACT.Copy).then_inc(S(f"ada_part{c}"), 1)

            def ada_round(r):
                for c in range(3):
                    act.wait_ge(S(f"slot_free{(1 + c) % 3}"), 4 + r + 2)
                    act.wait_ge(S(f"ada_cols{c}"), 4 + r + 1)
                    A(part[:, c, :], PB[c], ACT.Copy).then_inc(S(f"ada_part{c}"), 1)

            def norm_squares(k, n):
                A(h[:, 0:4, 0:n], resid[:, 0:4, 0:n], ACT.Square).then_inc(S("sq_a"), 1)

            def norm_sqrt(k, n):
                act.wait_ge(S("ms"), k + 1)
                A(rm[:, 0:n // P], rm[:, 0:n // P], ACT.Sqrt).then_inc(S("rms"), 1)

            def norm_affine(k):
                act.wait_ge(S("hn"), affine_no(k) + 1)
                a = NORMS[k][0]
                layer, _, row = NORM_SETS[a]
                for t in range(KT):
                    i_ = A(h[:, t, 0:T], h[:, t, 0:T], ACT.Identity, bias=modv[:, layer, row - 8 + t, 0:1],
                           scale=asc[:, a, t, 0:1])
                i_.then_inc(S("h_a"), 1)

            def tile_out(ins_fn):
                ins_fn().then_inc(S("tile_out_A"), 1)

            act.wait_ge(S("first_in"), 32)
            act.wait_ge(S("csil_zero"), 1)
            for b in range(2):
                A(csil[:, b, :, 0:2], v0("cv", 2, 2, KT)[:, b, :, :].rearrange("p s k -> p k s"), ACT.Silu) \
                    .then_inc(S("silu_c"), 1)
            A(lg[:, 1, :], v0("rdl", 8), ACT.Abs).then_inc(S("lg_steps"), 1)
            ada_first()
            act.wait_ge(S("tokens_in"), 32)
            norm_squares(0, N2)
            norm_sqrt(0, N2)
            norm_affine(0)
            n = 0
            for g, group in enumerate(proj1_tiles()):
                if g == 1:
                    n += 1
                if g == 2:
                    for tt in range(4):
                        act.wait_ge(S("gate_ps"), tt + 1)
                        A(la[:, tt, :], PB[4 + tt], ACT.Copy).then_inc(S("gate_out"), 1)
                for M, N, _, _, _, owner, dst, func in group:
                    if owner == "A":
                        act.wait_ge(S("tile_in"), n + 1)
                        if func == "silu":
                            i_ = A(dst, PB[n % 4][0:M, 0:N], ACT.Silu)
                        else:
                            i_ = A(dst, PB[n % 4][0:M, 0:N], ACT.Copy, scale=func or 1.0)
                        i_.then_inc(S("tile_out_A"), 1)
                    n += 1
            act.wait_ge(S("gate_out"), 4)
            link(A(lt, la, ACT.Abs))
            link(A(lt, lt, ACT.Exp, scale=-1.0))
            act.wait_ge(S("lg_steps"), 1)
            link(A(lg[:, 1, :], lg[:, 1, :], ACT.Exp, scale=-1.0))
            A(lt, lt, ACT.Ln, bias=1.0).then_inc(S("lt_ready"), 1)
            A(lg[:, 1, :], lg[:, 1, :], ACT.Ln, bias=1.0).then_inc(S("lg_steps"), 1)
            for r in (0,):
                ada_round(r)
            for n in range(4):
                act.wait_ge(S("kdec_ps"), n + 1)
                dst = kw[:, n, :] if n < 2 else ke[:, n - 2, :]
                A(dst, PB[4 + n], ACT.Exp, scale=1 / GATE_TAU).then_inc(S("kdec_out"), 1)
            for d in range(2):
                act.wait_ge(S("b_ps"), d + 1)
                i_ = A(EA[:, d, :], PB[4 + d], ACT.Exp, scale=1 / GATE_TAU)
            i_.then_inc(S("EA_ready"), 1)
            act.wait_ge(S("bm_out"), 2)
            link(A(ep, em, ACT.Exp, scale=1 / GATE_TAU))
            A(em, em, ACT.Exp, scale=-1 / GATE_TAU).then_inc(S("e_ready"), 1)
            act.wait_ge(S("wk_in"), 1)
            A(wk, wk, ACT.Exp).then_inc(S("wk_ready"), 1)
            for r in (1, 2, 3):
                ada_round(r)
            for hp2 in range(2):
                act.wait_ge(S("gj_ps"), hp2 + 1)
                A(og[:, hp2:GH:2, :], PB[4 + hp2][:, :].rearrange("p (a b) -> p a b", a=2), ACT.Copy).then_inc(S("j_out"), 1)
            for r in (4, 5):
                ada_round(r)
            act.wait_ge(S("Sr_ps"), 1)
            for d in range(2):
                i_ = A(Sr[:, d, :, :], PB[4 + d][:, :].rearrange("p (a b) -> p a b", a=4), ACT.Copy)
            i_.then_inc(S("Sr_out"), 1)
            for r in (6,):
                ada_round(r)
            act.wait_ge(S("lg_ready"), 1)
            act.wait_ge(S("og_ready"), 1)

            def decays(hh):
                b = hh % 2
                if hh >= 2:
                    act.wait_ge(S("pr_ready"), hh - 1)
                    act.wait_ge(S("or_ps"), hh - 1)
                for d in range(2):
                    i_ = A(dec[:, b, d * 512:(d + 1) * 512], c1("rel", 2, 512)[:, d, :], ACT.Exp,
                           scale=lg[:, 0, d * 4 + hh:d * 4 + hh + 1])
                i_.then_inc(S("dec_in"), 1)
                for d in range(2):
                    i_ = A(rqd[:, b, d * T:(d + 1) * T], c1("qpos", 2, T)[:, d, :], ACT.Exp,
                           scale=lg[:, 0, d * 4 + hh:d * 4 + hh + 1])
                i_.then_inc(S("rqe"), 1)

            decays(0)
            for hh in range(RH):
                if hh + 1 < RH:
                    decays(hh + 1)
                act.wait_ge(S("or_ps"), hh + 1)
                A(orr[:, hh, :], PB[6 + hh % 2][:, 0:T], ACT.Copy).then_inc(S("or_out"), 1)
            act.wait_ge(S("hn_ms"), 1)
            A(tmp1, tmp1, ACT.Sqrt).then_inc(S("hn_rms"), 1)
            ada_round(7)

            def norm(k):
                n = NORMS[k][2]
                if k not in ROLLED:
                    norm_squares(k, n)
                norm_sqrt(k, n)
                if NORMS[k][0] is not None and k < 3:
                    norm_affine(k)

            def norm_high(k):
                a, _, n = NORMS[k]
                layer, _, row = NORM_SETS[a]
                for t in range(KT):
                    act.wait_ge(S("h_scaled"), KT * (k - 3) + t + 1)
                    for s_ in range(n // T):
                        c_ = slice(s_ * T, (s_ + 1) * T)
                        i_ = A(h_hi[t][:, c_], h[:, t, c_], ACT.Identity, bias=modv[:, layer, row - 8 + t, s_:s_ + 1])
                    i_.then_inc(S("h_hi_ready"), 1)

            act.wait_ge(S("tile_out_D"), 13 + KT)
            norm(1)
            for q in range(4):
                act.wait_ge(S("htm_ps"), q + 1)
                A(htm[:, q // 2, (q % 2) * 512:(q % 2 + 1) * 512], PB[q], ACT.Copy).then_inc(S("htm_out"), 1)
            act.wait_ge(S("routed"), 1)
            A(aff, aff, ACT.Exp).then_inc(S("affe"), 1)
            for k in range(KT):
                act.wait_ge(S("xeT_ps"), k + 1)
                A(xeT[:, k, :], PB[k % 4], ACT.Copy).then_inc(S("xeT_out"), 1)
            act.wait_ge(S("xeT_out"), KT)
            with act.Fori(0, E) as i:
                act.wait_ge(S("slot_free1"), 12 + 2 * i + 1)
                A(xe, xeT[:, :, bass.ds(i * CAP, CAP)], ACT.Copy).then_inc(S("xe_ready"), 1)
                act.wait_ge(S("slot_free3"), 2 * i + 1 + 1)
                act.wait_ge(S("gu_ready"), i + 1)
                A(gs, PB[4][:, 0:FQ], ACT.Silu).then_inc(S("gs_out"), 1)
                act.wait_ge(S("bc_ps"), i + 1 + 1)
                act.wait_ge(S("selg_ready"), i + 1)
                A(bcs, PB[7], ACT.Copy).then_inc(S("bcs_out"), 1)
                act.wait_ge(S("slot_free5"), 2 * i + 2 + 1)
                act.wait_ge(S("z_ps"), i + 1)
                A(ye, PB[6][:, 0:256], ACT.Copy).then_inc(S("ye_out"), 1)
            act.wait_ge(S("acc_done"), E + 1)
            norm(2)
            act.wait_ge(S("x_in2"), 1)
            act.wait_ge(S("second_in"), 64)
            FUNC = {None: ACT.Copy, "silu": ACT.Silu, "gelu": ACT.Gelu_apprx_tanh, "sigmoid": ACT.Sigmoid}
            for layer in range(2):
                nf = N2 if layer == 0 else T
                k0 = 3 + 2 * layer

                def w_high(j):
                    if j % 4 == 0:
                        s = j // 4 % 3 if j < 28 else 0
                        loads = mlp_loads[layer][s] - (7 - s + 2) // 3 + j // 12 if j < 28 else mlp_loads[layer][0]
                        act.wait_ge(S(f"slot_full{s}"), 16 * (loads + 1))
                    if j >= NWB:
                        act.wait_ge(S("tile_in"), PROJ2_AT[layer] + unit_tiles(j - NWB))
                    A(proj_split(w_hi, j), proj_unit(layer, j) if j < 28 else w_unit(j - 28), ACT.Copy) \
                        .then_inc(S("w_hi_ready"), 1)

                def h_high(tiles_):
                    for k in tiles_:
                        A(h_hi[k][:, 0:nf], h[:, k, 0:nf], ACT.Copy).then_inc(S("h_hi_ready"), 1)

                for j in range(NWB):
                    w_high(j)
                norm(k0)
                norm_high(k0)
                n = PROJ2_AT[layer]
                for group in proj2_tiles(layer):
                    for M, N, tok_major, _, _, owner, dst, func in group:
                        if owner == "A":
                            act.wait_ge(S("tile_in"), n + 1)
                            src = PB[n % 4][0:M, 0:N]
                            if tok_major:
                                src = src.rearrange("p (t n) -> p t n", n=GW)
                            A(dst, src, FUNC[func]).then_inc(S("tile_out_A"), 1)
                        w_high(n - PROJ2_AT[layer] + NWB)
                        n += 1
                act.wait_ge(S("lam_in"), layer + 1)
                A(s4[:, 2:4], s4[:, 0:2], ACT.Exp).then_inc(S("lam_exp"), 1)
                units = attn_units(layer)
                u0 = UNIT_AT[layer]

                def exps(u):
                    nk = 512 if units[u][0] == 0 else 256
                    act.wait_ge(S("amax"), u0 + u + 1)
                    if u >= 2:
                        act.wait_ge(S("wt_ps"), u0 + u - 1)
                    for comp in range(2):
                        i_ = A(Eb[:, u % 2, comp, 0:nk], PB[2 * (u % 2) + comp][:, 0:nk], ACT.Exp,
                               bias=s4[:, 16 + 2 * (u % 2) + comp:17 + 2 * (u % 2) + comp], scale=float(DQ) ** -0.5,
                               accum_out=s4[:, 20 + 2 * (u % 2) + comp:21 + 2 * (u % 2) + comp])
                    i_.then_inc(S("exp_done"), 1)

                exps(0)
                for u, (s_, qt, hh) in enumerate(units):
                    if u + 1 < len(units):
                        exps(u + 1)
                    nk = 512 if s_ == 0 else 256
                    act.wait_ge(S("wt_ps"), u0 + u + 1)
                    if u >= 2:
                        act.wait_ge(S("pv_ps"), u0 + u - 1)
                    A(WT[:, u % 2, 0:nk], PB[4 + u % 2][:, 0:nk], ACT.Copy).then_inc(S("wt_ready"), 1)
                    if u == 2:
                        act.wait_ge(S("ln_var"), layer + 1)
                        A(rs[:, 0:nf], rs[:, 0:nf], ACT.Sqrt).then_inc(S("ln_std"), 1)
                        act.wait_ge(S("sv_var"), layer + 1)
                        A(s4[:, 12:12 + nf // P], s4[:, 12:12 + nf // P], ACT.Sqrt).then_inc(S("sv_std"), 1)
                    if u == 5:
                        act.wait_ge(S("ln_out"), layer + 1)
                        for m_ in range(2):
                            i_ = A(mix[:, m_, 0:nf], acca[:, m_, 0:nf], ACT.Silu,
                                   bias=v2(layer, "lab", 2)[:, m_:m_ + 1], scale=v2(layer, "lag", 2)[:, m_:m_ + 1])
                        i_.then_inc(S("ya_ready"), 1)
                    if u == 6:
                        act.wait_ge(S("ya_ready"), layer + 1)
                        h_high(MIX_ORDER[:2])
                        act.wait_ge(S("yd_ready"), layer + 1)
                        h_high(MIX_ORDER[2:4])
                act.wait_ge(S("yc_ready"), layer + 1)
                h_high(MIX_ORDER[4:6])
                act.wait_ge(S("o_ms"), layer + 1)
                A(tc[:, :, 0:nf], tc[:, :, 0:nf], ACT.Sqrt).then_inc(S("o_rms"), 1)
                act.wait_ge(S("mix2_ready"), layer + 1)
                h_high(MIX_ORDER[6:])
                for q in range(KT):
                    w_high(20 + q + NWB)
                    act.wait_ge(S("tile_out_D"), D_TILES_AFTER_OUT[layer] - KT + q + 1)
                    i_ = A(sq_out[:, q, 0:nf], resid[:, q, 0:nf], ACT.Square)
                i_.then_inc(S("sq_a"), 1)
                norm(k0 + 1)
                norm_high(k0 + 1)

                def mlp_round(i, last):
                    for n in range(16):
                        c, q = n // 4, n % 4
                        act.wait_ge(*unit_done(layer, i, n))
                        if n < 8:
                            act.wait_ge(S(f"y_ps{c}"), 32 * layer + 8 * i + 9)
                            A(h1[:, c, q, 0:nf], PB[q][:, 0:nf], ACT.Relu).then_inc(S("h1_relu"), 1)
                        if n < 12 or not last:
                            m, r = (n + NWB) % 16, i + (n >= 12)
                            if m % 4 == 0:
                                s = m // 4
                                act.wait_ge(S(f"slot_full{s}"), 16 * (mlp_loads[layer][s] + 1) + r * 16)
                            A(round_split(w_hi, m), w_unit(m), ACT.Copy).then_inc(S("w_hi_ready"), 1)
                        if n >= 12 and last:
                            nx = N2 if layer == 0 else T
                            for dt in (2 * q, 2 * q + 1):
                                act.wait_ge(S("y_out"), 64 * layer + 56 + dt + 1 + 4)
                                i_ = A(h[:, dt, 0:nx], resid[:, dt, 0:nx], ACT.Square)
                            if n == 15:
                                i_.then_inc(S("sq_a"), 1)
                        if n < 8:
                            act.wait_ge(S("h1_sq"), 32 * layer + 8 * i + n + 1)
                            A(h1_hi[c][:, q, 0:nf], h1[:, c, q, 0:nf], ACT.Copy).then_inc(S("h1_hi_ready"), 1)

                with act.Fori(0, 3) as i:
                    mlp_round(i, False)
                mlp_round(3, True)
                act.wait_ge(S("y_out"), 64 * (layer + 1) + 4)
            norm(7)

        @block.vector
        def _(dve):
            link = linker(dve, "dve_chain")
            V = nc.vector
            credit(dve, ["gu_ready", "acc_done", "selg_ready"])
            dve.sem_inc(S("w_lo_ready"), LEAD)
            dve.sem_inc(S("y_out"), 4)

            def tt(o, a, b, op):
                return V.tensor_tensor(o, a, b, op)

            def norm_squares(k, n):
                tt(h[:, 4:8, 0:n], resid[:, 4:8, 0:n], resid[:, 4:8, 0:n], ALU.mult).then_inc(S("sq_d"), 1)

            def norm_rest(k, n):
                nt = n // P
                dve.wait_ge(S("ss"), k + 1)
                V.tensor_scalar(rm[:, 0:nt], PB[4][:, 0:2 * nt].rearrange("p (t x) -> p t x", x=2)[:, :, 0],
                                1.0 / D, EPS, ALU.mult, ALU.add).then_inc(S("ms"), 1)
                dve.wait_ge(S("rms"), k + 1)
                link(V.reciprocal(rm[:, 0:nt], rm[:, 0:nt]))
                tt(rs[:, 0:n].rearrange("p (t x) -> p t x", x=P), bc(ident, 1, [P, nt, P]),
                   bc(rm[:, 0:nt], 2, [P, nt, P]), ALU.mult).then_inc(S("diag"), 1)
                dve.wait_ge(S("rstd_ps"), k + 1)
                rstd = PB[4]
                a, w, _ = NORMS[k]
                if a is None:
                    for t in range(KT):
                        i_ = V.scalar_tensor_tensor(resid[:, t, 0:n], resid[:, t, 0:n],
                                                    v0("norms", 8, KT)[:, w, t:t + 1], rstd[:, 0:n], ALU.mult, ALU.mult)
                    return i_
                layer, _, row = NORM_SETS[a]
                if k < 3:
                    tt(h[:, :, 0:T], resid[:, :, 0:T], bc(rstd[:, 0:T], 1, [P, KT, T]), ALU.mult).then_inc(S("hn"), 1)
                    if n > T:
                        link(tt(h[:, :, T:N2], resid[:, :, T:N2], bc(rstd[:, T:N2], 1, [P, KT, T]), ALU.mult))
                        for t in range(KT):
                            i_ = V.tensor_scalar(h[:, t, T:N2], h[:, t, T:N2], asc[:, a, t, 1:2],
                                                 modv[:, layer, row - 8 + t, 1:2], ALU.mult, ALU.add)
                        i_.then_inc(S("h_d"), 1)
                    return
                for t in range(KT + 1):
                    if t < KT:
                        for s_ in range(n // T):
                            c_ = slice(s_ * T, (s_ + 1) * T)
                            i_ = V.scalar_tensor_tensor(h[:, t, c_], resid[:, t, c_], asc[:, a, t, s_:s_ + 1],
                                                        rstd[:, c_], ALU.mult, ALU.mult)
                        i_.then_inc(S("h_scaled"), 1)
                    if t:
                        dve.wait_ge(S("h_hi_ready"), 24 * (layer - 1) + 16 * ((k - 3) % 2) + t)
                        for s_ in range(n // T):
                            c_ = slice(s_ * T, (s_ + 1) * T)
                            i_ = V.scalar_tensor_tensor(h_lo[t - 1][:, c_], h[:, t - 1, c_],
                                                        modv[:, layer, row - 9 + t, s_:s_ + 1],
                                                        h_hi[t - 1][:, c_].bitcast(F32), ALU.add, ALU.subtract)
                        i_.then_inc(S("h_split"), 1)

            TAPS_AT = [0]
            d_out = [n_d(proj1_tiles()) + 1 + KT]
            V.memset(csil, 0.0).then_inc(S("csil_zero"), 1)
            V.memset(gz[32:33, :], 1.0)
            dve.wait_ge(S("tokens_in"), 32)
            norm_squares(0, N2)
            def modulation(layers, rounds, bank, sets):
                for c in range(3):
                    dve.wait_ge(S(f"ada_cols{c}"), rounds + 1)
                for x, layer in enumerate(layers):
                    tt(modv[:, layer, :, :], PB[bank][:, 96 * x:96 * x + 96].rearrange("p (a b) -> p a b", a=48),
                       bc(v0("bada", 3, 48)[:, layer, :], 2, [P, 48, 2]), ALU.add).then_inc(S("mod_out"), 1)
                dve.wait_ge(S("mod_out"), layers[-1] + 1)
                for k in sets:
                    layer, w, row = NORM_SETS[k]
                    i_ = V.scalar_tensor_tensor(asc[:, k, :, :], modv[:, layer, row:row + 8, :], 1.0,
                                                bc(v0("norms", 8, KT)[:, w, :], 2, [P, KT, 2]), ALU.add, ALU.mult)
                link(i_)

            dve.wait_ge(S("first_in"), 32)
            modulation([0], 4, 7, (0, 1))
            norm_rest(0, N2)
            n = 0
            for g, group in enumerate(proj1_tiles()):
                for M, N, _, _, _, owner, dst, func in group:
                    if owner == "D":
                        dve.wait_ge(S("tile_in"), n + 1)
                        V.tensor_copy(dst, PB[n % 4][0:M, 0:N]).then_inc(S("tile_out_D"), 1)
                    n += 1
                if g == 0:
                    dve.wait_ge(S("tile_in"), n + 1)
                    V.tensor_copy(gz[0:32, :], PB[n % 4][0:32, 0:N2]).then_inc(S("tile_out_D"), 1)
                    n += 1
            dve.wait_ge(S("lt_ready"), 1)
            V.scalar_tensor_tensor(la, la, 0.0, lt, ALU.min, ALU.subtract).then_inc(S("la_ready"), 1)
            dve.wait_ge(S("lg_steps"), 2)
            V.scalar_tensor_tensor(lg[:, 0, :], v0("rdl", 8), 0.0, lg[:, 1, :], ALU.min, ALU.subtract) \
                .then_inc(S("lg_ready"), 1)
            dve.wait_ge(S("c1_in"), 64)
            dve.wait_ge(S("lg_ready"), 1)
            tt(wk, c1("kpos", 2, 8), bc(lg[:, 0, :], 1, [P, 2, 8]), ALU.mult).then_inc(S("wk_in"), 1)
            dve.wait_ge(S("kdec_out"), 2)
            for x in range(2):
                i_ = tt(kw[:, x, :].rearrange("p (a b) -> p a b", a=2), kw[:, x, :].rearrange("p (a b) -> p a b", a=2),
                        bc(gktm[:, 2 + x, :], 1, [P, 2, 256]), ALU.mult)
            i_.then_inc(S("kwe_ready"), 1)
            dve.wait_ge(S("kdec_out"), 4)
            for x in range(2):
                i_ = tt(ke[:, x, :].rearrange("p (a b) -> p a b", a=2), ke[:, x, :].rearrange("p (a b) -> p a b", a=2),
                        bc(gktm[:, x, :], 1, [P, 2, 256]), ALU.mult)
            i_.then_inc(S("kwe_ready"), 1)
            dve.wait_ge(S("tile_in"), PROJ1_END[-1])
            for d in range(2):
                dve.wait_ge(S("bm_ps"), d + 1)
                V.tensor_scalar(em[:, d, :], PB[6 + d], EXP_CLAMP * GATE_TAU, -EXP_CLAMP * GATE_TAU,
                                ALU.min, ALU.max).then_inc(S("bm_out"), 1)
            dve.wait_ge(S("EA_ready"), 1)
            gq2, gk2 = b1("gq", 512), b1("gk", 512)
            tt(qe, EA, bc(gq2, 1, [P, 2, 512]), ALU.mult)
            dve.wait_ge(S("e_ready"), 1)
            tt(qd, qd, bc(gq2, 1, [P, 2, 512]), ALU.mult)
            tt(kd, em, bc(gk2, 1, [P, 2, 512]), ALU.mult).then_inc(S("qk_ready"), 1)
            dve.wait_ge(S("S0_ps"), 1)
            V.tensor_copy(Sg[:, 0, 0, :, :], PB[4][:, 0:256].rearrange("p (a b) -> p a b", a=2))
            V.tensor_copy(Sg[:, 1, 3, :, :], PB[4][:, 256:512].rearrange("p (a b) -> p a b", a=2)) \
                .then_inc(S("S0_out"), 1)
            dve.wait_ge(S("S0_out"), 1)
            V.memset(pg, 0.0)
            dve.wait_ge(S("U_ps"), 4)
            for step in range(1, 4):
                for d, (c_old, c_new) in enumerate(((step - 1, step), (4 - step, 3 - step))):
                    bank, col = U_AT[(c_old, d)]
                    for hp in range(2):
                        e = hp * 256 + c_old * 64 + (63 if d == 0 else 0)
                        i_ = V.scalar_tensor_tensor(Sg[:, d, c_new, hp, :], Sg[:, d, c_old, hp, :],
                                                    EA[:, d, e:e + 1], PB[bank][:, col + hp * P:col + (hp + 1) * P],
                                                    ALU.mult, ALU.add)
                        if d == 1 and hp == 1 and step == 3:
                            i_.then_inc(S("states_done"), 1)
                        elif d == 1 and hp == 1:
                            link(i_)
            dve.wait_ge(S("gsc_ps"), 2)
            for hp2 in range(2):
                i_ = tt(prt[:, 4 * hp2:4 * hp2 + 4, :], PB[4 + hp2][:, :].rearrange("p (a b) -> p a b", a=4),
                        bc(c1("cmask", P), 1, [P, 4, P]), ALU.mult)
            link(i_)
            for hp2 in range(2):
                for cp in range(2):
                    ps_ = slice(64 * cp, 64 * cp + 64)
                    i_ = tt(pg[ps_, hp2, :, 64 * cp:64 * cp + 64], prt[ps_, 4 * hp2:4 * hp2 + 4, 0:64],
                            prt[ps_, 4 * hp2:4 * hp2 + 4, 64:128], ALU.add)
            i_.then_inc(S("pg_ready"), 1)
            dve.wait_ge(S("gi_ps"), 1)
            dve.wait_ge(S("j_out"), 2)
            for hp in range(2):
                i_ = tt(og[:, 2 * hp:2 * hp + 2, :], og[:, 2 * hp:2 * hp + 2, :],
                        PB[6 + hp][:, :].rearrange("p (a b) -> p a b", a=2), ALU.add)
            i_.then_inc(S("og_ready"), 1)
            dve.wait_ge(S("wk_ready"), 1)
            for x in range(2):
                for d in range(2):
                    i_ = tt(kwr[:, x, d, :].rearrange("p (a b) -> p a b", a=4), rktm[:, x, :].rearrange("p (a b) -> p a b", a=4),
                            bc(wk[:, x, d * 4:d * 4 + 4], 2, [P, 4, P]), ALU.mult)
            i_.then_inc(S("kwr_ready"), 1)
            for n, src in enumerate((rq, rk)):
                for half in range(2):
                    dve.wait_ge(S("rope_ps"), 2 * n + half + 1)
                    tmp = tmp1[:, 2 * n + half, :].rearrange("p (a b) -> p a b", a=2)
                    tt(tmp, PB[6 + half][:, :].rearrange("p (a b) -> p a b", a=2), bc(c1("sin1", T), 1, [P, 2, T]), ALU.mult) \
                        .then_inc(S("rope_out"), 1)
                    sh = src[:, 2 * half:2 * half + 2, :]
                    link(tt(sh, sh, bc(c1("cos1", T), 1, [P, 2, T]), ALU.mult))
                    i_ = tt(sh, sh, tmp, ALU.add)
            i_.then_inc(S("rk_ready"), 1)
            dve.wait_ge(S("rk_ready"), 1)
            for hh in range(RH):
                b = hh % 2
                dve.wait_ge(S("dec_in"), hh + 1)
                link(tt(dec[:, b, :], dec[:, b, :], c1("msk", 1024), ALU.mult))
                link(tt(dec[:, b, 0:512], dec[:, b, 0:512], dec[:, b, 512:1024], ALU.add))
                if hh >= 2:
                    dve.wait_ge(S("or_ps"), hh - 1)
                dve.wait_ge(S("rsc_ps"), hh + 1)
                tt(pr[:, b, :], PB[4 + b], dec[:, b, 0:512], ALU.mult).then_inc(S("pr_ready"), 1)
                dve.wait_ge(S("rqe"), hh + 1)
                q2 = rqd[:, b, :].rearrange("p (a b) -> p a b", a=2)
                tt(q2, q2, bc(rq[:, hh, :], 1, [P, 2, T]), ALU.mult).then_inc(S("rqd_ready"), 1)
            dve.wait_ge(S("or_out"), 4)
            tt(gn_t, og, og, ALU.mult).then_inc(S("gsq_ready"), 1)
            dve.wait_ge(S("hnorm_ps"), 2)
            for half in range(2):
                o2 = orr[:, 2 * half:2 * half + 2, :]
                i_ = V.scalar_tensor_tensor(o2, PB[6 + half][:, :].rearrange("p (a b) -> p a b", a=2), -1.0 / P, o2,
                                            ALU.mult, ALU.add)
            link(i_)
            tt(gn_t, orr, orr, ALU.mult).then_inc(S("rsq_ready"), 1)
            for half in range(2):
                V.tensor_scalar(tmp1[:, half, :], PB[4 + half], 1.0 / P, EPS, ALU.mult, ALU.add)
            dve.wait_ge(S("hnorm_ps"), 3)
            for half in range(2):
                i_ = V.tensor_scalar(tmp1[:, 2 + half, :], PB[6 + half], 1.0 / P, EPS, ALU.mult, ALU.add)
            i_.then_inc(S("hn_ms"), 1)
            dve.wait_ge(S("hn_rms"), 1)
            link(V.reciprocal(tmp1, tmp1))
            t4 = view(B1["la"][0], 8, T)
            tt(og, og, t4[:, 0:4, :], ALU.mult)
            link(tt(orr, orr, t4[:, 4:8, :], ALU.mult))
            for hh in range(GH):
                V.scalar_tensor_tensor(mixb1[:, hh, :], og[:, hh, :], v0("gnorm", 4)[:, hh:hh + 1], sgg[:, hh, :],
                                       ALU.mult, ALU.mult)
            for hh in range(RH):
                i_ = V.scalar_tensor_tensor(mixb1[:, 4 + hh, :], orr[:, hh, :], v0("rnorm", 4)[:, hh:hh + 1], srg[:, hh, :],
                                            ALU.mult, ALU.mult)
            i_.then_inc(S("mix1_ready"), 1)
            modulation([1, 2], 12, 3, (2, 3, 4, 5))
            n = PROJ1_END[-1]
            for mt in range(KT):
                dve.wait_ge(S("tile_in"), n + 1)
                V.scalar_tensor_tensor(resid[:, mt, 0:T], PB[n % 4][:, 0:T], modv[:, 0, 16 + mt, 0:1], resid[:, mt, 0:T],
                                       ALU.mult, ALU.add).then_inc(S("tile_out_D"), 1)
                n += 1

            def norm(k):
                if k not in ROLLED:
                    norm_squares(k, NORMS[k][2])
                return norm_rest(k, NORMS[k][2])

            dve.wait_ge(S("tile_out_D"), 13 + KT)
            norm(1)
            lgt = PB[5][:, 0:2 * E].rearrange("p (a b) -> p a b", a=2)
            dve.wait_ge(S("router_ps"), 1)
            link(V.reduce_max(sm[:, 0:2], lgt, AX.X))
            tt(aff, lgt, bc(sm[:, 0:2], 2, [P, 2, E]), ALU.subtract).then_inc(S("routed"), 1)
            dve.wait_ge(S("affe"), 1)
            link(V.reduce_sum(sm[:, 2:4], aff, AX.X))
            link(V.reciprocal(sm[:, 4:6], sm[:, 2:4]))
            tt(aff, aff, bc(sm[:, 4:6], 2, [P, 2, E]), ALU.mult).then_inc(S("routed"), 1)
            dve.wait_ge(S("router_ps"), 2)
            V.tensor_copy(pa[:, T:2 * T], PB[6][0:E, 0:T])
            link(V.tensor_copy(affw[:, 0, :], PB[6][0:E, 0:T]))
            for r in range(CAP // 8):
                link(V.max(m8, affw[:, r % 2, :]))
                link(V.match_replace(affw[:, 1 - r % 2, :], m8, affw[:, r % 2, :], -1.0))
            V.tensor_scalar(mkT, affw[:, 0, :], 0.0, None, ALU.is_lt).then_inc(S("routed"), 1)
            dve.wait_ge(S("router_ps"), 3)
            V.tensor_copy(mk, PB[7][:, 0:2 * E].rearrange("p (a b) -> p a b", a=2)).then_inc(S("routed"), 1)
            dve.wait_ge(S("router_ps"), 4)
            dve.wait_ge(S("routed"), 4)
            tt(pos, PB[4][:, 0:2 * E].rearrange("p (a b) -> p a b", a=2), mk, ALU.mult).then_inc(S("routed"), 1)
            dve.wait_ge(S("routed"), 5)
            for x in range(2):
                i_ = tt(sel[:, x, :].rearrange("p (a b) -> p a b", a=E), bc(pos[:, x, :], 2, [P, E, CAP]),
                        bc(c0("iota32", CAP), 1, [P, E, CAP]), ALU.is_equal)
            i_.then_inc(S("routed"), 1)
            dve.wait_ge(S("router_ps"), 5)
            V.tensor_copy(pa[:, 0:T], PB[6][0:E, 0:T]).then_inc(S("routed"), 1)
            dve.wait_ge(S("routed"), 7)
            with dve.Fori(0, E) as i:
                dve.wait_ge(S("bc_ps"), i + 1)
                V.tensor_scalar(bcm, pa, ident[0:E, bass.ds(i, 1)], None, ALU.mult).then_inc(S("bcm_ready"), 1)
                dve.wait_ge(S("gs_out"), i + 1 + 1)
                dve.wait_ge(S("slot_free1"), 12 + 2 * i + 2 + 1)
                tt(gu, gs, PB[5][:, 0:FQ], ALU.mult).then_inc(S("gu_ready"), 1)
                dve.wait_ge(S("gu_ready"), i + 1 + 1)
                dve.wait_ge(S("slot_free5"), 2 * i + 1)
                V.transpose(hx, gu.rearrange("p (q t) -> p t q", t=FT)).then_inc(S("hx_ready"), 1)
                dve.wait_ge(S("bcs_out"), i + 1 + 1)
                dve.wait_ge(S("z_ps"), i + 1)
                V.scalar_tensor_tensor(selg, bcs[:, 0:T], c0("slot1", 1), bcs[:, T:2 * T], ALU.is_equal, ALU.mult) \
                    .then_inc(S("selg_ready"), 1)
                dve.wait_ge(S("z_ps"), i + 1 + 1)
                for t in range(KT):
                    i_ = V.scalar_tensor_tensor(resid[:, t, 0:T], PB[t // 2][:, (t % 2) * T:(t % 2 + 1) * T],
                                                modv[:, 0, 40 + t, 0:1], resid[:, t, 0:T], ALU.mult, ALU.add)
                i_.then_inc(S("acc_done"), 1)
                dve.wait_ge(S("acc_done"), i + 1 + 1)
            norm(2).then_inc(S("x_in2"), 1)
            dve.wait_ge(S("x_in2"), 1)
            dve.wait_ge(S("second_in"), 64)
            for layer in range(2):
                nf = N2 if layer == 0 else T
                ns = nf // T
                k0 = 3 + 2 * layer
                V.memset(glu, 0.0)
                link(V.memset(cx, 0.0))

                def w_low(j):
                    dve.wait_ge(S("w_hi_ready"), split_no(layer, j + 1))
                    tt(proj_split(w_lo, j), proj_unit(layer, j) if j < 28 else w_unit(j - 28),
                       proj_split(w_hi, j).bitcast(F32), ALU.subtract).then_inc(S("w_lo_ready"), 1)

                def h_low(tiles_, before, n_):
                    for x, k in enumerate(tiles_):
                        dve.wait_ge(S("h_hi_ready"), 24 * layer + before + x + 1)
                        tt(h_lo[k][:, 0:n_], h[:, k, 0:n_], h_hi[k][:, 0:n_].bitcast(F32), ALU.subtract) \
                            .then_inc(S("h_split"), 1)

                for j in range(NWB):
                    w_low(j)
                norm(k0)
                lam = v2(layer, "lam", 2, 2, DQ)
                link(tt(s4[:, 24:56].rearrange("p (a b) -> p a b", a=1), lam[:, 0:1, 0, :], lam[:, 0:1, 1, :], ALU.mult))
                link(V.reduce_sum(s4[:, 0:1], s4[:, 24:56], AX.X))
                link(tt(s4[:, 24:56].rearrange("p (a b) -> p a b", a=1), lam[:, 1:2, 0, :], lam[:, 1:2, 1, :], ALU.mult))
                V.reduce_sum(s4[:, 1:2], s4[:, 24:56], AX.X).then_inc(S("lam_in"), 1)
                n = PROJ2_AT[layer]
                a_out = A_TILES_BEFORE[layer]

                def seg(t, m):
                    return t[:, m, 0:nf].rearrange("p (s t) -> p s t", s=ns)

                def taps(src, acc, w, first, last, bias):
                    for x in range(first, last):
                        for m in range(2):
                            win = src[:, m, 0:ns, x:x + T]
                            sc = w[:, m, x:x + 1]
                            if x:
                                dve.wait_ge(S("taps"), TAPS_AT[0] - 1)
                                i_ = V.scalar_tensor_tensor(seg(acc, m), win, sc, seg(acc, m), ALU.mult, ALU.add)
                            else:
                                b_ = bias[:, m:m + 1] if bias is not None else 0.0
                                i_ = V.tensor_scalar(seg(acc, m), win, sc, b_, ALU.mult, ALU.add) if bias is not None \
                                    else V.tensor_scalar(seg(acc, m), win, sc, None, ALU.mult)
                            i_.then_inc(S("taps"), 1)
                            TAPS_AT[0] += 1
                    dve.wait_ge(S("taps"), TAPS_AT[0])

                for g, group in enumerate(proj2_tiles(layer)[:2]):
                    for x, (M, N, _, _, _, owner, dst, func) in enumerate(group):
                        if owner == "D":
                            dve.wait_ge(S("tile_in"), n + 1)
                            dve.wait_ge(S("tile_out_A"), a_out)
                            tt(dst, PB[n % 4][0:M, 0:N].rearrange("p (s t) -> p s t", s=ns),
                               func[1].rearrange("p (s t) -> p s t", s=ns), ALU.mult).then_inc(S("tile_out_D"), 1)
                            d_out[0] += 1
                        else:
                            a_out += 1
                        n += 1
                        w_low(4 * g + x + NWB)
                        if g:
                            taps(glu, acca, v2(layer, "caw", 2, 31), 3 * x, 3 * x + 3, v2(layer, "cab", 2))
                    dve.wait_ge(S("tile_out_D"), d_out[0])
                for j in range(8, 15):
                    w_low(j + NWB)
                    taps(glu, acca, v2(layer, "caw", 2, 31), 3 * j - 12, min(3 * j - 9, 31), None)
                w_low(15 + NWB)
                taps(cx, accd, v2(layer, "cdw", 2, 3), 0, 3, None)
                V.tensor_copy(s4[:, 56:57], s4[:, 0:1]).then_inc(S("ln_in"), 1)
                dve.wait_ge(S("ln_ps"), 2 * layer + 1)
                for m_ in range(2):
                    i_ = V.scalar_tensor_tensor(acca[:, m_, 0:nf], PB[6][:, 0:nf], -1.0 / GW, acca[:, m_, 0:nf],
                                                ALU.mult, ALU.add)
                link(i_)
                tt(ln_sq[:, :, 0:nf], acca[:, :, 0:nf], acca[:, :, 0:nf], ALU.mult).then_inc(S("ln_in"), 1)
                for x, src in enumerate((qf, kf)):
                    dve.wait_ge(S("rope2_ps"), 2 * layer + x + 1)
                    t2 = rope_t
                    link(tt(t2, PB[4 + x][:, :].rearrange("p (a b) -> p a b", a=2), bc(c2("sin2", T), 1, [P, 2, T]), ALU.mult))
                    link(tt(src[:, :, 0:T], src[:, :, 0:T], bc(c2("cos2", T), 1, [P, 2, T]), ALU.mult))
                    i_ = tt(src[:, :, 0:T], src[:, :, 0:T], t2, ALU.add)
                    if x == 0:
                        link(i_)
                i_.then_inc(S("qk2_ready"), 1)
                w_low(16 + NWB)
                w_low(17 + NWB)
                dve.wait_ge(S("lam_exp"), layer + 1)
                link(tt(s4[:, 4:5], s4[:, 3:4], s4[:, 2:3], ALU.subtract))
                link(V.tensor_scalar(s4[:, 4:5], s4[:, 4:5], LAM_INIT[layer], None, ALU.subtract))
                w_low(18 + NWB)
                units = attn_units(layer)
                u0 = UNIT_AT[layer]

                def maxima(u):
                    nk = 512 if units[u][0] == 0 else 256
                    dve.wait_ge(S("asc_ps"), u0 + u + 1)
                    for comp in range(2):
                        c_ = 16 + 2 * (u % 2) + comp
                        i_ = V.reduce_max(s4[:, c_:c_ + 1], PB[2 * (u % 2) + comp][:, 0:nk], AX.X, negate=True)
                    link(i_)
                    c_ = 16 + 2 * (u % 2)
                    V.tensor_scalar(s4[:, c_:c_ + 2], s4[:, c_:c_ + 2], float(DQ) ** -0.5, None, ALU.mult) \
                        .then_inc(S("amax"), 1)

                nt = nf // P
                svv, sv_t = sv[:, 0:nt, :], sv_sq[:, 0:nt, :]

                def mixer_step(u):
                    if u == 0:
                        w_low(19 + NWB)
                        dve.wait_ge(S("ln_ps"), 2 * layer + 2)
                        V.tensor_scalar(rs[:, 0:nf], PB[6][:, 0:nf], 1.0 / GW, EPS, ALU.mult, ALU.add) \
                            .then_inc(S("ln_var"), 1)
                        dve.wait_ge(S("tile_out_A"), A_TILES_BEFORE[layer] + n_a(proj2_tiles(layer)[:4]) + 2)
                        link(V.reduce_sum(s4[:, 8:8 + nt], svv, AX.X))
                        link(V.tensor_scalar(s4[:, 8:8 + nt], s4[:, 8:8 + nt], 1.0 / GW, None, ALU.mult))
                        link(tt(svv, svv, bc(s4[:, 8:8 + nt], 2, [P, nt, GW]), ALU.subtract))
                    if u == 1:
                        link(tt(sv_t, svv, svv, ALU.mult))
                        link(V.reduce_sum(s4[:, 12:12 + nt], sv_t, AX.X))
                        V.tensor_scalar(s4[:, 12:12 + nt], s4[:, 12:12 + nt], 1.0 / GW, EPS, ALU.mult, ALU.add) \
                            .then_inc(S("sv_var"), 1)
                    if u == 3:
                        dve.wait_ge(S("ln_std"), layer + 1)
                        link(V.reciprocal(rs[:, 0:nf], rs[:, 0:nf]))
                        tt(acca[:, :, 0:nf], acca[:, :, 0:nf], bc(rs[:, 0:nf], 1, [P, 2, nf]), ALU.mult) \
                            .then_inc(S("ln_out"), 1)
                    if u == 4:
                        dve.wait_ge(S("sv_std"), layer + 1)
                        link(V.reciprocal(s4[:, 12:12 + nt], s4[:, 12:12 + nt]))
                        link(tt(svv, svv, bc(s4[:, 12:12 + nt], 2, [P, nt, GW]), ALU.mult))
                        link(tt(svv, svv, bc(v2(layer, "sglng", GW), 1, [P, nt, GW]), ALU.mult))
                        tt(svv, svv, bc(v2(layer, "sglnb", GW), 1, [P, nt, GW]), ALU.add).then_inc(S("svn_ready"), 1)
                    if u == 5:
                        dve.wait_ge(S("tile_out_A"), A_TILES_BEFORE[layer] + n_a(proj2_tiles(layer)))
                        tt(mix[:, 6:8, 0:nf], accd[:, :, 0:nf], bgf[:, :, 0:nf], ALU.mult).then_inc(S("yd_ready"), 1)

                maxima(0)
                for u, (s_, qt, hh) in enumerate(units):
                    if u + 1 < len(units):
                        maxima(u + 1)
                    nk = 512 if s_ == 0 else 256
                    c_ = 20 + 2 * (u % 2)
                    dve.wait_ge(S("exp_done"), u0 + u + 1)
                    link(V.reciprocal(s4[:, c_:c_ + 2], s4[:, c_:c_ + 2]))
                    link(tt(s4[:, c_ + 1:c_ + 2], s4[:, c_ + 1:c_ + 2], s4[:, 4:5], ALU.mult))
                    e1, e2 = Eb[:, u % 2, 0, 0:nk], Eb[:, u % 2, 1, 0:nk]
                    link(V.tensor_scalar(e1, e1, s4[:, c_:c_ + 1], None, ALU.mult))
                    V.scalar_tensor_tensor(e1, e2, s4[:, c_ + 1:c_ + 2], e1, ALU.mult, ALU.add).then_inc(S("w_ready"), 1)
                    mixer_step(u)
                    if u == 7:
                        h_low(MIX_ORDER[:4], KT, nf)
                dve.wait_ge(S("sg_ps"), layer + 1)
                for gt in range(2):
                    m4 = mix[:, 4 + gt, 0:nf].rearrange("p (a b) -> p a b", b=P)
                    i_ = tt(m4, PB[gt][:, 0:nf].rearrange("p (a b) -> p a b", b=P),
                            bc(v2(layer, "sgb", 2, P)[:, gt, :], 1, [P, nt, P]), ALU.add)
                link(i_)
                tt(mix[:, 4:6, 0:nf], mix[:, 4:6, 0:nf], uf[:, :, 0:nf], ALU.mult).then_inc(S("yc_ready"), 1)
                dve.wait_ge(S("pv_ps"), u0 + len(units))
                for s_ in range(ns):
                    i_ = V.tensor_copy(mix[:, 2:4, s_ * T:(s_ + 1) * T], PB[6 + s_][:, :].rearrange("p (a b) -> p a b", a=2))
                link(i_)
                tt(tg[:, :, 0:nf], mix[:, 2:4, 0:nf], mix[:, 2:4, 0:nf], ALU.mult).then_inc(S("osq_ready"), 1)
                h_low(MIX_ORDER[4:6], KT + 4, nf)
                dve.wait_ge(S("oss_ps"), layer + 1)
                for m_ in range(2):
                    i_ = V.tensor_scalar(tc[:, m_, 0:nf], PB[2 + m_][:, 0:nf], 1.0 / 64, EPS, ALU.mult, ALU.add)
                i_.then_inc(S("o_ms"), 1)
                dve.wait_ge(S("o_rms"), layer + 1)
                link(V.reciprocal(tc[:, :, 0:nf], tc[:, :, 0:nf]))
                link(tt(mix[:, 2:4, 0:nf], mix[:, 2:4, 0:nf], tc[:, :, 0:nf], ALU.mult))
                V.tensor_scalar(mix[:, 2:4, 0:nf], mix[:, 2:4, 0:nf], v2(layer, "subg", 1), 1.0 - LAM_INIT[layer],
                                ALU.mult, ALU.mult).then_inc(S("mix2_ready"), 1)
                h_low(MIX_ORDER[6:], KT + 6, nf)
                n = OUT2_AT[layer]

                def add_residual(dt, bank, row):
                    for s_ in range(ns):
                        c_ = slice(s_ * T, (s_ + 1) * T)
                        i_ = V.scalar_tensor_tensor(resid[:, dt, c_], bank[:, c_], modv[:, 1 + layer, row + dt, s_:s_ + 1],
                                                    resid[:, dt, c_], ALU.mult, ALU.add)
                    return i_

                for dt in range(KT):
                    dve.wait_ge(S("tile_in"), n + dt + 1)
                    add_residual(dt, PB[(n + dt) % 4], 16).then_inc(S("tile_out_D"), 1)
                    d_out[0] += 1
                    w_low(20 + dt + NWB)
                dve.wait_ge(S("tile_out_D"), d_out[0])
                norm(k0 + 1)

                def take_unit(i, n):
                    c, q = n // 4 % 2, n % 4
                    if n < 8:
                        dve.wait_ge(S("h1_relu"), 32 * layer + 8 * i + n + 1 + 4)
                        tt(h1[:, c, q, 0:nf], h1[:, c, q, 0:nf], h1[:, c, q, 0:nf], ALU.mult) \
                            .then_inc(S("h1_sq"), 1)
                        return
                    for dt in (2 * q, 2 * q + 1):
                        dve.wait_ge(S(f"y_ps{c}"), 32 * layer + 8 * i + dt + 1 + 9)
                        dve.wait_ge(S("y_out"), 64 * layer + 16 * i + 8 * c + dt + 1)
                        add_residual(dt, PB[4 + dt % 4], 40).then_inc(S("y_out"), 1)

                def h1_low(i, n):
                    c, q = n // 4, n % 4
                    dve.wait_ge(S("h1_hi_ready"), 32 * layer + 8 * i + n + 1)
                    tt(h1_lo[c][:, q, 0:nf], h1[:, c, q, 0:nf], h1_hi[c][:, q, 0:nf].bitcast(F32), ALU.subtract) \
                        .then_inc(S("h1_ready"), 1)

                def mlp_round(i, last):
                    for n in range(16):
                        take_unit(i, n)
                        if n < 12 or not last:
                            m = (n + NWB) % 16
                            dve.wait_ge(S("w_hi_ready"), split_no(layer, 28) + 16 * i + n + NWB + 1)
                            tt(round_split(w_lo, m), w_unit(m), round_split(w_hi, m).bitcast(F32), ALU.subtract) \
                                .then_inc(S("w_lo_ready"), 1)
                        if n < 8:
                            h1_low(i, n)

                with dve.Fori(0, 3) as i:
                    mlp_round(i, False)
                mlp_round(3, True)
                dve.wait_ge(S("y_out"), 64 * (layer + 1) + 4)
            norm(7).then_inc(S("final"), 1)
    return


def pack_inputs(inputs):
    I = {k: np.asarray(v) for k, v in inputs.items()}

    def fm(a):
        return np.ascontiguousarray(a.T.reshape(-1, P, a.shape[0]).transpose(1, 0, 2))

    def vec(a):
        return a.reshape(-1, P).T

    def rows(a):
        return np.broadcast_to(a.reshape(1, -1), (P, a.size))

    c0, c1, c2 = shape_constants()
    arr = {"xT": fm(I["x"][0]), "ctxT": fm(I["ctx"][0]), "ctx2T": fm(I["ctx_2"][0]), "c0": c0, "c1": c1, "c2": c2}
    cv = [I["c"][0], I["c_ctx"], I["c_2"][0], I["c_ctx_2"]]
    norms = [I["norm1_w"][0], I["norm2_w"][0], I["final_norm_w"], I["norm1_g_2"][0], I["norm1_g_2"][1],
             I["norm2_g_2"][0], I["norm2_g_2"][1], I["final_g_2"]]
    bada = [I["b_ada"][0], I["ada_b_2"][0], I["ada_b_2"][1]]
    arr["v0"] = np.ascontiguousarray(np.concatenate(
        [vec(a) for a in cv + norms + bada] + [vec(I["gla_norm_w"][0]), vec(I["ret_norm_w"][0]),
                                               rows(I["ret_decay_logit"][0])], 1))
    per = []
    for l in range(2):
        sgb = I["sg_b_2"][l]
        sgb = sgb.reshape(2, 2, 1, P)
        sgb = np.broadcast_to(sgb, (2, 2, 64, P)).transpose(1, 2, 0, 3).reshape(P, 2 * P)
        lam = np.concatenate([I["lam_q1_2"][l], I["lam_k1_2"][l], I["lam_q2_2"][l], I["lam_k2_2"][l]])
        per += [I["conv_a_w_2"][l].T.reshape(2, P, 31).transpose(1, 0, 2).reshape(P, 62),
                vec(I["conv_a_b_2"][l]), vec(I["ln_a_g_2"][l]), vec(I["ln_a_b_2"][l]),
                I["conv_d_w_2"][l].T.reshape(2, P, 3).transpose(1, 0, 2).reshape(P, 6),
                np.concatenate([I["subln_g_2"][l], I["subln_g_2"][l]]).reshape(P, 1),
                rows(I["sg_ln_g_2"][l]), rows(I["sg_ln_b_2"][l]), sgb, rows(lam)]
    arr["v2"] = np.ascontiguousarray(np.concatenate(per, 1))
    arr["sgw"] = np.ascontiguousarray(I["sg_w_2"].transpose(3, 0, 1, 2).reshape(P, -1))
    arr["wr"] = np.ascontiguousarray(I["w_router"][0].reshape(KT, P, E).transpose(1, 0, 2))
    gw = np.zeros((33, 512), np.float32)
    gw[0:16, 0:256] = I["gla_gate_w"][0, 0]
    gw[16:32, 256:512] = I["gla_gate_w"][0, 1]
    gw[32] = I["gla_gate_b"][0].reshape(-1)
    arr["gw"] = gw
    for name in ("w_ada", "w_in", "w_out", "w_exp_gate", "w_exp_up", "w_exp_down", "ada_w_2", "w_in_2", "w_out_2",
                 "mlp_w1_2", "mlp_w2_2"):
        arr[name] = np.ascontiguousarray(I[name])
    return arr


def kernel(**inputs):
    import concourse.bacc as bacc
    from concourse.bass_utils import run_bass_kernel_spmd

    nc = bacc.Bacc("TRN2", target_bir_lowering=False, num_devices=1)
    arrays = pack_inputs(inputs)
    aps = {k: nc.dram_tensor(f"in_{k}", a.shape, mybir.dt.from_np(a.dtype), kind="ExternalInput").ap()
           for k, a in arrays.items()}
    out = nc.dram_tensor("out", (P, KT, T), F32, kind="ExternalOutput").ap()
    build(nc, aps, out)
    r = run_bass_kernel_spmd(nc, [{f"in_{k}": a for k, a in arrays.items()}], core_ids=[0])
    got = r.results[0]["out"]
    return np.ascontiguousarray(got.transpose(2, 1, 0).reshape(1, T, D))
```
